# Optimizing a Trainium2 kernel written in Bass

```python
import jax, jax.numpy as jnp
from jax import lax
import numpy as np

D_MODEL = 1024
BATCH = 1
SEQ = 1024
DEPTH = 1

HEAD_DIM = 64
NSA_HEADS = 8
NSA_KV_HEADS = 2
NSA_GROUP = NSA_HEADS // NSA_KV_HEADS
SB_HEADS = 8
MIX_WIDTH = (NSA_HEADS + SB_HEADS) * HEAD_DIM
ROPE_THETA = 500000.0
ROPE_DIM = HEAD_DIM // 4
CMP_LEN = 32
CMP_STRIDE = 16
CMP_HIDDEN = 256
SEL_LEN = 64
SEL_TOP = 16
SEL_BONUS = 1.0e4
WINDOW = 512
Q_BLOCK = 128
N_GROUPS = 4
EXPERTS_PER_GROUP = 4
N_EXPERTS = N_GROUPS * EXPERTS_PER_GROUP
TOP_K_IN_GROUP = 2
EXPERT_FF = 512
MOE_BLOCK = 128
EPS = 1e-6
NEG = -1e30

N_Q = NSA_HEADS * HEAD_DIM
N_KV = 3 * 2 * NSA_KV_HEADS * HEAD_DIM
N_GATE = NSA_HEADS * 3
N_SB = 3 * SB_HEADS * HEAD_DIM
IN_COLS = N_Q + N_KV + N_GATE + N_SB

kernel_name = "hymba_nsa_stickbreak_hiermoe"

def rms_norm(x, w):
    xf = x.astype(jnp.float32)
    y = xf * lax.rsqrt(jnp.mean(xf * xf, axis=-1, keepdims=True) + EPS)
    return (y * w.astype(jnp.float32)).astype(x.dtype)

def rope_partial(x, cos, sin):
    half = ROPE_DIM // 2
    xr = x[..., :ROPE_DIM].astype(jnp.float32)
    x1, x2 = xr[..., :half], xr[..., half:]
    rot = jnp.concatenate([x1 * cos - x2 * sin, x2 * cos + x1 * sin], axis=-1)
    return jnp.concatenate([rot.astype(x.dtype), x[..., ROPE_DIM:]], axis=-1)

def masked_softmax(s, m):
    s = jnp.where(m, s, NEG)
    mx = jnp.max(s, axis=-1, keepdims=True)
    e = jnp.where(m, jnp.exp(s - mx), 0.0)
    return e / jnp.maximum(jnp.sum(e, axis=-1, keepdims=True), 1e-30)

def compress(k, pe, w1, w2):
    B, T, G, dh = k.shape
    n_cmp = (T - CMP_LEN) // CMP_STRIDE + 1
    idx = jnp.arange(n_cmp)[:, None] * CMP_STRIDE + jnp.arange(CMP_LEN)[None, :]
    blocks = k[:, idx] + pe[:, None, :].astype(k.dtype)
    blocks = blocks.transpose(0, 3, 1, 2, 4).reshape(B, G, n_cmp, CMP_LEN * dh)
    return jax.nn.silu(blocks @ w1) @ w2

def gather_blocks(blocks, idx):
    return jax.vmap(jax.vmap(lambda bl, ix: bl[ix]))(blocks, idx)

def nsa_attention(q, k_cmp, v_cmp, k_sel, v_sel, k_win, v_win, gates, cmp_pe_k, cmp_pe_v,
                  cmp_k_w1, cmp_k_w2, cmp_v_w1, cmp_v_w2):
    B, T, H, dh = q.shape
    G, R = NSA_KV_HEADS, NSA_GROUP
    scale = dh ** -0.5
    kc = compress(k_cmp, cmp_pe_k, cmp_k_w1, cmp_k_w2)
    vc = compress(v_cmp, cmp_pe_v, cmp_v_w1, cmp_v_w2)
    n_cmp = kc.shape[2]
    cmp_start = jnp.arange(n_cmp) * CMP_STRIDE
    cmp_end = cmp_start + CMP_LEN - 1
    n_sel = T // SEL_LEN
    n_top = min(SEL_TOP, n_sel)
    sel_start = jnp.arange(n_sel) * SEL_LEN
    overlap = ((cmp_start[:, None] < sel_start[None, :] + SEL_LEN)
               & (cmp_start[:, None] + CMP_LEN > sel_start[None, :])).astype(jnp.float32)
    ks_blocks = k_sel.reshape(B, n_sel, SEL_LEN, G, dh).transpose(0, 3, 1, 2, 4)
    vs_blocks = v_sel.reshape(B, n_sel, SEL_LEN, G, dh).transpose(0, 3, 1, 2, 4)
    pad = ((0, 0), (WINDOW, 0), (0, 0), (0, 0))
    kw_pad = jnp.pad(k_win, pad)
    vw_pad = jnp.pad(v_win, pad)
    jsel = jnp.arange(n_sel)

    def block(b):
        q0 = b * Q_BLOCK
        t = q0 + jnp.arange(Q_BLOCK)
        qb = lax.dynamic_slice_in_dim(q, q0, Q_BLOCK, axis=1).reshape(B, Q_BLOCK, G, R, dh)
        s_c = jnp.einsum('bqgrd,bgnd->bgrqn', qb, kc).astype(jnp.float32) * scale
        p_c = masked_softmax(s_c, cmp_end[None, :] <= t[:, None])
        o_c = jnp.einsum('bgrqn,bgnd->bqgrd', p_c.astype(vc.dtype), vc)
        imp = jnp.einsum('bgrqn,nm->bgqm', p_c, overlap)
        bq = t // SEL_LEN
        forced = (jsel[None, :] == 0) | (jsel[None, :] == bq[:, None]) | (jsel[None, :] == bq[:, None] - 1)
        allowed = jsel[None, :] <= bq[:, None]
        score = jnp.where(allowed, imp + jnp.where(forced, SEL_BONUS, 0.0), NEG)
        _, sel_idx = lax.top_k(score, n_top)
        kg = gather_blocks(ks_blocks, sel_idx).reshape(B, G, Q_BLOCK, n_top * SEL_LEN, dh)
        vg = gather_blocks(vs_blocks, sel_idx).reshape(B, G, Q_BLOCK, n_top * SEL_LEN, dh)
        tok = (sel_idx[..., None] * SEL_LEN + jnp.arange(SEL_LEN)).reshape(B, G, Q_BLOCK, n_top * SEL_LEN)
        m_s = (tok <= t[None, None, :, None])[:, :, None]
        s_s = jnp.einsum('bqgrd,bgqkd->bgrqk', qb, kg).astype(jnp.float32) * scale
        p_s = masked_softmax(s_s, m_s)
        o_s = jnp.einsum('bgrqk,bgqkd->bqgrd', p_s.astype(vg.dtype), vg)
        kwb = lax.dynamic_slice_in_dim(kw_pad, q0, WINDOW + Q_BLOCK, axis=1)
        vwb = lax.dynamic_slice_in_dim(vw_pad, q0, WINDOW + Q_BLOCK, axis=1)
        kpos = q0 - WINDOW + jnp.arange(WINDOW + Q_BLOCK)
        m_w = (kpos[None, :] <= t[:, None]) & (t[:, None] - kpos[None, :] < WINDOW) & (kpos[None, :] >= 0)
        s_w = jnp.einsum('bqgrd,bkgd->bgrqk', qb, kwb).astype(jnp.float32) * scale
        p_w = masked_softmax(s_w, m_w)
        o_w = jnp.einsum('bgrqk,bkgd->bqgrd', p_w.astype(vwb.dtype), vwb)
        gb = lax.dynamic_slice_in_dim(gates, q0, Q_BLOCK, axis=1).reshape(B, Q_BLOCK, G, R, 3)
        o = gb[..., 0:1] * o_c + gb[..., 1:2] * o_s + gb[..., 2:3] * o_w
        return o.reshape(B, Q_BLOCK, H * dh)

    out = lax.map(block, jnp.arange(T // Q_BLOCK))
    return out.transpose(1, 0, 2, 3).reshape(B, T, H * dh)

def stick_breaking_attention(q, k, v):
    B, T, H, dh = q.shape
    scale = dh ** -0.5
    s_pos = jnp.arange(T)

    def block(b):
        q0 = b * Q_BLOCK
        t = q0 + jnp.arange(Q_BLOCK)
        qb = lax.dynamic_slice_in_dim(q, q0, Q_BLOCK, axis=1)
        z = jnp.einsum('bqhd,bshd->bhqs', qb, k).astype(jnp.float32) * scale
        mask = s_pos[None, :] < t[:, None]
        log_not = jnp.where(mask, jax.nn.log_sigmoid(-z), 0.0)
        after = lax.cumsum(log_not, axis=3, reverse=True) - log_not
        a = jnp.where(mask, jnp.exp(jax.nn.log_sigmoid(z) + after), 0.0)
        o = jnp.einsum('bhqs,bshd->bqhd', a.astype(v.dtype), v)
        return o.reshape(B, Q_BLOCK, H * dh)

    out = lax.map(block, jnp.arange(T // Q_BLOCK))
    return out.transpose(1, 0, 2, 3).reshape(B, T, H * dh)

def hybrid_mixer(h, positions, w_in, cmp_pe_k, cmp_pe_v, cmp_k_w1, cmp_k_w2, cmp_v_w1, cmp_v_w2,
                 nsa_out_norm_w, sb_out_norm_w, w_out):
    B, T, _ = h.shape
    proj = h @ w_in
    o1, o2, o3 = N_Q, N_Q + N_KV, N_Q + N_KV + N_GATE
    q_n = proj[..., :o1].reshape(B, T, NSA_HEADS, HEAD_DIM)
    kv = proj[..., o1:o2].reshape(B, T, 3, 2, NSA_KV_HEADS, HEAD_DIM)
    gates = jax.nn.sigmoid(proj[..., o2:o3].reshape(B, T, NSA_HEADS, 3))
    sb = proj[..., o3:].reshape(B, T, 3, SB_HEADS, HEAD_DIM)
    inv_freq = ROPE_THETA ** (-jnp.arange(0, ROPE_DIM, 2, dtype=jnp.float32) / ROPE_DIM)
    ang = positions.astype(jnp.float32)[..., None] * inv_freq
    cos, sin = jnp.cos(ang)[:, :, None, :], jnp.sin(ang)[:, :, None, :]
    q_n = rope_partial(q_n, cos, sin)
    k_sel = rope_partial(kv[:, :, 1, 0], cos, sin)
    k_win = rope_partial(kv[:, :, 2, 0], cos, sin)
    o_nsa = nsa_attention(q_n, kv[:, :, 0, 0], kv[:, :, 0, 1], k_sel, kv[:, :, 1, 1], k_win, kv[:, :, 2, 1],
                          gates, cmp_pe_k, cmp_pe_v, cmp_k_w1, cmp_k_w2, cmp_v_w1, cmp_v_w2)
    o_sb = stick_breaking_attention(sb[:, :, 0], sb[:, :, 1], sb[:, :, 2])
    o = jnp.concatenate([rms_norm(o_nsa, nsa_out_norm_w), rms_norm(o_sb, sb_out_norm_w)], axis=-1)
    return o @ w_out

def hierarchical_moe(h, rg_w, rg_b, re_w, re_b, w_gate, w_up, w_down):
    B, T, D = h.shape
    hf = h.reshape(B * T, D)
    N = B * T
    g_logits = (hf @ rg_w).astype(jnp.float32) + rg_b
    grp = jnp.argmax(g_logits, axis=-1)
    g_gate = jnp.take_along_axis(jax.nn.softmax(g_logits, axis=-1), grp[:, None], axis=1)[:, 0]
    e_logits = ((hf @ re_w).astype(jnp.float32) + re_b).reshape(N, N_GROUPS, EXPERTS_PER_GROUP)
    e_logits = jnp.take_along_axis(e_logits, grp[:, None, None], axis=1)[:, 0]
    top_val, top_loc = lax.top_k(e_logits, TOP_K_IN_GROUP)
    weight = g_gate[:, None] * jax.nn.softmax(top_val, axis=-1)
    expert = grp[:, None] * EXPERTS_PER_GROUP + top_loc
    flat_e = expert.reshape(-1)
    flat_t = jnp.repeat(jnp.arange(N, dtype=jnp.int32), TOP_K_IN_GROUP)
    flat_w = weight.reshape(-1)
    A = N * TOP_K_IN_GROUP
    order = jnp.argsort(flat_e)
    se = flat_e[order]
    counts = jnp.bincount(flat_e, length=N_EXPERTS)
    padded = ((counts + MOE_BLOCK - 1) // MOE_BLOCK) * MOE_BLOCK
    start = jnp.cumsum(counts) - counts
    pend = jnp.cumsum(padded)
    pstart = pend - padded
    dest = pstart[se] + jnp.arange(A) - start[se]
    R = (-(-A // MOE_BLOCK) + N_EXPERTS) * MOE_BLOCK
    nb = R // MOE_BLOCK
    row_tok = jnp.zeros((R,), jnp.int32).at[dest].set(flat_t[order])
    row_w = jnp.zeros((R,), jnp.float32).at[dest].set(flat_w[order])
    blk_exp = jnp.minimum(jnp.searchsorted(pend, jnp.arange(nb) * MOE_BLOCK, side='right'), N_EXPERTS - 1)

    def expert_block(args):
        toks, e = args
        xb = hf[toks]
        return (jax.nn.silu(xb @ w_gate[e]) * (xb @ w_up[e])) @ w_down[e]

    y = lax.map(expert_block, (row_tok.reshape(nb, MOE_BLOCK), blk_exp)).reshape(R, D)
    y = y * row_w[:, None].astype(y.dtype)
    out = jnp.zeros((N, D), h.dtype).at[row_tok].add(y)
    return out.reshape(B, T, D)

def setup_inputs(seed: int = 0) -> dict:
    key = jax.random.key(seed)
    ks = jax.random.split(key, 24)
    L, D = DEPTH, D_MODEL
    nrm = lambda k, shape, fan: jax.random.normal(k, shape, jnp.float32) * (fan ** -0.5)
    gain = lambda k, shape: 1.0 + 0.02 * jax.random.normal(k, shape, jnp.float32)
    return {
        "x": jax.random.normal(ks[0], (BATCH, SEQ, D), jnp.float32),
        "positions": jnp.broadcast_to(jnp.arange(SEQ, dtype=jnp.int32), (BATCH, SEQ)),
        "attn_norm_w": gain(ks[1], (L, D)),
        "w_in": nrm(ks[2], (L, D, IN_COLS), D),
        "cmp_pe_k": 0.02 * jax.random.normal(ks[3], (L, CMP_LEN, HEAD_DIM), jnp.float32),
        "cmp_pe_v": 0.02 * jax.random.normal(ks[4], (L, CMP_LEN, HEAD_DIM), jnp.float32),
        "cmp_k_w1": nrm(ks[5], (L, CMP_LEN * HEAD_DIM, CMP_HIDDEN), CMP_LEN * HEAD_DIM),
        "cmp_k_w2": nrm(ks[6], (L, CMP_HIDDEN, HEAD_DIM), CMP_HIDDEN),
        "cmp_v_w1": nrm(ks[7], (L, CMP_LEN * HEAD_DIM, CMP_HIDDEN), CMP_LEN * HEAD_DIM),
        "cmp_v_w2": nrm(ks[8], (L, CMP_HIDDEN, HEAD_DIM), CMP_HIDDEN),
        "nsa_out_norm_w": gain(ks[9], (L, NSA_HEADS * HEAD_DIM)),
        "sb_out_norm_w": gain(ks[10], (L, SB_HEADS * HEAD_DIM)),
        "w_out": nrm(ks[11], (L, MIX_WIDTH, D), MIX_WIDTH),
        "ffn_norm_w": gain(ks[12], (L, D)),
        "router_group_w": nrm(ks[13], (L, D, N_GROUPS), D),
        "router_group_b": 0.01 * jax.random.normal(ks[14], (L, N_GROUPS), jnp.float32),
        "router_expert_w": nrm(ks[15], (L, D, N_EXPERTS), D),
        "router_expert_b": 0.01 * jax.random.normal(ks[16], (L, N_EXPERTS), jnp.float32),
        "w_gate": nrm(ks[17], (L, N_EXPERTS, D, EXPERT_FF), D),
        "w_up": nrm(ks[18], (L, N_EXPERTS, D, EXPERT_FF), D),
        "w_down": nrm(ks[19], (L, N_EXPERTS, EXPERT_FF, D), EXPERT_FF),
        "final_norm_w": gain(ks[20], (D,)),
    }

def reference(x, positions, attn_norm_w, w_in, cmp_pe_k, cmp_pe_v, cmp_k_w1, cmp_k_w2, cmp_v_w1, cmp_v_w2,
              nsa_out_norm_w, sb_out_norm_w, w_out, ffn_norm_w, router_group_w, router_group_b,
              router_expert_w, router_expert_b, w_gate, w_up, w_down, final_norm_w):
    for i in range(DEPTH):
        h = rms_norm(x, attn_norm_w[i])
        x = x + hybrid_mixer(h, positions, w_in[i], cmp_pe_k[i], cmp_pe_v[i], cmp_k_w1[i], cmp_k_w2[i],
                             cmp_v_w1[i], cmp_v_w2[i], nsa_out_norm_w[i], sb_out_norm_w[i], w_out[i])
        h = rms_norm(x, ffn_norm_w[i])
        x = x + hierarchical_moe(h, router_group_w[i], router_group_b[i], router_expert_w[i],
                                 router_expert_b[i], w_gate[i], w_up[i], w_down[i])
    return rms_norm(x, final_norm_w)


_drawn_inputs = setup_inputs


def setup_inputs(seed=0):
    import zlib

    import numpy as np

    out = dict(_drawn_inputs(seed))
    spreads = {}
    factors = {'cmp_pe_k': 8.0,
     'nsa_out_norm_w': 3.229,
     'sb_out_norm_w': 2.932,
     'ffn_norm_w': 2.705,
     'router_group_b': 5.171,
     'router_expert_b': 8.0,
     'final_norm_w': 2.928}
    for name, (base, spread) in spreads.items():
        noise = np.random.default_rng([zlib.crc32(name.encode()), seed]).standard_normal(out[name].shape)
        drawn = base * np.exp(spread * noise) if base else spread * noise
        out[name] = __import__('jax').numpy.asarray(drawn.astype(out[name].dtype))
    for name, factor in factors.items():
        out[name] = (out[name] * factor).astype(out[name].dtype)
    return out
```

```python
from contextlib import ExitStack

import numpy as np

import concourse.bass as bass
from concourse import mybir
from concourse.alu_op_type import AluOpType as ALU

F32 = mybir.dt.float32
BF16 = mybir.dt.bfloat16
I32 = mybir.dt.int32
U32 = mybir.dt.uint32
ACT = mybir.ActivationFunctionType
AX_X = mybir.AxisListType.X

P = 128
T = 1024
D = 1024
NT = T // P
ND = D // P
BANK = 512
DH = 64
HALF = DH // 8
NSA_H, KV_G, SB_H = 8, 2, 8
R_G = NSA_H // KV_G
N_Q = NSA_H * DH
COL_CMP = N_Q
COL_SEL = COL_CMP + 2 * KV_G * DH
COL_GATE = N_Q + 6 * KV_G * DH
N_GATE = 3 * NSA_H
COL_SBQ = COL_GATE + N_GATE
COL_SBK = COL_SBQ + SB_H * DH
COL_SBV = COL_SBK + SB_H * DH
CMP_LEN, CMP_STRIDE, CMP_HID = 32, 16, 256
N_CMP = 64
WIN_TILES = 512 // P
N_EXP, N_GRP, E_PG, FF = 16, 4, 4, 512
NF = FF // P
BLK = 128
MAX_BLK = 2 * T // BLK + N_EXP
ROWS = (MAX_BLK + 1) * BLK
EPS = 1e-6
NEG = -1e30
SCALE = DH ** -0.5
THETA = 500000.0
CLIP = 40.0

C_ID, C_CAUSAL, C_STRICT, C_WIN, C_TRI, C_CMP = 0, 128, 256, 384, 512, 640
C_FREQ = C_CMP + NT * N_CMP
C_KEY = C_FREQ + 8
C_THR = C_KEY + 4
N_THR = T // BLK - 1
C_VALID = C_THR + N_THR
C_TOK = C_VALID + NT
C_ALL = C_TOK + NT


def constants():
    c = np.zeros((P, C_ALL), np.float32)
    r, k = np.arange(P)[:, None], np.arange(P)[None, :]
    c[:, C_ID:C_ID + P] = r == k
    c[:, C_CAUSAL:C_CAUSAL + P] = np.where(k > r, NEG, 0.0)
    c[:, C_STRICT:C_STRICT + P] = np.where(k >= r, NEG, 0.0)
    c[:, C_WIN:C_WIN + P] = np.where(k <= r, NEG, 0.0)
    c[:, C_TRI:C_TRI + P] = r < k
    n = np.arange(N_CMP)[None, :]
    for i in range(NT):
        seen = (n * CMP_STRIDE + CMP_LEN - 1 <= i * P + r) & (n < N_CMP - 1)
        c[:, C_CMP + i * N_CMP:C_CMP + (i + 1) * N_CMP] = np.where(seen, 0.0, NEG)
        c[:, C_VALID + i] = (i * P + r[:, 0]) >= CMP_LEN - 1
        c[:, C_TOK + i] = i * P + r[:, 0]
    c[:, C_FREQ:C_FREQ + 8] = np.float32(THETA) ** (-np.arange(0, 16, 2, dtype=np.float32) / np.float32(16))
    c[:, C_KEY:C_KEY + 4] = [4, 3, 2, 1]
    c[:, C_THR:C_THR + N_THR] = BLK * np.arange(1, N_THR + 1)
    return c


class Link:

    def __init__(self, eng, sem):
        self.eng, self.sem, self.n = eng, sem, 0

    def __call__(self, ins):
        self.n += 1
        ins.then_inc(self.sem, 1)
        self.eng.wait_ge(self.sem, self.n)

    def restart(self):
        self.eng.sem_clear(self.sem)
        self.n = 0


def table_rsqrt(act, m, ln_done, n, out, total, width):
    act.activation(out, total, ACT.Ln, scale=1.0 / width, bias=m.eps[:, 0:1]).then_inc(ln_done, 1)
    act.wait_ge(ln_done, n)
    return act.activation(out, out, ACT.Exp, scale=-0.5)


def newton_rsqrt(dve, link, r, total, width):
    t = total
    link(dve.tensor_scalar(t, total, -0.5 / width, -0.5 * EPS, ALU.mult, ALU.add))
    link(dve.tensor_tensor(t, t, r, ALU.mult))
    link(dve.tensor_tensor(t, t, r, ALU.mult))
    link(dve.scalar_tensor_tensor(out=r, in0=t, scalar=1.5, in1=r, op0=ALU.add, op1=ALU.mult))


class Mem:
    pass


def view(region, off, *shape):
    n = int(np.prod(shape))
    ap = region[:, off:off + n]
    if len(shape) == 2:
        ap = ap.rearrange("p (a b) -> p a b", b=shape[1])
    if len(shape) == 3:
        ap = ap.rearrange("p (a b c) -> p a b c", b=shape[1], c=shape[2])
    if len(shape) == 4:
        ap = ap.rearrange("p (a b c d) -> p a b c d", b=shape[1], c=shape[2], d=shape[3])
    return ap


KB = 256


def hidden_states(nc, ctx, m, a):
    sem = lambda n: ctx.enter_context(nc.semaphore(n))
    x_in = [sem(f"x_in{j}") for j in range(4)]
    const_in, small_in, x_sq, x_norm, h_tr, h_free, x_rstd, x_ln = map(
        sem, ("const_in", "small_in", "x_sq", "x_norm", "h_tr", "h_free", "x_rstd", "x_ln"))
    ang_r, trig, dlink = sem("ang_r"), sem("trig"), sem("dlink_h")
    m.consts_ready = sem("consts_ready")
    x = view(m.V, 0, 4, D)
    junk = view(m.V, 4 * D, D)
    cst = m.S[:, 0:C_ALL]
    tmp = view(m.S, C_ALL, 8, NT, 8)
    ps = m.ps
    freq = cst[:, C_FREQ:C_FREQ + 8]

    with nc.Block() as block:
        @block.sync
        def _(sp):
            sp.dma_start(x[:, 0, :], a.x[0:P, :]).then_inc(x_in[0], 16)
            sp.dma_start(cst, a.cst).then_inc(const_in, 16)
            sp.dma_start(m.ident[:], a.cst[:, C_ID:C_ID + P]).then_inc(const_in, 16)
            with nc.allow_non_contiguous_dma("gain columns, 12 KiB in all"):
                for dst, src in ((m.w_attn, a.attn_norm_w), (m.w_ffn, a.ffn_norm_w)):
                    sp.dma_start(dst[:], src.rearrange("(c p) -> p c", p=P)).then_inc(small_in, 16)
                sp.dma_start(m.w_mix[:, 0:4], a.nsa_out_norm_w.rearrange("(c p) -> p c", p=P)).then_inc(small_in, 16)
                sp.dma_start(m.w_mix[:, 4:8], a.sb_out_norm_w.rearrange("(c p) -> p c", p=P)).then_inc(small_in, 16)
                sp.dma_start(m.pos[:], a.positions.rearrange("(c p) -> p c", p=P)).then_inc(small_in, 16)
            for j in range(1, 4):
                sp.dma_start(x[:, j, :], a.x[j * P:(j + 1) * P, :]).then_inc(x_in[j], 16)
            for j in range(4):
                sp.wait_ge(h_tr, 2 * j + 2)
                sp.dma_start(x[:, j, :], a.x[(4 + j) * P:(5 + j) * P, :]).then_inc(x_in[j], 16)
            for g in range(2):
                sp.dma_start(m.w_ring[:, g, :, :], a.w_in_rows[:, :, m.groups[g]:m.groups[g] + BANK]).then_inc(m.w_loaded[g], 16)
            with nc.allow_non_contiguous_dma("the gate columns, 96 bytes a row"):
                sp.dma_start(m.w_gates[:], a.w_in_rows[:, :, COL_GATE:COL_GATE + N_GATE]).then_inc(m.w_gates_loaded, 16)
                sp.dma_start(m.w_router[:, :, 0:N_GRP], a.router_group_w.rearrange("(c p) n -> p c n", p=P)).then_inc(m.router_in, 16)
                sp.dma_start(m.w_router[:, :, N_GRP:N_GRP + N_EXP], a.router_expert_w.rearrange("(c p) n -> p c n", p=P)).then_inc(m.router_in, 16)
                sp.dma_start(m.b_router[:, 0:N_GRP], a.router_group_b.partition_broadcast(P)).then_inc(m.router_in, 16)
                sp.dma_start(m.b_router[:, N_GRP:N_GRP + N_EXP], a.router_expert_b.partition_broadcast(P)).then_inc(m.router_in, 16)

        @block.scalar
        def _(act):
            act.wait_ge(ang_r, 1)
            act.activation(m.trig[:].rearrange("p a b c -> p (a b c)"), tmp[:, 4:6].rearrange("p a b c -> p (a b c)"), ACT.Sin).then_inc(trig, 1)
            act.preload_act_table_set("natural_log_exp_and_others")
            with act.Fori(0, 2) as it:
                for j in range(4):
                    act.wait_ge(x_in[j], it * 16 + 16)
                    if j == 0:
                        act.wait_ge(x_norm, it * 4 + 1)
                    act.activation(junk, x[:, j, :], ACT.Square, accum_out=m.stat[:, j:j + 1]).then_inc(x_sq, 1)
                    act.wait_ge(x_sq, it * 4 + j + 1)
                    table_rsqrt(act, m, x_ln, it * 4 + j + 1, m.rstd[:, j:j + 1], m.stat[:, j:j + 1], D).then_inc(x_rstd, 1)

        @block.vector
        def _(dve):
            link = Link(dve, dlink)
            dve.memset(m.clip[:], CLIP)
            dve.memset(m.zero_i[:], 0)
            dve.memset(m.one[:], 1.0)
            dve.memset(m.eps[:], EPS).then_inc(x_norm, 1)
            dve.wait_ge(const_in, 32)
            dve.wait_ge(small_in, 80)
            for dst, c0 in ((m.ident_b, C_ID), (m.causal, C_CAUSAL), (m.strict, C_STRICT), (m.winmask, C_WIN), (m.tri, C_TRI)):
                dve.tensor_copy(dst[:], cst[:, c0:c0 + P])
            dve.tensor_copy(m.cmpmask[:].rearrange("p a b -> p (a b)"), cst[:, C_CMP:C_CMP + NT * N_CMP])
            dve.tensor_copy(m.idx_c[:], cst[:, C_KEY:C_ALL])
            dve.memset(m.ones_b[:], 1.0)
            dve.memset(m.ones[:], 1.0)
            pos = tmp[:, 7, :, 0]
            link(dve.tensor_copy(pos, m.pos[:]))
            ang = tmp[:, 0]
            link(dve.tensor_tensor(ang, pos.unsqueeze(2).broadcast_to([P, NT, 8]), freq.unsqueeze(1).broadcast_to([P, NT, 8]), ALU.mult))
            magic = 1.5 * 2 ** 23
            two_pi = 2 * np.pi
            c1 = 6.28125
            c2 = float(np.float32(int((two_pi - c1) * 2 ** 20) / 2 ** 20))
            c3 = two_pi - c1 - c2
            for which, turn, shift in ((0, 0.0, 0.0), (1, 0.25, np.pi / 2)):
                k, r = tmp[:, 2 + which], tmp[:, 4 + which]
                link(dve.tensor_scalar(k, ang, 1.0 / two_pi, turn, ALU.mult, ALU.add))
                link(dve.tensor_scalar(k, k, magic, None, ALU.add))
                link(dve.tensor_scalar(k, k, magic, None, ALU.subtract))
                link(dve.scalar_tensor_tensor(out=r, in0=k, scalar=-c1, in1=ang, op0=ALU.mult, op1=ALU.add))
                link(dve.scalar_tensor_tensor(out=r, in0=k, scalar=-c2, in1=r, op0=ALU.mult, op1=ALU.add))
                link(dve.scalar_tensor_tensor(out=r, in0=k, scalar=-c3, in1=r, op0=ALU.mult, op1=ALU.add))
                if which:
                    link(dve.tensor_scalar(r, r, shift, None, ALU.add))
                ins = dve.tensor_scalar(r, r, 3.1415925, -3.1415925, ALU.min, ALU.max)
                if which:
                    ins.then_inc(ang_r, 1)
                else:
                    link(ins)
            with dve.Fori(0, 2) as it:
                link.restart()
                for j in range(4):
                    dve.wait_ge(x_rstd, it * 4 + j + 1)
                    newton_rsqrt(dve, link, m.rstd[:, j:j + 1], m.stat[:, j:j + 1], D)
                    dve.tensor_scalar(x[:, j, :], x[:, j, :], m.rstd[:, j:j + 1], None, ALU.mult).then_inc(x_norm, 1)
                    for half in range(2):
                        dve.wait_ge(h_tr, it * 8 + 2 * j + half + 1)
                        dve.tensor_tensor(m.hT[:, 4 * half:4 * half + 4, bass.ds(it * 512 + j * P, P)],
                                          ps[:, 4 + half, :].rearrange("p (c n) -> p c n", n=P),
                                          m.w_attn[:, 4 * half:4 * half + 4].unsqueeze(2).broadcast_to([P, 4, P]),
                                          ALU.mult).then_inc(h_free, 1)

        @block.tensor
        def _(pe):
            pe.sem_inc(h_free, 2)
            pe.wait_ge(const_in, 32)
            with pe.Fori(0, 2) as it:
                for j in range(4):
                    pe.wait_ge(x_norm, it * 4 + j + 2)
                    for half in range(2):
                        pe.wait_ge(h_free, it * 8 + 2 * j + half + 1)
                        for c in range(4):
                            ins = pe.transpose(ps[:, 4 + half, c * P:(c + 1) * P], x[:, j, (4 * half + c) * P:(4 * half + c + 1) * P], m.ident[:])
                        ins.then_inc(h_tr, 1)


def projections(nc, ctx, m, a):
    sem = lambda n: ctx.enter_context(nc.semaphore(n))
    mm, mm_free, rot_in, rot, rtmp, tr, tr_free = map(
        sem, ("proj_mm", "proj_free", "rot_in", "rot_done", "rot_link", "rot_tr", "rot_free"))
    gate_mm, gate_exp = sem("gate_mm"), sem("gate_exp")
    chunk_in = [sem(f"chunk_in{j}") for j in range(2)]
    stored = [sem(f"stage_stored{j}") for j in range(4)]
    m.proj_stored = stored
    ps = m.ps
    NB = 4
    stage = view(m.S, 0, 4, BANK)
    rows = view(m.S, 4 * BANK, 2, BANK)
    tmp = view(m.S, 6 * BANK, 4, 64)
    chunk = view(m.V, 0, 2, ND, P)
    cmpw = view(m.V, 2 * ND * P, 2, ND, 2, DH)
    cmp_in = sem("cmp_w_in")
    LOOPC = 2 * SB_H * DH // P
    N_ROW = 3 * NT
    N_LOOP = 2 * LOOPC

    with nc.Block() as block:
        @block.sync
        def _(sp):
            sp.wait_ge(mm, NT)
            sp.dma_start(m.w_ring[:, 0, :, :], a.w_in_rows[:, :, COL_SBV:COL_SBV + BANK]).then_inc(m.w_loaded[0], 16)
            for g in range(KV_G):
                for kv in range(2):
                    c0 = COL_CMP + kv * KV_G * DH + g * DH
                    sp.dma_start(cmpw[:, g, :, kv, :], a.w_in_rows[:, :, c0:c0 + DH]).then_inc(cmp_in, 16)
            sp.dma_start(chunk[:, 0], a.w_in_rows[:, :, COL_SBQ:COL_SBQ + P]).then_inc(chunk_in[0], 16)
            sp.dma_start(chunk[:, 1], a.w_in_rows[:, :, COL_SBQ + P:COL_SBQ + 2 * P]).then_inc(chunk_in[1], 16)
            for t in range(NT):
                sp.wait_ge(mm_free, 2 * NT + t + 1)
                sp.dma_start(m.sbv_d[t], stage[:, t % 4]).then_inc(stored[t % 4], 16)
            with sp.Fori(0, LOOPC // 2) as it:
                for j in range(2):
                    for half in range(2):
                        sp.wait_ge(mm_free, N_ROW + it * 4 + 2 * j + half + 1)
                        sp.dma_start(m.sbqk_rows[bass.ds((it * 2 + j) * P, P), half * BANK:(half + 1) * BANK],
                                     stage[:, 2 * j + half]).then_inc(stored[2 * j + half], 16)
                    with sp.If(it < LOOPC // 2 - 1):
                        sp.wait_ge(mm, N_ROW + it * 4 + 2 * j + 2)
                        sp.dma_start(chunk[:, j], a.w_in_rows[:, :, bass.ds(COL_SBQ + (it * 2 + j + 2) * P, P)]).then_inc(chunk_in[j], 16)

        @block.tensor
        def _(pe):
            def product(n, t, w):
                if n >= NB:
                    pe.wait_ge(mm_free, n - NB + 1)
                for c in range(ND):
                    ins = pe.matmul(ps[:, n % NB, :], m.hT[:, c, t * P:(t + 1) * P], w[:, c, :], start=c == 0, stop=c == ND - 1)
                ins.then_inc(mm, 1)

            def back(k, heads):
                pe.wait_ge(rot, k + 1)
                if k >= 2:
                    pe.wait_ge(tr_free, k - 1)
                for q, c0 in enumerate(heads):
                    ins = pe.transpose(ps[:, 4 + k % 2, q * P:(q + 1) * P], rows[:, k % 2, c0:c0 + P], m.ident[:])
                ins.then_inc(tr, 1)

            q_cols, k_cols = [0, P, 2 * P, 3 * P], [0, 2 * P]
            pe.wait_ge(m.w_loaded[0], 16)
            for t in range(NT):
                product(t, t, m.w_ring[:, 0])
                if t:
                    back(t - 1, q_cols)
            pe.wait_ge(m.w_loaded[1], 16)
            for t in range(NT):
                product(NT + t, t, m.w_ring[:, 1])
                back(NT + t - 1, q_cols if t == 0 else k_cols)
            pe.wait_ge(m.w_gates_loaded, 16)
            for t in range(NT):
                for c in range(ND):
                    ins = pe.matmul(ps[:, 6, t * N_GATE:(t + 1) * N_GATE], m.hT[:, c, t * P:(t + 1) * P], m.w_gates[:, c, :],
                                    start=c == 0, stop=c == ND - 1)
            ins.then_inc(gate_mm, 1)
            back(2 * NT - 1, k_cols)
            pe.wait_ge(m.w_loaded[0], 32)
            for t in range(NT):
                product(2 * NT + t, t, m.w_ring[:, 0])
            with pe.Fori(0, LOOPC // 2) as it:
                for j in range(2):
                    pe.wait_ge(chunk_in[j], it * 16 + 16)
                    for half in range(2):
                        n = 2 * j + half
                        pe.wait_ge(mm_free, it * 4 + N_ROW + n - NB + 1)
                        for c in range(ND):
                            ins = pe.matmul(ps[:, n, :], chunk[:, j, c, :], m.hT[:, c, half * BANK:(half + 1) * BANK],
                                            start=c == 0, stop=c == ND - 1)
                        ins.then_inc(mm, 1)
            pe.wait_ge(cmp_in, 64)
            for g in range(KV_G):
                for half in range(2):
                    n = N_ROW + N_LOOP + 2 * g + half
                    pe.wait_ge(mm_free, n - NB + 1)
                    for c in range(ND):
                        ins = pe.matmul(ps[:, n % NB, :], cmpw[:, g, c].rearrange("p a b -> p (a b)"),
                                        m.hT[:, c, half * BANK:(half + 1) * BANK], start=c == 0, stop=c == ND - 1)
                    ins.then_inc(mm, 1)

        @block.scalar
        def _(act):
            for t in range(NT):
                act.wait_ge(mm, t + 1)
                if t >= 2:
                    act.wait_ge(tr, t - 1)
                act.activation(rows[:, t % 2], ps[:, t % NB, :], ACT.Copy).then_inc(mm_free, 1)
            for t in range(NT):
                n = NT + t
                act.wait_ge(mm, n + 1)
                act.wait_ge(tr, n - 1)
                act.activation(rows[:, n % 2], ps[:, n % NB, :], ACT.Copy).then_inc(rot_in, 1)
                act.activation(m.vsw[:, t, :, :], ps[:, n % NB, :].rearrange("p (w v c) -> p w v c", w=2, v=2)[:, :, 1, :],
                               ACT.Copy).then_inc(mm_free, 1)
            act.wait_ge(gate_mm, 1)
            act.activation(m.gates[:].rearrange("p a b -> p (a b)"), ps[:, 6, 0:NT * N_GATE], ACT.Exp, scale=-1.0).then_inc(gate_exp, 1)
            for t in range(NT):
                n = 2 * NT + t
                act.wait_ge(mm, n + 1)
                if t >= 4:
                    act.wait_ge(stored[t % 4], 16)
                act.activation(stage[:, t % 4], ps[:, n % NB, :], ACT.Copy).then_inc(mm_free, 1)
            with act.Fori(0, LOOPC // 2) as it:
                for n in range(4):
                    act.wait_ge(mm, it * 4 + N_ROW + n + 1)
                    act.wait_ge(stored[n], it * 16 + 32)
                    act.activation(stage[:, n], ps[:, n, :], ACT.Copy).then_inc(mm_free, 1)
            for g in range(KV_G):
                for half in range(2):
                    n = N_ROW + N_LOOP + 2 * g + half
                    act.wait_ge(mm, n + 1)
                    act.activation(m.ckv[:, g, half * BANK:(half + 1) * BANK], ps[:, n % NB, :], ACT.Copy).then_inc(mm_free, 1)

        @block.vector
        def _(dve):
            link = Link(dve, rtmp)

            def rotate(k, t, heads):
                v = heads(rows[:, k % 2])
                nh = NSA_H if len(v.shape) == 3 else 4
                x1, x2 = v[..., 0:8], v[..., 8:16]
                shape = [P] + list(v.shape[1:-1]) + [8]
                sin, cos = m.trig[:, 0, t, :], m.trig[:, 1, t, :]
                for _ in shape[1:-1]:
                    sin, cos = sin.unsqueeze(1), cos.unsqueeze(1)
                sin, cos = sin.broadcast_to(shape), cos.broadcast_to(shape)
                pr = [tmp[:, q, 0:nh * 8].rearrange("p (h c) -> p h c", c=8) if len(shape) == 3 else
                      tmp[:, q, 0:nh * 8].rearrange("p (w h c) -> p w h c", w=2, c=8) for q in range(4)]
                dve.tensor_tensor(pr[0], x1, cos, ALU.mult)
                dve.tensor_tensor(pr[1], x2, sin, ALU.mult)
                dve.tensor_tensor(pr[2], x2, cos, ALU.mult)
                link(dve.tensor_tensor(pr[3], x1, sin, ALU.mult))
                dve.tensor_tensor(x1, pr[0], pr[1], ALU.subtract)
                link(dve.tensor_tensor(x2, pr[2], pr[3], ALU.add))

            q_heads = lambda r: r.rearrange("p (h c) -> p h c", c=DH)[:, :, 0:16]
            k_heads = lambda r: r.rearrange("p (w v h c) -> p w v h c", w=2, v=2, c=DH)[:, :, 0, :, 0:16]

            def collect(k):
                t = k % NT
                dve.wait_ge(tr, k + 1)
                if k < NT:
                    dve.tensor_copy(m.qT[:, :, t * P:(t + 1) * P], ps[:, 4 + k % 2, :].rearrange("p (a b) -> p a b", b=P)).then_inc(tr_free, 1)
                else:
                    dve.tensor_copy(m.kT[:, :, t * P:(t + 1) * P], ps[:, 4 + k % 2, 0:2 * P].rearrange("p (a b) -> p a b", b=P)).then_inc(tr_free, 1)

            for k in range(2 * NT):
                if k < NT:
                    dve.wait_ge(mm_free, k + 1)
                else:
                    dve.wait_ge(rot_in, k - NT + 1)
                rotate(k, k % NT, q_heads if k < NT else k_heads)
                dve.memset(m.mark[:], 0.0).then_inc(rot, 1)
                if k:
                    collect(k - 1)
            collect(2 * NT - 1)
            dve.wait_ge(gate_exp, 1)
            g = m.gates[:].rearrange("p a b -> p (a b)")
            link(dve.tensor_scalar(g, g, 1.0, None, ALU.add))
            link(dve.reciprocal(g, g))


class Count:

    def __init__(self, sem, steps, credit=0):
        self.sem, self.credit = sem, credit
        self.upto = [0]
        for s in steps:
            self.upto.append(self.upto[-1] + s)
        self.total = self.upto[-1]

    def after(self, it, n):
        k = len(self.upto) - 1
        back = 0
        while n < 0:
            n, back = n + k, back + self.total
        c = self.upto[n + 1] - back + self.credit
        return it * self.total + c


def stick_breaking(nc, ctx, m, a):
    sem = lambda n: ctx.enter_context(nc.semaphore(n))
    units = []
    for j in range(2):
        for i in range(NT):
            top = 4 if i >= 4 else 0
            w = i + 1 - top
            if 2 * w <= 4:
                units.append((j, i, [(0, top, i + 1, 0), (1, top, i + 1, w)]))
            else:
                units += [(j, i, [(h, top, i + 1, 0)]) for h in range(2)]
            if top:
                units += [(j, i, [(h, 0, top, 0)]) for h in range(2)]
    N = len(units)
    width = [sum(b1 - b0 for _, b0, b1, _ in u[2]) * P for u in units]
    last = [n + 1 == N or units[n + 1][:2] != units[n][:2] for n in range(N)]
    tile_of = [sum(last[:n]) for n in range(N)]
    one = [1] * N
    loaded = [sem("sb_in0"), sem("sb_in1")]
    scores = Count(sem("sb_scores"), one)
    soft = Count(sem("sb_soft"), one)
    arg = Count(sem("sb_arg"), one, 4)
    prob = Count(sem("sb_prob"), one)
    trans = Count(sem("sb_trans"), one, 4)
    moved = Count(sem("sb_moved"), one, 2)
    summed = Count(sem("sb_summed"), [int(any(b0 == 0 for _, b0, _, _ in u[2])) for u in units], 4)
    out = Count(sem("sb_out"), [1] * sum(last), 2)
    alink, dlink = sem("sb_alink"), sem("sb_dlink")
    ps = m.ps
    q, v = view(m.S, 0, 2, T), view(m.S, 2 * T, 2, NT, P)
    k = m.keys
    zeroed = sem("sb_zeroed")
    E, C, AT = view(m.V, 0, 6, BANK), view(m.V, 6 * BANK, 4, BANK), view(m.S, 4 * T, 4, BANK)
    m.w1 = view(m.Y, 0, CMP_LEN, CMP_HID)
    LAG_P, LAG_T, LAG_W = 2, 3, 4

    def cols(span):
        h, b0, b1, at = span
        return slice(at * P, (at + b1 - b0) * P)

    def later(n, h):
        return next((b, span) for b in range(n) for span in units[b][2] if units[b][:2] == units[n][:2] and span[0] == h)

    with nc.Block() as block:
        @block.sync
        def _(sp):
            def load(j, hp):
                sp.dma_start(q[:, j], m.sbqk_rows[bass.ds(hp * P, P), :]).then_inc(loaded[j], 16)
                for h in range(2):
                    sp.dma_start(k[h * DH:(h + 1) * DH, j, h], m.sbqk_rows[bass.ds(hp * P + SB_H * DH + h * DH, DH), :]).then_inc(loaded[j], 16)
                sp.dma_start(v[:, j], m.sbv_d[:, :, bass.ds(hp * P, P)].rearrange("t p c -> p t c")).then_inc(loaded[j], 16)

            for n in range(4):
                sp.wait_ge(m.proj_stored[n], 96)
            sp.wait_ge(zeroed, 2)
            load(0, 0)
            load(1, 1)
            for kv, (w1, w2, pe_) in enumerate(((a.cmp_k_w1, a.cmp_k_w2, a.cmp_pe_k), (a.cmp_v_w1, a.cmp_v_w2, a.cmp_pe_v))):
                sp.dma_start(m.w1[kv * DH:(kv + 1) * DH], w1.rearrange("(l d) h -> d l h", d=DH)).then_inc(m.cmp_w, 16)
                sp.dma_start(m.pe_rows[:, kv, :], pe_).then_inc(m.cmp_w, 16)
                for dup in range(2):
                    sp.dma_start(m.w2[:, kv, :, dup, :], w2.rearrange("(c p) n -> p c n", p=P)).then_inc(m.cmp_w, 16)
            for j in range(2):
                sp.wait_ge(summed.sem, summed.after(0, (j + 1) * N // 2 - 1))
                load(j, 2 + j)

        @block.tensor
        def _(pe):
            pe.sem_inc(trans.sem, trans.credit)
            pe.sem_inc(summed.sem, summed.credit)

            def score(it, n):
                j, i, spans = units[n]
                if n % (N // 2) == 0:
                    pe.wait_ge(loaded[j], it * 64 + 64)
                pe.wait_ge(arg.sem, arg.after(it, n - 4))
                for span in spans:
                    h, b0, b1, at = span
                    ins = pe.matmul(ps[:, n % 4, cols(span)], q[:, j, i * P:(i + 1) * P], k[:, j, h, b0 * P:b1 * P],
                                    start=True, stop=b1 <= i)
                    if b1 > i:
                        d = (at + i - b0) * P
                        ins = pe.matmul(ps[:, n % 4, d:d + P], m.ident_b[:], m.strict[:], start=False, stop=True)
                ins.then_inc(scores.sem, 1)

            def transpose(it, n):
                pe.wait_ge(prob.sem, prob.after(it, n))
                pe.wait_ge(moved.sem, moved.after(it, n - 2))
                for c in range(width[n] // P):
                    ins = pe.transpose(ps[:, 4 + n % 2, c * P:(c + 1) * P], C[:, n % 4, c * P:(c + 1) * P], m.ident[:])
                ins.then_inc(trans.sem, 1)

            def weigh(it, n):
                j, i, spans = units[n]
                t = tile_of[n]
                pe.wait_ge(moved.sem, moved.after(it, n))
                pe.wait_ge(out.sem, out.after(it, t - 2))
                ins = None
                for span in spans:
                    h, b0, b1, at = span
                    if b0 > 0:
                        continue
                    parts = ([] if b1 > i else [later(n, h)]) + [(n, span)]
                    for b, (_, c0, c1, to) in parts:
                        for c in range(c0, c1):
                            ins = pe.matmul(ps[:, 6 + t % 2, h * DH:(h + 1) * DH], AT[:, b % 4, (to + c - c0) * P:(to + c - c0 + 1) * P],
                                            v[:, j, c, h * DH:(h + 1) * DH], start=c == parts[0][1][1], stop=c == b1 - 1 and b == n)
                if ins:
                    ins.then_inc(summed.sem, 1)

            with pe.Fori(0, 2) as it:
                for s in range(N + LAG_W):
                    if s < N:
                        score(it, s)
                    if 0 <= s - LAG_T < N:
                        transpose(it, s - LAG_T)
                    if s >= LAG_W:
                        weigh(it, s - LAG_W)

        @block.scalar
        def _(act):
            act.sem_inc(out.sem, out.credit)
            link = Link(act, alink)
            with act.Fori(0, 2) as it:
                link.restart()
                for s in range(N + LAG_W + 1):
                    if s < N:
                        e = E[:, s % 6, 0:width[s]]
                        act.wait_ge(scores.sem, scores.after(it, s))
                        act.wait_ge(arg.sem, arg.after(it, s - 4))
                        link(act.activation(e, ps[:, s % 4, 0:width[s]], ACT.Relu, scale=-SCALE, bias=m.clip[:, 0:1]))
                        link(act.activation(e, e, ACT.Exp, scale=-1.0, bias=m.clip[:, 0:1]))
                        act.activation(e, e, ACT.Ln, bias=m.one[:, 0:1]).then_inc(soft.sem, 1)
                    if 0 <= s - LAG_P < N:
                        n = s - LAG_P
                        c = C[:, n % 4, 0:width[n]]
                        act.wait_ge(arg.sem, arg.after(it, n))
                        act.activation(c, c, ACT.Exp).then_inc(prob.sem, 1)
                    n = s - LAG_W - 1
                    if n >= 0 and last[n]:
                        j, i, _ = units[n]
                        act.wait_ge(summed.sem, summed.after(it, n))
                        act.activation(m.o[:, i, bass.ds(it * 2 * P + N_Q + j * P, P)], ps[:, 6 + tile_of[n] % 2, 0:P],
                                       ACT.Copy).then_inc(out.sem, 1)

        @block.vector
        def _(dve):
            for h in range(2):
                dve.memset(k[(1 - h) * DH:(2 - h) * DH, :, h, :], 0.0).then_inc(zeroed, 1)
            dve.sem_inc(arg.sem, arg.credit)
            dve.sem_inc(moved.sem, moved.credit)
            link = Link(dve, dlink)

            def exponent(it, n):
                j, i, spans = units[n]
                w = width[n]
                z, e, c = ps[:, n % 4, 0:w], E[:, n % 6, 0:w], C[:, n % 4, 0:w]
                dve.wait_ge(soft.sem, soft.after(it, n))
                link(dve.scalar_tensor_tensor(out=e, in0=z, scalar=SCALE, in1=e, op0=ALU.mult, op1=ALU.max))
                for x, span in enumerate(spans):
                    h, b0, b1, at = span
                    es = e[:, cols(span)][:, ::-1]
                    start = 0.0
                    if b1 <= i:
                        b, (_, _, _, to) = later(n, h)
                        start = E[:, b % 6, to * P:to * P + 1]
                    ins = dve.tensor_tensor_scan(es, m.one[:, 0:1].broadcast_to([P, (b1 - b0) * P]), es, start, ALU.mult, ALU.add)
                    link(ins)
                dve.wait_ge(trans.sem, trans.after(it, n - 4))
                dve.scalar_tensor_tensor(out=c, in0=z, scalar=SCALE, in1=e, op0=ALU.mult, op1=ALU.subtract).then_inc(arg.sem, 1)

            with dve.Fori(0, 2) as it:
                link.restart()
                for s in range(N + 2):
                    if s < N:
                        exponent(it, s)
                    if s >= 2:
                        n = s - 2
                        dve.wait_ge(trans.sem, trans.after(it, n))
                        dve.wait_ge(summed.sem, summed.after(it, n - 2))
                        dve.tensor_copy(AT[:, n % 4, 0:width[n]], ps[:, 4 + n % 2, 0:width[n]]).then_inc(moved.sem, 1)


def compression(nc, ctx, m, a):
    sem = lambda n: ctx.enter_context(nc.semaphore(n))
    pe_t, pe_c, blocks, hid, hexp, hsilu, fin, clink = map(
        sem, ("cmp_pe_t", "cmp_pe_c", "cmp_blocks", "cmp_hid", "cmp_exp", "cmp_silu", "cmp_fin", "cmp_link"))
    ps = m.ps
    kb = view(m.S, 0, KV_G, CMP_LEN, N_CMP)
    peT = m.S[:, 4096:4096 + CMP_LEN]
    ex = view(m.S, 4352, 2, 2, KV_G * N_CMP)
    hk = view(m.S, 4864, 2, KV_G * N_CMP)
    hv = view(m.S, 5120, 2, KV_G, 2, N_CMP)

    with nc.Block() as block:
        @block.tensor
        def _(pe):
            pe.wait_ge(m.cmp_w, 128)
            pe.transpose(ps[:, 7, 0:CMP_LEN], m.pe_rows[:].rearrange("p a b -> p (a b)"), m.ident[0:CMP_LEN, 0:CMP_LEN]).then_inc(pe_t, 1)
            pe.wait_ge(blocks, 5)
            for kv in range(2):
                lo = kv * DH
                for c in range(2):
                    for l in range(CMP_LEN):
                        ins = pe.matmul(ps[:, 2 * kv + c, 0:P], m.w1[lo:lo + DH, l, c * P:(c + 1) * P], kb[lo:lo + DH, :, l, :],
                                        start=l == 0, stop=l == CMP_LEN - 1)
                    ins.then_inc(hid, 1)
            pe.wait_ge(hsilu, 4)
            for c in range(2):
                pe.matmul(ps[:, 4, 0:P], m.w2[:, 0, c].rearrange("p a b -> p (a b)"), hk[:, c], start=c == 0, stop=c == 1)
            for g in range(KV_G):
                for c in range(2):
                    ins = pe.matmul(ps[:, 5, g * DH:(g + 1) * DH], hv[:, c, g].rearrange("p a b -> p (a b)"), m.w2[:, 1, c, 0],
                                    start=c == 0, stop=c == 1)
            ins.then_inc(fin, 1)

        @block.vector
        def _(dve):
            link = Link(dve, clink)
            dve.wait_ge(pe_t, 1)
            dve.tensor_copy(peT, ps[:, 7, 0:CMP_LEN]).then_inc(pe_c, 1)
            dve.wait_ge(pe_c, 1)
            dve.memset(kb[:, :, CMP_STRIDE:, N_CMP - 1:N_CMP], 0.0).then_inc(blocks, 1)
            for g in range(KV_G):
                src = m.ckv[:, g].rearrange("p (n l) -> p l n", l=CMP_STRIDE)
                for half, n1 in ((0, N_CMP), (1, N_CMP - 1)):
                    l0 = half * CMP_STRIDE
                    dve.tensor_tensor(kb[:, g, l0:l0 + CMP_STRIDE, 0:n1], src[:, :, half:half + n1],
                                      peT[:, l0:l0 + CMP_STRIDE].unsqueeze(2).broadcast_to([P, CMP_STRIDE, n1]), ALU.add).then_inc(blocks, 1)
            for kv in range(2):
                for c in range(2):
                    n = 2 * kv + c
                    e = ex[:, kv, c]
                    dve.wait_ge(hexp, n + 1)
                    link(dve.tensor_scalar(e, e, 1.0, None, ALU.add))
                    link(dve.reciprocal(e, e))
                    if kv == 0:
                        dve.tensor_tensor(hk[:, c], ps[:, n, 0:P], e, ALU.mult).then_inc(hsilu, 1)
                    else:
                        dst = hv[:, c]
                        for dup in range(2):
                            ins = dve.tensor_tensor(dst[:, :, dup, :], ps[:, n, 0:P].rearrange("p (g n) -> p g n", g=KV_G),
                                                    e.rearrange("p (g n) -> p g n", g=KV_G), ALU.mult)
                            if dup == 0:
                                link(ins)
                        ins.then_inc(hsilu, 1)
            dve.wait_ge(fin, 1)
            dve.tensor_copy(m.kc[:].rearrange("p a b -> p (a b)"), ps[:, 4, 0:P])
            dve.tensor_copy(m.vc[:].rearrange("p a b -> p (a b)"), ps[:, 5, 0:P])

        @block.scalar
        def _(act):
            for kv in range(2):
                for c in range(2):
                    act.wait_ge(hid, 2 * kv + c + 1)
                    act.activation(ex[:, kv, c], ps[:, 2 * kv + c, 0:P], ACT.Exp, scale=-1.0).then_inc(hexp, 1)


def native_sparse(nc, ctx, m, a):
    sem = lambda n: ctx.enter_context(nc.semaphore(n))
    items = []
    for i in range(NT):
        items.append(("cmp", i, None, 0, 2))
        for h in range(R_G):
            items.append(("sel", i, h, 0, i + 1))
            items.append(("win", i, h, max(0, i - WIN_TILES), i + 1))
    N = len(items)
    blocks = [b1 - b0 for _, _, _, b0, b1 in items]
    one = [1] * N
    two = [int(b > 4) for b in blocks]
    loaded = sem("nsa_in")
    scores = Count(sem("nsa_scores"), one)
    shift = Count(sem("nsa_shift"), one)
    prob = Count(sem("nsa_prob"), one, 2)
    transA = Count(sem("nsa_transA"), one, 2)
    transB = Count(sem("nsa_transB"), two, 2)
    movedA = Count(sem("nsa_movedA"), one, 2)
    movedB = Count(sem("nsa_movedB"), two, 2)
    summed = Count(sem("nsa_summed"), one, 3)
    added = Count(sem("nsa_added"), one, 4)
    dlink = sem("nsa_dlink")
    ps = m.ps
    q, v = view(m.S, 0, 2, T), view(m.S, 2 * T, 2, NT, DH)
    keys = m.keys
    kc, vc = view(m.S, 3 * T, 2, N_CMP), view(m.S, 3 * T + 2 * N_CMP, 2, DH)
    gate = view(m.S, 3 * T + 4 * N_CMP, NT, 3 * R_G)
    zeroed = sem("nsa_zeroed")
    Pr, PT = view(m.V, 0, 2, T), view(m.V, 2 * T, 2, T)
    L = view(m.V, 4 * T, 4, 8)
    mx = view(m.V, 4 * T + 64, 2, 8)
    valid = m.idx_c[:, C_VALID - C_KEY:C_VALID - C_KEY + NT]

    def s_of(n, w=None):
        b = 2 * (n % 2)
        return ps[:, b:b + 2, :].rearrange("p a b -> p (a b)")[:, 0:w or blocks[n] * P]

    with nc.Block() as block:
        @block.sync
        def _(sp):
            sp.dma_start(m.w_out, a.w_out.rearrange("(c p) n -> p c n", p=P)).then_inc(m.w_out_in, 16)
            sp.wait_ge(zeroed, 2)
            with sp.Fori(0, KV_G) as g:
                sp.wait_ge(summed.sem, g * N + summed.credit)
                sp.dma_start(q, m.qT[:, bass.ds(g * 2, 2), :]).then_inc(loaded, 16)
                for group, mine in ((0, g < 1), (1, g > 0)):
                    with sp.If(mine):
                        for up in range(2):
                            for kind in range(2):
                                sp.dma_start(keys[up * DH:(up + 1) * DH, kind, up], m.kT[group * DH:(group + 1) * DH, kind, :]).then_inc(loaded, 16)
                for b in range(2):
                    sp.dma_start(v[:, b], m.vsw[:, :, b, bass.ds(g * DH, DH)]).then_inc(loaded, 16)
                for up in range(2):
                    half = slice(up * DH, (up + 1) * DH)
                    sp.dma_start(kc[half, up], m.kc[half, g, :]).then_inc(loaded, 16)
                    sp.dma_start(vc[half, up], m.vc[half, g, :]).then_inc(loaded, 16)
                sp.wait_ge(added.sem, g * N + added.credit)
                sp.dma_start(gate, m.gates[:, :, bass.ds(g * 3 * R_G, 3 * R_G)]).then_inc(loaded, 16)
        LOADS = 16 * 12

        @block.tensor
        def _(pe):
            for c in (transA, transB, summed):
                pe.sem_inc(c.sem, c.credit)

            def score(it, n):
                kind, i, h, b0, b1 = items[n]
                if n == 0:
                    pe.wait_ge(loaded, it * LOADS + LOADS)
                pe.wait_ge(prob.sem, prob.after(it, n - 2))
                s = s_of(n, T)
                if kind == "cmp":
                    pe.matmul(s[:, 0:R_G * N_CMP], m.ident_b[:], m.cmpmask[:, i, :].unsqueeze(1).broadcast_to([P, R_G, N_CMP]),
                              start=True, stop=False)
                    for pair in range(2):
                        ins = pe.matmul(s[:, pair * P:(pair + 1) * P], q[:, pair, i * P:(i + 1) * P],
                                        kc.rearrange("p a b -> p (a b)"), start=False, stop=pair == 1)
                    ins.then_inc(scores.sem, 1)
                    return
                w = (b1 - b0) * P
                masks = [(i - b0, m.causal)] + ([(0, m.winmask)] if kind == "win" and i >= WIN_TILES else [])
                for c in range(0, w, BANK):
                    e = min(w, c + BANK)
                    here = [(blk, t) for blk, t in masks if c <= blk * P < e]
                    pe.matmul(s[:, c:e], q[:, h // 2, i * P:(i + 1) * P], keys[:, int(kind == "win"), h % 2, b0 * P + c:b0 * P + e],
                              start=True, stop=not here)
                    for x, (blk, t) in enumerate(here):
                        ins = pe.matmul(s[:, blk * P:(blk + 1) * P], m.ident_b[:], t[:], start=False, stop=x == len(here) - 1)
                ins.then_inc(scores.sem, 1)

            def transpose(it, n):
                pe.wait_ge(prob.sem, prob.after(it, n))
                for bank, c0, t, mv in ((4, 0, transA, movedA), (5, 4, transB, movedB)):
                    if blocks[n] <= c0:
                        continue
                    pe.wait_ge(mv.sem, mv.after(it, n - 1))
                    for c in range(c0, min(c0 + 4, blocks[n])):
                        ins = pe.transpose(ps[:, bank, (c - c0) * P:(c - c0 + 1) * P], Pr[:, n % 2, c * P:(c + 1) * P], m.ident[:])
                    ins.then_inc(t.sem, 1)

            def weigh(it, n):
                kind, i, h, b0, b1 = items[n]
                pe.wait_ge(movedA.sem, movedA.after(it, n))
                pe.wait_ge(movedB.sem, movedB.after(it, n))
                pe.wait_ge(added.sem, added.after(it, n - 2))
                if kind == "cmp":
                    for pair in range(2):
                        ins = pe.matmul(ps[:, 6 + n % 2, pair * P:(pair + 1) * P], PT[:, n % 2, pair * P:(pair + 1) * P],
                                        vc.rearrange("p a b -> p (a b)"), start=True, stop=True)
                else:
                    for c in range(b0, b1):
                        ins = pe.matmul(ps[:, 6 + n % 2, 0:DH], PT[:, n % 2, (c - b0) * P:(c - b0 + 1) * P],
                                        v[:, int(kind == "win"), c, :], start=c == b0, stop=c == b1 - 1)
                ins.then_inc(summed.sem, 1)

            with pe.Fori(0, KV_G) as it:
                for s in range(N + 2):
                    if s < N:
                        score(it, s)
                    if 1 <= s <= N:
                        transpose(it, s - 1)
                    if s >= 2:
                        weigh(it, s - 2)

        @block.scalar
        def _(act):
            act.sem_inc(prob.sem, prob.credit)
            act.sem_inc(movedA.sem, movedA.credit)
            with act.Fori(0, KV_G) as it:
                for s in range(N + 1):
                    if s < N:
                        kind = items[s][0]
                        p = Pr[:, s % 2, 0:blocks[s] * P]
                        act.wait_ge(shift.sem, shift.after(it, s))
                        if kind == "cmp":
                            act.activation(p, p, ACT.Exp, scale=SCALE).then_inc(prob.sem, 1)
                        else:
                            act.wait_ge(transA.sem, transA.after(it, s - 2))
                            act.wait_ge(transB.sem, transB.after(it, s - 2))
                            act.wait_ge(added.sem, added.after(it, s - 4))
                            act.activation(p, s_of(s), ACT.Exp, scale=SCALE, bias=mx[:, s % 2, 4:5],
                                           accum_out=L[:, s % 4, 0:1]).then_inc(prob.sem, 1)
                    if s >= 1:
                        n = s - 1
                        w = min(4, blocks[n]) * P
                        act.wait_ge(transA.sem, transA.after(it, n))
                        act.wait_ge(summed.sem, summed.after(it, n - 2))
                        act.activation(PT[:, n % 2, 0:w], ps[:, 4, 0:w], ACT.Copy).then_inc(movedA.sem, 1)

        @block.vector
        def _(dve):
            dve.memset(kc.rearrange("p a b -> p (a b)"), 0.0).then_inc(zeroed, 1)
            dve.memset(vc.rearrange("p a b -> p (a b)"), 0.0).then_inc(zeroed, 1)
            dve.sem_inc(added.sem, added.credit)
            dve.sem_inc(movedB.sem, movedB.credit)
            link = Link(dve, dlink)

            def shift_of(it, n):
                kind = items[n][0]
                dve.wait_ge(scores.sem, scores.after(it, n))
                dve.wait_ge(prob.sem, prob.after(it, n - 2))
                if kind == "cmp":
                    s = s_of(n, R_G * N_CMP).rearrange("p (h n) -> p h n", h=R_G)
                    p = Pr[:, n % 2, 0:R_G * N_CMP].rearrange("p (h n) -> p h n", h=R_G)
                    link(dve.reduce_max(mx[:, n % 2, 0:R_G], s, AX_X))
                    dve.wait_ge(transA.sem, transA.after(it, n - 2))
                    dve.wait_ge(transB.sem, transB.after(it, n - 2))
                    dve.tensor_tensor(p, s, mx[:, n % 2, 0:R_G].unsqueeze(2).broadcast_to([P, R_G, N_CMP]),
                                      ALU.subtract).then_inc(shift.sem, 1)
                else:
                    link(dve.reduce_max(mx[:, n % 2, 0:1], s_of(n), AX_X))
                    dve.tensor_scalar(mx[:, n % 2, 4:5], mx[:, n % 2, 0:1], -SCALE, None, ALU.mult).then_inc(shift.sem, 1)

            def weight_cmp(it, n):
                i = items[n][1]
                l = L[:, n % 4, 0:R_G]
                dve.wait_ge(prob.sem, prob.after(it, n))
                link(dve.reduce_sum(l, Pr[:, n % 2, 0:R_G * N_CMP].rearrange("p (h n) -> p h n", h=R_G), AX_X))
                link(dve.reciprocal(l, l))
                link(dve.scalar_tensor_tensor(out=l, in0=l, scalar=valid[:, i:i + 1], in1=gate[:, i, 0:3 * R_G:3], op0=ALU.mult, op1=ALU.mult))

            def add(it, n):
                kind, i, h, _, _ = items[n]
                l = L[:, n % 4, 0:R_G if kind == "cmp" else 1]
                if kind == "cmp":
                    dve.wait_ge(summed.sem, summed.after(it, n))
                    o = m.o[:, i, bass.ds(it * R_G * DH, R_G * DH)].rearrange("p (h c) -> p h c", c=DH)
                    link(dve.tensor_tensor(o, ps[:, 6 + n % 2, 0:R_G * DH].rearrange("p (h c) -> p h c", c=DH),
                                           l.unsqueeze(2).broadcast_to([P, R_G, DH]), ALU.mult))
                    dve.memset(m.mark[:], 0.0).then_inc(added.sem, 1)
                    return
                g = 3 * h + (1 if kind == "sel" else 2)
                link(dve.reciprocal(l, l))
                link(dve.tensor_tensor(l, l, gate[:, i, g:g + 1], ALU.mult))
                dve.wait_ge(summed.sem, summed.after(it, n))
                o = m.o[:, i, bass.ds(it * R_G * DH + h * DH, DH)]
                dve.scalar_tensor_tensor(out=o, in0=ps[:, 6 + n % 2, 0:DH], scalar=l, in1=o, op0=ALU.mult,
                                         op1=ALU.add).then_inc(added.sem, 1)

            with dve.Fori(0, KV_G) as it:
                link.restart()
                dve.wait_ge(loaded, it * LOADS + LOADS)
                for s in range(N + 2):
                    if s < N:
                        shift_of(it, s)
                    if 1 <= s <= N and two[s - 1]:
                        n = s - 1
                        w = (blocks[n] - 4) * P
                        dve.wait_ge(transB.sem, transB.after(it, n))
                        dve.wait_ge(summed.sem, summed.after(it, n - 2))
                        dve.tensor_copy(PT[:, n % 2, 4 * P:4 * P + w], ps[:, 5, 0:w]).then_inc(movedB.sem, 1)
                    if 1 <= s <= N and items[s - 1][0] == "cmp":
                        weight_cmp(it, s - 1)
                    if s >= 2:
                        add(it, s - 2)


def mix_and_route(nc, ctx, m, a):
    sem = lambda n: ctx.enter_context(nc.semaphore(n))
    U = 4
    one = [1] * U
    x_in = [sem(f"res_in{j}") for j in range(2)]
    o_sq = Count(sem("mix_sq"), one)
    o_norm = Count(sem("mix_norm"), one, 3)
    o_tr = Count(sem("mix_tr"), [2] * U, 5)
    oT_in = Count(sem("mix_oT"), [2] * U, 2)
    proj = Count(sem("mix_proj"), one, 3)
    x1_done = Count(sem("mix_x1"), one, 3)
    h_sq = Count(sem("ffn_sq"), one)
    h_norm = Count(sem("ffn_norm"), one, 3)
    h_tr = Count(sem("ffn_tr"), [2] * U, 5)
    hT_in = Count(sem("ffn_hT"), [2] * U, 2)
    logit = Count(sem("logits_mm"), one, 3)
    logit_in = Count(sem("logits_in"), one, 2)
    stored = [sem(f"h_stored{j}") for j in range(2)]
    m.h_stored = stored
    aln, dlink = sem("mix_ln"), sem("mix_dlink")
    ps = m.ps
    xt, oT, hr = view(m.V, 0, 2, D), view(m.V, 2 * D, 2, ND, P), view(m.V, 4 * D, 2, D)
    hT, junk = view(m.S, 0, 2, ND, P), view(m.S, 2 * D, D)
    o_stage = view(m.S, 3 * D, 2, D)
    st = view(m.S, 5 * D, 2, 8)
    st2 = view(m.S, 5 * D + 16, 2, 8)

    with nc.Block() as block:
        @block.sync
        def _(sp):
            sp.sem_inc(stored[0], 16)
            sp.sem_inc(stored[1], 16)
            sp.dma_start(m.list_d.rearrange("(p n) o -> p (n o)", p=P), m.zero_i[:]).then_inc(m.list_zero, 16)
            with sp.Fori(0, NT // U) as it:
                for n in range(U + 2):
                    if n < U:
                        sp.wait_ge(x1_done.sem, x1_done.after(it, n - 2))
                        sp.dma_start(xt[:, n % 2], a.x[bass.ds((it * U + n) * P, P), :]).then_inc(x_in[n % 2], 16)
                    if n >= 2:
                        k = n - 2
                        sp.wait_ge(h_norm.sem, h_norm.after(it, k))
                        sp.dma_start(m.h_d[bass.ds((it * U + k) * P, P), :], hr[:, k % 2]).then_inc(stored[k % 2], 16)

        @block.scalar
        def _(act):
            link = Link(act, aln)
            with act.Fori(0, NT // U) as it:
                link.restart()
                for s in range(U + 1):
                    if s < U:
                        t = it * U + s
                        act.wait_ge(o_norm.sem, o_norm.after(it, s - 2))
                        for g in range(2):
                            link(act.activation(junk[:, 0:N_Q], m.o[:, bass.ds(t, 1), g * N_Q:(g + 1) * N_Q].rearrange("p a b -> p (a b)"),
                                                ACT.Square, accum_out=st[:, s % 2, g:g + 1]))
                        r = st[:, s % 2, 4:6]
                        link(act.activation(r, st[:, s % 2, 0:2], ACT.Ln, scale=1.0 / N_Q, bias=m.eps[:, 0:1]))
                        act.activation(r, r, ACT.Exp, scale=-0.5).then_inc(o_sq.sem, 1)
                    if s >= 1:
                        n = s - 1
                        t = it * U + n
                        act.wait_ge(x1_done.sem, x1_done.after(it, n))
                        act.wait_ge(h_norm.sem, h_norm.after(it, n - 2))
                        link(act.activation(junk, m.x1[:, bass.ds(t, 1), :].rearrange("p a b -> p (a b)"), ACT.Square,
                                            accum_out=st2[:, n % 2, 0:1]))
                        r = st2[:, n % 2, 4:5]
                        link(act.activation(r, st2[:, n % 2, 0:1], ACT.Ln, scale=1.0 / D, bias=m.eps[:, 0:1]))
                        act.activation(r, r, ACT.Exp, scale=-0.5).then_inc(h_sq.sem, 1)

        @block.vector
        def _(dve):
            for c in (o_norm, oT_in, x1_done, h_norm, hT_in, logit_in):
                dve.sem_inc(c.sem, c.credit)
            link = Link(dve, dlink)

            def gain(it, n, tr, done, w, dst, bank, used):
                dve.wait_ge(used.sem, used.after(it, n - 2))
                for half in range(2):
                    dve.wait_ge(tr.sem, tr.after(it, n) - 1 + half)
                    dve.tensor_tensor(dst[:, n % 2, 4 * half:4 * half + 4, :], ps[:, bank + half, :].rearrange("p (c n) -> p c n", n=P),
                                      w[:, 4 * half:4 * half + 4].unsqueeze(2).broadcast_to([P, 4, P]), ALU.mult).then_inc(done.sem, 1)

            with dve.Fori(0, NT // U) as it:
                link.restart()
                for s in range(U + 2):
                    if s < U:
                        t = it * U + s
                        dve.wait_ge(o_sq.sem, o_sq.after(it, s))
                        newton_rsqrt(dve, link, st[:, s % 2, 4:6], st[:, s % 2, 0:2], N_Q)
                        dve.wait_ge(o_tr.sem, o_tr.after(it, s - 2))
                        for g in range(2):
                            o = m.o[:, bass.ds(t, 1), g * N_Q:(g + 1) * N_Q].rearrange("p a b -> p (a b)")
                            ins = dve.tensor_scalar(o_stage[:, s % 2, g * N_Q:(g + 1) * N_Q], o, st[:, s % 2, 4 + g:5 + g], None, ALU.mult)
                        ins.then_inc(o_norm.sem, 1)
                        gain(it, s, o_tr, oT_in, m.w_mix, oT, 0, proj)
                    if 1 <= s <= U:
                        n = s - 1
                        t = it * U + n
                        dve.wait_ge(proj.sem, proj.after(it, n))
                        dve.wait_ge(x_in[n % 2], it * 16 * (U // 2) + 16 * (n // 2) + 16)
                        dve.tensor_tensor(m.x1[:, bass.ds(t, 1), :].rearrange("p a b -> p (a b)"),
                                          ps[:, 2:4, :].rearrange("p a b -> p (a b)"), xt[:, n % 2], ALU.add).then_inc(x1_done.sem, 1)
                        dve.wait_ge(h_sq.sem, h_sq.after(it, n))
                        newton_rsqrt(dve, link, st2[:, n % 2, 4:5], st2[:, n % 2, 0:1], D)
                        dve.wait_ge(stored[n % 2], it * 16 * (U // 2) + 16 * (n // 2) + 16)
                        dve.wait_ge(h_tr.sem, h_tr.after(it, n - 2))
                        dve.tensor_scalar(hr[:, n % 2], m.x1[:, bass.ds(t, 1), :].rearrange("p a b -> p (a b)"), st2[:, n % 2, 4:5], None,
                                          ALU.mult).then_inc(h_norm.sem, 1)
                    if s >= 2:
                        n = s - 2
                        t = it * U + n
                        gain(it, n, h_tr, hT_in, m.w_ffn, hT, 4, logit)
                        dve.wait_ge(logit.sem, logit.after(it, n))
                        dve.tensor_tensor(m.logits[:, bass.ds(t, 1), :].rearrange("p a b -> p (a b)"), ps[:, 6, 0:N_GRP + N_EXP],
                                          m.b_router[:], ALU.add).then_inc(logit_in.sem, 1)

        @block.tensor
        def _(pe):
            for c in (o_tr, proj, h_tr, logit):
                pe.sem_inc(c.sem, c.credit)
            pe.wait_ge(m.w_out_in, 16)
            pe.wait_ge(m.router_in, 64)
            with pe.Fori(0, NT // U) as it:
                for s in range(U + 2):
                    if s < U:
                        pe.wait_ge(o_norm.sem, o_norm.after(it, s))
                        for half in range(2):
                            pe.wait_ge(oT_in.sem, oT_in.after(it, s - 1) - 1 + half)
                            for c in range(4):
                                k = 4 * half + c
                                ins = pe.transpose(ps[:, half, c * P:(c + 1) * P], o_stage[:, s % 2, k * P:(k + 1) * P], m.ident[:])
                            ins.then_inc(o_tr.sem, 1)
                    if 1 <= s <= U:
                        n = s - 1
                        pe.wait_ge(oT_in.sem, oT_in.after(it, n))
                        pe.wait_ge(x1_done.sem, x1_done.after(it, n - 1))
                        for half in range(2):
                            for c in range(ND):
                                ins = pe.matmul(ps[:, 2 + half, :], oT[:, n % 2, c, :], m.w_out[:, c, half * BANK:(half + 1) * BANK],
                                                start=c == 0, stop=c == ND - 1)
                        ins.then_inc(proj.sem, 1)
                    if s >= 2:
                        n = s - 2
                        pe.wait_ge(h_norm.sem, h_norm.after(it, n))
                        for half in range(2):
                            pe.wait_ge(hT_in.sem, hT_in.after(it, n - 1) - 1 + half)
                            for c in range(4):
                                k = 4 * half + c
                                ins = pe.transpose(ps[:, 4 + half, c * P:(c + 1) * P], hr[:, n % 2, k * P:(k + 1) * P], m.ident[:])
                            ins.then_inc(h_tr.sem, 1)
                        pe.wait_ge(hT_in.sem, hT_in.after(it, n))
                        pe.wait_ge(logit_in.sem, logit_in.after(it, n - 1))
                        for c in range(ND):
                            ins = pe.matmul(ps[:, 6, 0:N_GRP + N_EXP], hT[:, n % 2, c, :], m.w_router[:, c, :], start=c == 0, stop=c == ND - 1)
                        ins.then_inc(logit.sem, 1)


def route(nc, ctx, m, a):
    sem = lambda n: ctx.enter_context(nc.semaphore(n))
    link_s, dif, ex_s, hot, rank, table, listed = map(
        sem, ("route_link", "route_dif", "route_exp", "route_hot", "route_rank", "route_table", "route_listed"))
    ps = m.ps
    r4 = lambda k: view(m.S, k * 32, NT, 4)
    eq, key, og, df, es, o1, o2, e2 = (r4(k) for k in range(8))
    r1 = lambda k: m.S[:, 256 + 8 * k:264 + 8 * k]
    gmax, kmax, gg, m1, m2, ex, den = (r1(k) for k in range(7))
    r16 = lambda k: view(m.S, 512 + k * 128, NT, N_GRP, E_PG)
    sel, H1, H2, dst, pick = (r16(k) for k in range(5))
    cnt, nb, end, start = (m.S[:, 1280 + 16 * k:1296 + 16 * k] for k in range(4))
    over = view(m.S, 1408, N_EXP, N_THR)
    d_f = view(m.S, 1600, 2, NT)
    gl = m.logits[:, :, 0:N_GRP]
    el = m.logits[:, :, N_GRP:].rearrange("p t (g e) -> p t g e", g=N_GRP)
    keys = m.idx_c[:, 0:4].unsqueeze(1).broadcast_to([P, NT, 4])
    thr = m.idx_c[:, C_THR - C_KEY:C_THR - C_KEY + N_THR].unsqueeze(1).broadcast_to([P, N_EXP, N_THR])
    over4 = lambda v: v.unsqueeze(2).broadcast_to([P, NT, 4])

    with nc.Block() as block:
        @block.vector
        def _(dve):
            link = Link(dve, link_s)

            def first_max(v, top, hot_):
                link(dve.reduce_max(top, v, AX_X))
                link(dve.tensor_tensor(eq, v, over4(top), ALU.is_equal))
                link(dve.tensor_tensor(key, eq, keys, ALU.mult))
                link(dve.reduce_max(kmax, key, AX_X))
                link(dve.tensor_tensor(hot_, key, over4(kmax), ALU.is_equal))

            first_max(gl, gmax, og)
            dve.tensor_tensor(df, gl, over4(gmax), ALU.subtract).then_inc(dif, 1)
            link(dve.tensor_tensor(sel, el, og.unsqueeze(3).broadcast_to([P, NT, N_GRP, E_PG]), ALU.mult))
            link(dve.reduce_sum(es, sel.rearrange("p t g e -> p t e g"), AX_X))
            first_max(es, m1, o1)
            link(dve.scalar_tensor_tensor(out=e2.rearrange("p a b -> p (a b)"), in0=o1.rearrange("p a b -> p (a b)"), scalar=NEG,
                                          in1=es.rearrange("p a b -> p (a b)"), op0=ALU.mult, op1=ALU.add))
            first_max(e2, m2, o2)
            dve.tensor_tensor(ex, m2, m1, ALU.subtract).then_inc(dif, 1)
            for hot_, o in ((H1, o1), (H2, o2)):
                link(dve.tensor_tensor(hot_, og.unsqueeze(3).broadcast_to([P, NT, N_GRP, E_PG]),
                                       o.unsqueeze(2).broadcast_to([P, NT, N_GRP, E_PG]), ALU.mult))
            dve.tensor_tensor(m.hot[:].rearrange("p t (g e) -> p t g e", g=N_GRP), H1, H2, ALU.add).then_inc(hot, 1)
            dve.wait_ge(ex_s, 2)
            link(dve.reduce_sum(gg, df, AX_X))
            link(dve.tensor_scalar(den, ex, 1.0, None, ALU.add))
            link(dve.tensor_tensor(den, den, gg, ALU.mult))
            link(dve.reciprocal(m.weight[:, 0, :], den))
            link(dve.tensor_tensor(m.weight[:, 1, :], m.weight[:, 0, :], ex, ALU.mult))
            dve.wait_ge(rank, 1)
            link(dve.tensor_copy(cnt, ps[:, 1, 0:N_EXP]))
            link(dve.tensor_tensor(over, cnt.unsqueeze(2).broadcast_to([P, N_EXP, N_THR]), thr, ALU.is_gt))
            link(dve.reduce_sum(nb, over, AX_X))
            link(dve.tensor_scalar(nb, nb, 1.0, None, ALU.add))
            link(dve.tensor_tensor_scan(end, m.one[:, 0:1].broadcast_to([P, N_EXP]), nb, 0.0, ALU.mult, ALU.add))
            link(dve.tensor_tensor(start, end, nb, ALU.subtract))
            link(dve.tensor_copy(m.blocks[:, 2 * N_EXP:3 * N_EXP], start))
            link(dve.tensor_scalar(m.blocks[:, 3 * N_EXP:], end[:, N_EXP - 1:N_EXP], -1.0, MAX_BLK + 1.0, ALU.mult, ALU.add))
            link(dve.tensor_scalar(start, start, float(BLK), None, ALU.mult))
            d16 = dst.rearrange("p t g e -> p t (g e)")
            link(dve.tensor_tensor(d16, ps[:, 0, 0:NT * N_EXP].rearrange("p (t e) -> p t e", e=N_EXP),
                                   start.unsqueeze(1).broadcast_to([P, NT, N_EXP]), ALU.add))
            for k, hot_ in enumerate((H1, H2)):
                link(dve.tensor_tensor(pick, hot_, dst, ALU.mult))
                link(dve.reduce_sum(d_f[:, k, :], pick.rearrange("p t g e -> p t (g e)"), AX_X))
            dve.tensor_copy(m.dest[:].rearrange("p a b -> p (a b)"), d_f.rearrange("p a b -> p (a b)"))
            dve.tensor_copy(m.tokens[:], m.idx_c[:, C_TOK - C_KEY:C_TOK - C_KEY + NT])
            dve.tensor_copy(m.blocks[:, 0:N_EXP], nb)
            dve.tensor_copy(m.blocks[:, N_EXP:2 * N_EXP], end).then_inc(table, 1)

        @block.scalar
        def _(act):
            act.wait_ge(dif, 1)
            act.activation(df, df, ACT.Exp).then_inc(ex_s, 1)
            act.wait_ge(dif, 2)
            act.activation(ex, ex, ACT.Exp).then_inc(ex_s, 1)

        @block.tensor
        def _(pe):
            pe.wait_ge(hot, 1)
            for t in range(NT):
                for u in range(t + 1):
                    pe.matmul(ps[:, 0, t * N_EXP:(t + 1) * N_EXP], m.tri[:] if u == t else m.ones_b[:], m.hot[:, u, :],
                              start=u == 0, stop=u == t)
            for t in range(NT):
                ins = pe.matmul(ps[:, 1, 0:N_EXP], m.ones_b[:], m.hot[:, t, :], start=t == 0, stop=t == NT - 1)
            ins.then_inc(rank, 1)

        @block.gpsimd
        def _(pool):
            pool.wait_ge(m.list_zero, 16)
            pool.wait_ge(table, 1)
            for k in range(2):
                for t in range(NT):
                    pool.indirect_dma_start(m.list_d, bass.IndirectOffsetOnAxis(ap=m.dest[:, k, t:t + 1], axis=0),
                                            m.tokens[:, t:t + 1], None).then_inc(listed, 16)

        @block.sync
        def _(sp):
            load_expert(sp, nc, m, a, 0, 0)
            load_expert(sp, nc, m, a, 1, 1)
            sp.wait_ge(listed, 16 * 2 * NT)
            with nc.allow_non_contiguous_dma("17 KiB of row numbers, to one block a column"):
                sp.dma_start(m.row_tok[:], m.list_d.rearrange("(b p) o -> p (b o)", p=P)).then_inc(m.rows_in, 16)


def load_expert(eng, nc, m, a, slot, e):
    g, u, d = m.expert[slot]
    eng.dma_start(g, a.w_gate_rows[bass.ds(e * D, D), :].rearrange("(c p) f -> p c f", p=P)).then_inc(m.wg_in[slot], 16)
    eng.dma_start(u, a.w_up_rows[bass.ds(e * D, D), :].rearrange("(c p) f -> p c f", p=P)).then_inc(m.wu_in[slot], 16)
    eng.dma_start(d, a.w_down_rows[bass.ds(e * FF, FF), :].rearrange("(c p) f -> p c f", p=P)).then_inc(m.wd_in[slot], 16)


def experts(nc, ctx, m, a):
    sem = lambda n: ctx.enter_context(nc.semaphore(n))
    idx_s, x_tr, x_in, g_mm, u_mm, silu, hidden, h_tr, h_in, y_mm, y_out = map(
        sem, ("moe_idx", "moe_x_tr", "moe_x_in", "moe_gate", "moe_up", "moe_silu", "moe_hidden", "moe_h_tr", "moe_h_in",
              "moe_down", "moe_y_out"))
    gathered, m.y_stored, m.y_zeroed, zeroed = sem("moe_gathered"), sem("moe_y_stored"), sem("moe_y_zeroed"), sem("moe_zeros")
    zeros = m.M[:, NF * D:NF * D + D]
    ps = m.ps
    xg, xT = view(m.S, 0, D), view(m.S, D, ND, P)
    sg, hm, hT, y = view(m.S, 2 * D, FF), view(m.S, 2 * D + FF, FF), view(m.S, 3 * D, NF, P), view(m.S, 3 * D + FF, D)

    def blocks_in_all(eng):
        return eng.value_load(m.blocks[0:1, 2 * N_EXP - 1:2 * N_EXP], min_val=N_EXP, max_val=MAX_BLK)

    with nc.Block() as block:
        @block.sync
        def _(sp):
            sp.wait_ge(zeroed, 1)
            with sp.Fori(blocks_in_all(sp), MAX_BLK + 1) as b:
                sp.dma_start(m.y_d[bass.ds(b * P, P), :], zeros).then_inc(m.y_zeroed, 16)
            with sp.Fori(0, (N_EXP - 2) // 2) as it:
                for slot in range(2):
                    end = sp.value_load(m.blocks[0:1, bass.ds(N_EXP + it * 2 + slot, 1)], min_val=1, max_val=MAX_BLK)
                    sp.wait_ge(y_mm, end + 1)
                    load_expert(sp, nc, m, a, slot, it * 2 + slot + 2)

        @block.gpsimd
        def _(pool):
            pool.wait_ge(m.rows_in, 16)
            for j in range(2):
                pool.wait_ge(m.h_stored[j], 80)
            n = blocks_in_all(pool)
            with pool.Fori(0, n + 1) as b:
                pool.sem_clear(idx_s)
                pool.wait_ge(x_tr, b + 1)
                pool.tensor_copy(m.row_now[:], m.row_tok[:, bass.ds(b, 1)]).then_inc(idx_s, 1)
                pool.wait_ge(idx_s, 1)
                pool.indirect_dma_start(xg, None, m.h_d, bass.IndirectOffsetOnAxis(ap=m.row_now[:], axis=0)).then_inc(gathered, 16)
                pool.wait_ge(gathered, b * 16 + 16)

        @block.tensor
        def _(pe):
            pe.sem_inc(x_tr, 1)
            pe.sem_inc(y_mm, 1)
            pe.sem_inc(u_mm, 1)

            def transpose_x(b):
                pe.wait_ge(gathered, b * 16 + 16)
                for half in range(2):
                    for c in range(4):
                        k = 4 * half + c
                        ins = pe.transpose(ps[:, 2 + half, c * P:(c + 1) * P], xg[:, k * P:(k + 1) * P], m.ident[:])
                ins.then_inc(x_tr, 1)

            transpose_x(0)
            with pe.Fori(0, N_EXP // 2) as it:
                for slot in range(2):
                    wg, wu, wd = m.expert[slot]
                    n = pe.value_load(m.blocks[0:1, bass.ds(it * 2 + slot, 1)], min_val=1, max_val=NT)
                    before = pe.value_load(m.blocks[0:1, bass.ds(2 * N_EXP + it * 2 + slot, 1)], min_val=0, max_val=MAX_BLK)
                    with pe.Fori(0, n) as k:
                        b = before + k
                        pe.wait_ge(m.wg_in[slot], it * 16 + 16)
                        pe.wait_ge(m.wu_in[slot], it * 16 + 16)
                        pe.wait_ge(m.wd_in[slot], it * 16 + 16)
                        pe.wait_ge(x_in, b + 1)
                        pe.wait_ge(silu, b + 1)
                        for c in range(ND):
                            ins = pe.matmul(ps[:, 0, :], xT[:, c, :], wg[:, c, :], start=c == 0, stop=c == ND - 1)
                        ins.then_inc(g_mm, 1)
                        pe.wait_ge(hidden, b + 1)
                        for c in range(ND):
                            ins = pe.matmul(ps[:, 1, :], xT[:, c, :], wu[:, c, :], start=c == 0, stop=c == ND - 1)
                        ins.then_inc(u_mm, 1)
                        transpose_x(b + 1)
                        pe.wait_ge(hidden, b + 2)
                        pe.wait_ge(h_in, b + 1)
                        for f in range(NF):
                            ins = pe.transpose(ps[:, 4, f * P:(f + 1) * P], hm[:, f * P:(f + 1) * P], m.ident[:])
                        ins.then_inc(h_tr, 1)
                        pe.wait_ge(h_in, b + 2)
                        pe.wait_ge(y_out, b + 1)
                        for half in range(2):
                            for f in range(NF):
                                ins = pe.matmul(ps[:, 5 + half, :], hT[:, f, :], wd[:, f, half * BANK:(half + 1) * BANK],
                                                start=f == 0, stop=f == NF - 1)
                        ins.then_inc(y_mm, 1)

        @block.scalar
        def _(act):
            act.preload_act_table_set("silu_and_others")
            act.sem_inc(silu, 1)
            act.sem_inc(h_in, 1)
            act.sem_inc(y_out, 1)
            act.sem_inc(m.y_stored, 16)
            n = blocks_in_all(act)
            with act.Fori(0, n) as b:
                act.wait_ge(g_mm, b + 1)
                act.wait_ge(hidden, b + 1)
                act.activation(sg, ps[:, 0, :], ACT.Silu).then_inc(silu, 1)
                act.wait_ge(h_tr, b + 1)
                act.wait_ge(y_mm, b + 1)
                act.activation(hT.rearrange("p a b -> p (a b)"), ps[:, 4, :], ACT.Copy).then_inc(h_in, 1)
                act.wait_ge(y_mm, b + 2)
                act.wait_ge(m.y_stored, b * 16 + 16)
                act.activation(y, ps[:, 5:7, :].rearrange("p a b -> p (a b)"), ACT.Copy).then_inc(y_out, 1)
                act.wait_ge(y_out, b + 2)
                act.dma_start(m.y_d[bass.ds(b * P, P), :], y).then_inc(m.y_stored, 16)

        @block.vector
        def _(dve):
            dve.memset(zeros, 0.0).then_inc(zeroed, 1)
            dve.sem_inc(hidden, 1)
            n = blocks_in_all(dve)

            def rows_in(b):
                dve.wait_ge(x_tr, b + 2)
                dve.wait_ge(u_mm, b + 1)
                dve.tensor_tensor(xT, ps[:, 2:4, :].rearrange("p a (c n) -> p (a c) n", n=P),
                                  m.w_ffn[:].unsqueeze(2).broadcast_to([P, ND, P]), ALU.mult).then_inc(x_in, 1)

            rows_in(0)
            with dve.Fori(0, n) as b:
                dve.wait_ge(silu, b + 2)
                dve.wait_ge(u_mm, b + 2)
                dve.tensor_tensor(hm, sg, ps[:, 1, :], ALU.mult).then_inc(hidden, 1)
                rows_in(b + 1)


def combine(nc, ctx, m, a, out):
    sem = lambda n: ctx.enter_context(nc.semaphore(n))
    one = [1, 1]
    gathered = [sem("end_g0"), sem("end_g1")]
    idx_s = sem("end_idx")
    added = Count(sem("end_added"), one, 3)
    sq = Count(sem("end_sq"), one)
    done = Count(sem("end_done"), one, 3)
    stored = [sem("out_stored0"), sem("out_stored1")]
    aln, dlink, wf = sem("end_ln"), sem("end_dlink"), sem("end_wf")
    y = view(m.X, 0, 2, 2, D)
    acc, junk, w = view(m.X, 4 * D, 2, D), view(m.X, 6 * D, D), view(m.X, 7 * D, D)
    o = view(m.Y, 0, 2, D)
    st = view(m.S, 0, 2, 8)

    with nc.Block() as block:
        @block.gpsimd
        def _(pool):
            n = pool.value_load(m.blocks[0:1, 2 * N_EXP - 1:2 * N_EXP], min_val=N_EXP, max_val=MAX_BLK)
            unused = pool.value_load(m.blocks[0:1, 3 * N_EXP:3 * N_EXP + 1], min_val=1, max_val=MAX_BLK + 1 - N_EXP)
            with pool.Fori(0, NT // 2) as it:
                pool.sem_clear(idx_s)
                pool.wait_ge(m.y_stored, n * 16 + 16)
                pool.wait_ge(m.y_zeroed, unused * 16)
                for s in range(2):
                    pool.wait_ge(added.sem, added.after(it, s - 2))
                    for k in range(2):
                        pool.tensor_copy(m.dest_now[:, s, k:k + 1], m.dest[:, k, bass.ds(it * 2 + s, 1)]).then_inc(idx_s, 1)
                        pool.wait_ge(idx_s, 2 * s + k + 1)
                        pool.indirect_dma_start(y[:, s, k], None, m.y_d, bass.IndirectOffsetOnAxis(ap=m.dest_now[:, s, k:k + 1], axis=0)).then_inc(gathered[s], 16)

        @block.vector
        def _(dve):
            dve.sem_inc(added.sem, added.credit)
            dve.sem_inc(done.sem, done.credit)
            link = Link(dve, dlink)
            dve.wait_ge(wf, 16)
            with dve.Fori(0, NT // 2) as it:
                link.restart()
                for s in range(2):
                    t = it * 2 + s
                    dve.wait_ge(gathered[s], it * 32 + 32)
                    x1 = m.x1[:, bass.ds(t, 1), :].rearrange("p a b -> p (a b)")
                    wt = [m.weight[:, k, bass.ds(t, 1)] for k in range(2)]
                    link(dve.scalar_tensor_tensor(out=acc[:, s], in0=y[:, s, 0], scalar=wt[0], in1=x1, op0=ALU.mult, op1=ALU.add))
                    dve.scalar_tensor_tensor(out=acc[:, s], in0=y[:, s, 1], scalar=wt[1], in1=acc[:, s], op0=ALU.mult,
                                             op1=ALU.add).then_inc(added.sem, 1)
                    dve.wait_ge(sq.sem, sq.after(it, s))
                    newton_rsqrt(dve, link, st[:, s, 4:5], st[:, s, 0:1], D)
                    dve.wait_ge(stored[s], it * 16 + 16)
                    dve.scalar_tensor_tensor(out=o[:, s], in0=acc[:, s], scalar=st[:, s, 4:5], in1=w, op0=ALU.mult,
                                             op1=ALU.mult).then_inc(done.sem, 1)

        @block.scalar
        def _(act):
            act.preload_act_table_set("natural_log_exp_and_others")
            link = Link(act, aln)
            with act.Fori(0, NT // 2) as it:
                link.restart()
                for s in range(2):
                    act.wait_ge(added.sem, added.after(it, s))
                    act.wait_ge(done.sem, done.after(it, s - 2))
                    link(act.activation(junk, acc[:, s], ACT.Square, accum_out=st[:, s, 0:1]))
                    r = st[:, s, 4:5]
                    link(act.activation(r, st[:, s, 0:1], ACT.Ln, scale=1.0 / D, bias=m.eps[:, 0:1]))
                    act.activation(r, r, ACT.Exp, scale=-0.5).then_inc(sq.sem, 1)

        @block.sync
        def _(sp):
            for s in range(2):
                sp.sem_inc(stored[s], 16)
            sp.dma_start(w, a.final_norm_w.partition_broadcast(P)).then_inc(wf, 16)
            with sp.Fori(0, NT // 2) as it:
                for s in range(2):
                    sp.wait_ge(done.sem, done.after(it, s))
                    sp.dma_start(out[bass.ds((it * 2 + s) * P, P), :], o[:, s]).then_inc(stored[s], 16)
            for s in range(2):
                sp.wait_ge(stored[s], 16 + 16 * (NT // 2))


INPUTS = ["x", "positions", "attn_norm_w", "w_in", "cmp_pe_k", "cmp_pe_v", "cmp_k_w1", "cmp_k_w2", "cmp_v_w1",
          "cmp_v_w2", "nsa_out_norm_w", "sb_out_norm_w", "w_out", "ffn_norm_w", "router_group_w",
          "router_group_b", "router_expert_w", "router_expert_b", "w_gate", "w_up", "w_down", "final_norm_w"]


def build(nc, a, out):
    m = Mem()
    with ExitStack() as ctx:
        sb = lambda n, s, d=F32: ctx.enter_context(nc.sbuf_tensor(n, s, d))
        sem = lambda n: ctx.enter_context(nc.semaphore(n))
        m.ident = sb("ident", [P, P])
        m.ident_b = sb("ident_b", [P, P], BF16)
        m.causal = sb("causal", [P, P], BF16)
        m.strict = sb("strict", [P, P], BF16)
        m.winmask = sb("winmask", [P, P], BF16)
        m.tri = sb("tri", [P, P], BF16)
        m.ones_b = sb("ones_b", [P, P], BF16)
        m.ones = sb("ones", [P, 2])
        m.cmpmask = sb("cmpmask", [P, NT, N_CMP], BF16)
        m.idx_c = sb("idx_c", [P, C_ALL - C_KEY])
        m.w_attn = sb("w_attn", [P, ND])
        m.w_mix = sb("w_mix", [P, ND])
        m.w_ffn = sb("w_ffn", [P, ND])
        m.pos = sb("pos", [P, NT], I32)
        m.trig = sb("trig", [P, 2, NT, 8])
        m.eps, m.clip, m.one = sb("eps", [P, 1]), sb("clip", [P, 1]), sb("one", [P, 1])
        m.stat = sb("stat", [P, 8])
        m.rstd = sb("rstd", [P, 8])
        m.w_gates = sb("w_gates", [P, ND, N_GATE])
        m.gates = sb("gates", [P, NT, N_GATE])
        m.w_router = sb("w_router", [P, ND, N_GRP + N_EXP])
        m.b_router = sb("b_router", [P, N_GRP + N_EXP])
        m.X = sb("X", [P, 32 * KB])
        m.Y = sb("Y", [P, 32 * KB])
        m.Z = sb("Z", [P, 40 * KB])
        m.V = sb("V", [P, 24 * KB])
        m.S = sb("S", [P, 24 * KB])
        m.M = sb("M", [P, 28 * KB])
        m.ps = ctx.enter_context(nc.psum_tensor("ps", [P, 8, BANK], F32))
        m.hT = view(m.X, 0, ND, T)
        m.keys = view(m.M, 0, 2, 2, T)
        m.w_ring = view(m.Y, 0, 2, ND, BANK)
        m.groups = [0, COL_SEL, COL_SBV]
        m.w_loaded = [sem("w_loaded0"), sem("w_loaded1")]
        m.w_gates_loaded = sem("w_gates_loaded")
        m.router_in = sem("router_in")
        m.qT = view(m.Z, 0, 4, T)
        m.kT = view(m.Z, 16 * KB, 2, T)
        m.vsw = view(m.Z, 24 * KB, NT, 2, P)
        m.ckv = view(m.Z, 32 * KB, KV_G, T)
        m.mark = sb("mark", [P, 1])
        m.sbqk_rows = nc.dram_tensor("sb_qk_scratch", (2 * SB_H * DH, T), F32, kind="Internal").ap()
        m.sbv_d = nc.dram_tensor("sb_v_scratch", (NT, P, BANK), F32, kind="Internal").ap()
        m.w_out = view(m.Y, 0, ND, D)
        m.w_out_in = sem("w_out_in")
        m.x1 = view(m.Z, 0, NT, D)
        m.logits = sb("logits", [P, NT, N_GRP + N_EXP])
        m.hot = sb("hot", [P, NT, N_EXP], BF16)
        m.weight = sb("weight", [P, 2, NT])
        m.dest = sb("dest", [P, 2, NT], I32)
        m.dest_now = sb("dest_now", [P, 2, 2], I32)
        m.tokens = sb("tokens", [P, NT], I32)
        m.blocks = sb("blocks", [P, 3 * N_EXP + 1], I32)
        m.row_tok = sb("row_tok", [P, MAX_BLK + 1], I32)
        m.row_now = sb("row_now", [P, 1], I32)
        m.zero_i = sb("zero_i", [P, MAX_BLK + 1], I32)
        m.list_zero, m.rows_in = sem("list_zero"), sem("rows_in")
        m.expert = [(view(m.X, 0, ND, FF), view(m.X, ND * FF, ND, FF), view(m.M, 0, NF, D)),
                    (view(m.Y, 0, ND, FF), view(m.Y, ND * FF, ND, FF), view(m.V, 0, NF, D))]
        m.wg_in, m.wu_in, m.wd_in = ([sem(f"w{k}_in{j}") for j in range(2)] for k in "gud")
        m.list_d = nc.dram_tensor("row_list_scratch", (ROWS, 1), I32, kind="Internal").ap()
        m.h_d = nc.dram_tensor("h_scratch", (T, D), F32, kind="Internal").ap()
        m.y_d = nc.dram_tensor("y_scratch", (ROWS, D), F32, kind="Internal").ap()
        m.o = view(m.X, 0, NT, D)
        m.w2 = sb("cmp_w2", [P, 2, 2, 2, DH])
        m.pe_rows = sb("cmp_pe", [CMP_LEN, 2, DH])
        m.kc = sb("kc", [P, KV_G, N_CMP])
        m.vc = sb("vc", [P, KV_G, DH])
        m.cmp_w = sem("cmp_w_loaded")
        hidden_states(nc, ctx, m, a)
        projections(nc, ctx, m, a)
        stick_breaking(nc, ctx, m, a)
        compression(nc, ctx, m, a)
        native_sparse(nc, ctx, m, a)
        mix_and_route(nc, ctx, m, a)
        route(nc, ctx, m, a)
        experts(nc, ctx, m, a)
        combine(nc, ctx, m, a, out)


class Args:
    pass


def kernel(**inputs):
    import concourse.bacc as _bacc
    from concourse.bass_utils import run_bass_kernel_spmd as _run

    nc = _bacc.Bacc("TRN2", target_bir_lowering=False, num_devices=1)
    arrays, a = {}, Args()
    for name in INPUTS:
        arr = np.ascontiguousarray(inputs[name])
        if arr.ndim > 1:
            arr = arr[0]
        arrays[name] = arr
        a.__dict__[name] = nc.dram_tensor(name, arr.shape, mybir.dt.from_np(arr.dtype), kind="ExternalInput").ap()
    arrays["shape_constants"] = constants()
    a.cst = nc.dram_tensor("shape_constants", (P, C_ALL), F32, kind="ExternalInput").ap()
    a.w_gate_rows = a.w_gate.rearrange("e d f -> (e d) f")
    a.w_up_rows = a.w_up.rearrange("e d f -> (e d) f")
    a.w_down_rows = a.w_down.rearrange("e f d -> (e f) d")
    a.w_in_rows = a.w_in.rearrange("(c p) n -> p c n", p=P)
    out = nc.dram_tensor("out", (T, D), F32, kind="ExternalOutput").ap()
    build(nc, a, out)
    r = _run(nc, [arrays], core_ids=[0])
    return r.results[0]["out"].reshape(1, T, D)
```

```python
from contextlib import ExitStack

import numpy as np

import concourse.bass as bass
from concourse import mybir
from concourse.alu_op_type import AluOpType as ALU

F32 = mybir.dt.float32
F32R = mybir.dt.float32r
BF16 = mybir.dt.bfloat16
I32 = mybir.dt.int32
U32 = mybir.dt.uint32
ACT = mybir.ActivationFunctionType
AX_X = mybir.AxisListType.X

P = 128
T = 1024
D = 1024
NT = T // P
ND = D // P
BANK = 512
DH = 64
HALF = DH // 8
NSA_H, KV_G, SB_H = 8, 2, 8
R_G = NSA_H // KV_G
N_Q = NSA_H * DH
COL_CMP = N_Q
COL_SEL = COL_CMP + 2 * KV_G * DH
COL_GATE = N_Q + 6 * KV_G * DH
N_GATE = 3 * NSA_H
COL_SBQ = COL_GATE + N_GATE
COL_SBK = COL_SBQ + SB_H * DH
COL_SBV = COL_SBK + SB_H * DH
CMP_LEN, CMP_STRIDE, CMP_HID = 32, 16, 256
N_CMP = 64
WIN_TILES = 512 // P
N_EXP, N_GRP, E_PG, FF = 16, 4, 4, 512
NF = FF // P
BLK = 128
MAX_BLK = 2 * T // BLK + N_EXP
ROWS = (MAX_BLK + 1) * BLK
EPS = 1e-6
NEG = -1e30
SCALE = DH ** -0.5
THETA = 500000.0
CLIP = 40.0

C_ID, C_CAUSAL, C_STRICT, C_WIN, C_TRI, C_CMP = 0, 128, 256, 384, 512, 640
C_FREQ = C_CMP + NT * N_CMP
C_KEY = C_FREQ + 8
C_THR = C_KEY + 4
N_THR = T // BLK - 1
C_VALID = C_THR + N_THR
C_TOK = C_VALID + NT
C_ALL = C_TOK + NT


def constants():
    c = np.zeros((P, C_ALL), np.float32)
    r, k = np.arange(P)[:, None], np.arange(P)[None, :]
    c[:, C_ID:C_ID + P] = r == k
    c[:, C_CAUSAL:C_CAUSAL + P] = np.where(k > r, NEG, 0.0)
    c[:, C_STRICT:C_STRICT + P] = np.where(k >= r, NEG, 0.0)
    c[:, C_WIN:C_WIN + P] = np.where(k <= r, NEG, 0.0)
    c[:, C_TRI:C_TRI + P] = r < k
    n = np.arange(N_CMP)[None, :]
    for i in range(NT):
        seen = (n * CMP_STRIDE + CMP_LEN - 1 <= i * P + r) & (n < N_CMP - 1)
        c[:, C_CMP + i * N_CMP:C_CMP + (i + 1) * N_CMP] = np.where(seen, 0.0, NEG)
        c[:, C_VALID + i] = (i * P + r[:, 0]) >= CMP_LEN - 1
        c[:, C_TOK + i] = i * P + r[:, 0]
    c[:, C_FREQ:C_FREQ + 8] = np.float32(THETA) ** (-np.arange(0, 16, 2, dtype=np.float32) / np.float32(16))
    c[:, C_KEY:C_KEY + 4] = [4, 3, 2, 1]
    c[:, C_THR:C_THR + N_THR] = BLK * np.arange(1, N_THR + 1)
    return c


class Link:

    def __init__(self, eng, sem):
        self.eng, self.sem, self.n = eng, sem, 0

    def __call__(self, ins):
        self.n += 1
        ins.then_inc(self.sem, 1)
        self.eng.wait_ge(self.sem, self.n)

    def restart(self):
        self.eng.sem_clear(self.sem)
        self.n = 0


def table_rsqrt(act, m, ln_done, n, out, total, width):
    act.activation(out, total, ACT.Ln, scale=1.0 / width, bias=m.eps[:, 0:1]).then_inc(ln_done, 1)
    act.wait_ge(ln_done, n)
    return act.activation(out, out, ACT.Exp, scale=-0.5)


def newton_rsqrt(dve, link, r, total, width):
    t = total
    link(dve.tensor_scalar(t, total, -0.5 / width, -0.5 * EPS, ALU.mult, ALU.add))
    link(dve.tensor_tensor(t, t, r, ALU.mult))
    link(dve.tensor_tensor(t, t, r, ALU.mult))
    link(dve.scalar_tensor_tensor(out=r, in0=t, scalar=1.5, in1=r, op0=ALU.add, op1=ALU.mult))


class Mem:
    pass


def view(region, off, *shape):
    n = int(np.prod(shape))
    ap = region[:, off:off + n]
    if len(shape) == 2:
        ap = ap.rearrange("p (a b) -> p a b", b=shape[1])
    if len(shape) == 3:
        ap = ap.rearrange("p (a b c) -> p a b c", b=shape[1], c=shape[2])
    if len(shape) == 4:
        ap = ap.rearrange("p (a b c d) -> p a b c d", b=shape[1], c=shape[2], d=shape[3])
    return ap


KB = 256


def hidden_states(nc, ctx, m, a):
    sem = lambda n: ctx.enter_context(nc.semaphore(n))
    x_in = [sem(f"x_in{j}") for j in range(4)]
    const_in, small_in, x_sq, x_norm, h_tr, h_free, x_rstd, x_ln = map(
        sem, ("const_in", "small_in", "x_sq", "x_norm", "h_tr", "h_free", "x_rstd", "x_ln"))
    ang_r, trig, dlink = sem("ang_r"), sem("trig"), sem("dlink_h")
    m.consts_ready = sem("consts_ready")
    x = view(m.V, 0, 4, D)
    junk = view(m.V, 4 * D, D)
    cst = m.S[:, 0:C_ALL]
    tmp = view(m.S, C_ALL, 8, NT, 8)
    ps = m.ps
    freq = cst[:, C_FREQ:C_FREQ + 8]

    with nc.Block() as block:
        @block.sync
        def _(sp):
            sp.dma_start(x[:, 0, :], a.x[0:P, :]).then_inc(x_in[0], 16)
            sp.dma_start(cst, a.cst).then_inc(const_in, 16)
            sp.dma_start(m.ident[:], a.cst[:, C_ID:C_ID + P]).then_inc(const_in, 16)
            with nc.allow_non_contiguous_dma("gain columns, 12 KiB in all"):
                for dst, src in ((m.w_attn, a.attn_norm_w), (m.w_ffn, a.ffn_norm_w)):
                    sp.dma_start(dst[:], src.rearrange("(c p) -> p c", p=P)).then_inc(small_in, 16)
                sp.dma_start(m.w_mix[:, 0:4], a.nsa_out_norm_w.rearrange("(c p) -> p c", p=P)).then_inc(small_in, 16)
                sp.dma_start(m.w_mix[:, 4:8], a.sb_out_norm_w.rearrange("(c p) -> p c", p=P)).then_inc(small_in, 16)
                sp.dma_start(m.pos[:], a.positions.rearrange("(c p) -> p c", p=P)).then_inc(small_in, 16)
            for j in range(1, 4):
                sp.dma_start(x[:, j, :], a.x[j * P:(j + 1) * P, :]).then_inc(x_in[j], 16)
            for j in range(4):
                sp.wait_ge(h_tr, 2 * j + 2)
                sp.dma_start(x[:, j, :], a.x[(4 + j) * P:(5 + j) * P, :]).then_inc(x_in[j], 16)
            for g in range(2):
                sp.dma_start(m.w_ring[:, g, :, :], a.w_in_rows[:, :, m.groups[g]:m.groups[g] + BANK]).then_inc(m.w_loaded[g], 16)
            with nc.allow_non_contiguous_dma("the gate columns, 96 bytes a row"):
                sp.dma_start(m.w_gates[:], a.w_in_rows[:, :, COL_GATE:COL_GATE + N_GATE]).then_inc(m.w_gates_loaded, 16)
                sp.dma_start(m.w_router[:, :, 0:N_GRP], a.router_group_w.rearrange("(c p) n -> p c n", p=P)).then_inc(m.router_in, 16)
                sp.dma_start(m.w_router[:, :, N_GRP:N_GRP + N_EXP], a.router_expert_w.rearrange("(c p) n -> p c n", p=P)).then_inc(m.router_in, 16)
                sp.dma_start(m.b_router[:, 0:N_GRP], a.router_group_b.partition_broadcast(P)).then_inc(m.router_in, 16)
                sp.dma_start(m.b_router[:, N_GRP:N_GRP + N_EXP], a.router_expert_b.partition_broadcast(P)).then_inc(m.router_in, 16)

        @block.scalar
        def _(act):
            act.wait_ge(ang_r, 1)
            act.activation(m.trig[:].rearrange("p a b c -> p (a b c)"), tmp[:, 4:6].rearrange("p a b c -> p (a b c)"), ACT.Sin).then_inc(trig, 1)
            act.preload_act_table_set("natural_log_exp_and_others")
            with act.Fori(0, 2) as it:
                for j in range(4):
                    act.wait_ge(x_in[j], it * 16 + 16)
                    if j == 0:
                        act.wait_ge(x_norm, it * 4 + 1)
                    act.activation(junk, x[:, j, :], ACT.Square, accum_out=m.stat[:, j:j + 1]).then_inc(x_sq, 1)
                    act.wait_ge(x_sq, it * 4 + j + 1)
                    table_rsqrt(act, m, x_ln, it * 4 + j + 1, m.rstd[:, j:j + 1], m.stat[:, j:j + 1], D).then_inc(x_rstd, 1)

        @block.vector
        def _(dve):
            link = Link(dve, dlink)
            dve.memset(m.clip[:], CLIP)
            dve.memset(m.zero_i[:], 0)
            dve.memset(m.one[:], 1.0)
            dve.memset(m.eps[:], EPS).then_inc(x_norm, 1)
            dve.wait_ge(const_in, 32)
            dve.wait_ge(small_in, 80)
            for dst, c0 in ((m.ident_b, C_ID), (m.causal, C_CAUSAL), (m.strict, C_STRICT), (m.winmask, C_WIN), (m.tri, C_TRI)):
                dve.tensor_copy(dst[:], cst[:, c0:c0 + P])
            dve.tensor_copy(m.cmpmask[:].rearrange("p a b -> p (a b)"), cst[:, C_CMP:C_CMP + NT * N_CMP])
            dve.tensor_copy(m.idx_c[:], cst[:, C_KEY:C_ALL])
            dve.memset(m.ones_b[:], 1.0)
            dve.memset(m.ones[:], 1.0)
            pos = tmp[:, 7, :, 0]
            link(dve.tensor_copy(pos, m.pos[:]))
            ang = tmp[:, 0]
            link(dve.tensor_tensor(ang, pos.unsqueeze(2).broadcast_to([P, NT, 8]), freq.unsqueeze(1).broadcast_to([P, NT, 8]), ALU.mult))
            magic = 1.5 * 2 ** 23
            two_pi = 2 * np.pi
            c1 = 6.28125
            c2 = float(np.float32(int((two_pi - c1) * 2 ** 20) / 2 ** 20))
            c3 = two_pi - c1 - c2
            for which, turn, shift in ((0, 0.0, 0.0), (1, 0.25, np.pi / 2)):
                k, r = tmp[:, 2 + which], tmp[:, 4 + which]
                link(dve.tensor_scalar(k, ang, 1.0 / two_pi, turn, ALU.mult, ALU.add))
                link(dve.tensor_scalar(k, k, magic, None, ALU.add))
                link(dve.tensor_scalar(k, k, magic, None, ALU.subtract))
                link(dve.scalar_tensor_tensor(out=r, in0=k, scalar=-c1, in1=ang, op0=ALU.mult, op1=ALU.add))
                link(dve.scalar_tensor_tensor(out=r, in0=k, scalar=-c2, in1=r, op0=ALU.mult, op1=ALU.add))
                link(dve.scalar_tensor_tensor(out=r, in0=k, scalar=-c3, in1=r, op0=ALU.mult, op1=ALU.add))
                if which:
                    link(dve.tensor_scalar(r, r, shift, None, ALU.add))
                ins = dve.tensor_scalar(r, r, 3.1415925, -3.1415925, ALU.min, ALU.max)
                if which:
                    ins.then_inc(ang_r, 1)
                else:
                    link(ins)
            with dve.Fori(0, 2) as it:
                link.restart()
                for j in range(4):
                    dve.wait_ge(x_rstd, it * 4 + j + 1)
                    newton_rsqrt(dve, link, m.rstd[:, j:j + 1], m.stat[:, j:j + 1], D)
                    dve.tensor_scalar(x[:, j, :], x[:, j, :], m.rstd[:, j:j + 1], None, ALU.mult).then_inc(x_norm, 1)
                    for half in range(2):
                        dve.wait_ge(h_tr, it * 8 + 2 * j + half + 1)
                        dve.tensor_tensor(m.hT[:, 4 * half:4 * half + 4, bass.ds(it * 512 + j * P, P)],
                                          ps[:, 4 + half, :].rearrange("p (c n) -> p c n", n=P),
                                          m.w_attn[:, 4 * half:4 * half + 4].unsqueeze(2).broadcast_to([P, 4, P]),
                                          ALU.mult).then_inc(h_free, 1)

        @block.tensor
        def _(pe):
            pe.sem_inc(h_free, 2)
            pe.wait_ge(const_in, 32)
            with pe.Fori(0, 2) as it:
                for j in range(4):
                    pe.wait_ge(x_norm, it * 4 + j + 2)
                    for half in range(2):
                        pe.wait_ge(h_free, it * 8 + 2 * j + half + 1)
                        for c in range(4):
                            ins = pe.transpose(ps[:, 4 + half, c * P:(c + 1) * P], x[:, j, (4 * half + c) * P:(4 * half + c + 1) * P], m.ident[:])
                        ins.then_inc(h_tr, 1)


def projections(nc, ctx, m, a):
    sem = lambda n: ctx.enter_context(nc.semaphore(n))
    mm, mm_free, rot_in, rot, rtmp, tr, tr_free = map(
        sem, ("proj_mm", "proj_free", "rot_in", "rot_done", "rot_link", "rot_tr", "rot_free"))
    gate_mm, gate_exp = sem("gate_mm"), sem("gate_exp")
    chunk_in = [sem(f"chunk_in{j}") for j in range(2)]
    stored = [sem(f"stage_stored{j}") for j in range(4)]
    m.proj_stored = stored
    ps = m.ps
    NB = 4
    stage = view(m.S, 0, 4, BANK)
    rows = view(m.S, 4 * BANK, 2, BANK)
    tmp = view(m.S, 6 * BANK, 4, 64)
    chunk = view(m.V, 0, 2, ND, P)
    cmpw = view(m.V, 2 * ND * P, 2, ND, 2, DH)
    cmp_in = sem("cmp_w_in")
    LOOPC = 2 * SB_H * DH // P
    N_ROW = 3 * NT
    N_LOOP = 2 * LOOPC

    with nc.Block() as block:
        @block.sync
        def _(sp):
            sp.wait_ge(mm, NT)
            sp.dma_start(m.w_ring[:, 0, :, :], a.w_in_rows[:, :, COL_SBV:COL_SBV + BANK]).then_inc(m.w_loaded[0], 16)
            for g in range(KV_G):
                for kv in range(2):
                    c0 = COL_CMP + kv * KV_G * DH + g * DH
                    sp.dma_start(cmpw[:, g, :, kv, :], a.w_in_rows[:, :, c0:c0 + DH]).then_inc(cmp_in, 16)
            sp.dma_start(chunk[:, 0], a.w_in_rows[:, :, COL_SBQ:COL_SBQ + P]).then_inc(chunk_in[0], 16)
            sp.dma_start(chunk[:, 1], a.w_in_rows[:, :, COL_SBQ + P:COL_SBQ + 2 * P]).then_inc(chunk_in[1], 16)
            for t in range(NT):
                sp.wait_ge(mm_free, 2 * NT + t + 1)
                sp.dma_start(m.sbv_d[t], stage[:, t % 4]).then_inc(stored[t % 4], 16)
            with sp.Fori(0, LOOPC // 2) as it:
                for j in range(2):
                    for half in range(2):
                        sp.wait_ge(mm_free, N_ROW + it * 4 + 2 * j + half + 1)
                        sp.dma_start(m.sbqk_rows[bass.ds((it * 2 + j) * P, P), half * BANK:(half + 1) * BANK],
                                     stage[:, 2 * j + half]).then_inc(stored[2 * j + half], 16)
                    with sp.If(it < LOOPC // 2 - 1):
                        sp.wait_ge(mm, N_ROW + it * 4 + 2 * j + 2)
                        sp.dma_start(chunk[:, j], a.w_in_rows[:, :, bass.ds(COL_SBQ + (it * 2 + j + 2) * P, P)]).then_inc(chunk_in[j], 16)

        @block.tensor
        def _(pe):
            def product(n, t, w):
                if n >= NB:
                    pe.wait_ge(mm_free, n - NB + 1)
                for c in range(ND):
                    ins = pe.matmul(ps[:, n % NB, :], m.hT[:, c, t * P:(t + 1) * P], w[:, c, :], start=c == 0, stop=c == ND - 1)
                ins.then_inc(mm, 1)

            def back(k, heads):
                pe.wait_ge(rot, k + 1)
                if k >= 2:
                    pe.wait_ge(tr_free, k - 1)
                for q, c0 in enumerate(heads):
                    ins = pe.transpose(ps[:, 4 + k % 2, q * P:(q + 1) * P], rows[:, k % 2, c0:c0 + P], m.ident[:])
                ins.then_inc(tr, 1)

            q_cols, k_cols = [0, P, 2 * P, 3 * P], [0, 2 * P]
            pe.wait_ge(m.w_loaded[0], 16)
            for t in range(NT):
                product(t, t, m.w_ring[:, 0])
                if t:
                    back(t - 1, q_cols)
            pe.wait_ge(m.w_loaded[1], 16)
            for t in range(NT):
                product(NT + t, t, m.w_ring[:, 1])
                back(NT + t - 1, q_cols if t == 0 else k_cols)
            pe.wait_ge(m.w_gates_loaded, 16)
            for t in range(NT):
                for c in range(ND):
                    ins = pe.matmul(ps[:, 6, t * N_GATE:(t + 1) * N_GATE], m.hT[:, c, t * P:(t + 1) * P], m.w_gates[:, c, :],
                                    start=c == 0, stop=c == ND - 1)
            ins.then_inc(gate_mm, 1)
            back(2 * NT - 1, k_cols)
            pe.wait_ge(m.w_loaded[0], 32)
            for t in range(NT):
                product(2 * NT + t, t, m.w_ring[:, 0])
            with pe.Fori(0, LOOPC // 2) as it:
                for j in range(2):
                    pe.wait_ge(chunk_in[j], it * 16 + 16)
                    for half in range(2):
                        n = 2 * j + half
                        pe.wait_ge(mm_free, it * 4 + N_ROW + n - NB + 1)
                        for c in range(ND):
                            ins = pe.matmul(ps[:, n, :], chunk[:, j, c, :], m.hT[:, c, half * BANK:(half + 1) * BANK],
                                            start=c == 0, stop=c == ND - 1)
                        ins.then_inc(mm, 1)
            pe.wait_ge(cmp_in, 64)
            for g in range(KV_G):
                for half in range(2):
                    n = N_ROW + N_LOOP + 2 * g + half
                    pe.wait_ge(mm_free, n - NB + 1)
                    for c in range(ND):
                        ins = pe.matmul(ps[:, n % NB, :], cmpw[:, g, c].rearrange("p a b -> p (a b)"),
                                        m.hT[:, c, half * BANK:(half + 1) * BANK], start=c == 0, stop=c == ND - 1)
                    ins.then_inc(mm, 1)

        @block.scalar
        def _(act):
            for t in range(NT):
                act.wait_ge(mm, t + 1)
                if t >= 2:
                    act.wait_ge(tr, t - 1)
                act.activation(rows[:, t % 2], ps[:, t % NB, :], ACT.Copy).then_inc(mm_free, 1)
            for t in range(NT):
                n = NT + t
                act.wait_ge(mm, n + 1)
                act.wait_ge(tr, n - 1)
                act.activation(rows[:, n % 2], ps[:, n % NB, :], ACT.Copy).then_inc(rot_in, 1)
                act.activation(m.vsw[:, t, :, :], ps[:, n % NB, :].rearrange("p (w v c) -> p w v c", w=2, v=2)[:, :, 1, :],
                               ACT.Copy).then_inc(mm_free, 1)
            act.wait_ge(gate_mm, 1)
            act.activation(m.gates[:].rearrange("p a b -> p (a b)"), ps[:, 6, 0:NT * N_GATE], ACT.Exp, scale=-1.0).then_inc(gate_exp, 1)
            for t in range(NT):
                n = 2 * NT + t
                act.wait_ge(mm, n + 1)
                if t >= 4:
                    act.wait_ge(stored[t % 4], 16)
                act.activation(stage[:, t % 4], ps[:, n % NB, :], ACT.Copy).then_inc(mm_free, 1)
            with act.Fori(0, LOOPC // 2) as it:
                for n in range(4):
                    act.wait_ge(mm, it * 4 + N_ROW + n + 1)
                    act.wait_ge(stored[n], it * 16 + 32)
                    act.activation(stage[:, n], ps[:, n, :], ACT.Copy).then_inc(mm_free, 1)
            for g in range(KV_G):
                for half in range(2):
                    n = N_ROW + N_LOOP + 2 * g + half
                    act.wait_ge(mm, n + 1)
                    act.activation(m.ckv[:, g, half * BANK:(half + 1) * BANK], ps[:, n % NB, :], ACT.Copy).then_inc(mm_free, 1)

        @block.vector
        def _(dve):
            link = Link(dve, rtmp)

            def rotate(k, t, heads):
                v = heads(rows[:, k % 2])
                nh = NSA_H if len(v.shape) == 3 else 4
                x1, x2 = v[..., 0:8], v[..., 8:16]
                shape = [P] + list(v.shape[1:-1]) + [8]
                sin, cos = m.trig[:, 0, t, :], m.trig[:, 1, t, :]
                for _ in shape[1:-1]:
                    sin, cos = sin.unsqueeze(1), cos.unsqueeze(1)
                sin, cos = sin.broadcast_to(shape), cos.broadcast_to(shape)
                pr = [tmp[:, q, 0:nh * 8].rearrange("p (h c) -> p h c", c=8) if len(shape) == 3 else
                      tmp[:, q, 0:nh * 8].rearrange("p (w h c) -> p w h c", w=2, c=8) for q in range(4)]
                dve.tensor_tensor(pr[0], x1, cos, ALU.mult)
                dve.tensor_tensor(pr[1], x2, sin, ALU.mult)
                dve.tensor_tensor(pr[2], x2, cos, ALU.mult)
                link(dve.tensor_tensor(pr[3], x1, sin, ALU.mult))
                dve.tensor_tensor(x1, pr[0], pr[1], ALU.subtract)
                link(dve.tensor_tensor(x2, pr[2], pr[3], ALU.add))

            q_heads = lambda r: r.rearrange("p (h c) -> p h c", c=DH)[:, :, 0:16]
            k_heads = lambda r: r.rearrange("p (w v h c) -> p w v h c", w=2, v=2, c=DH)[:, :, 0, :, 0:16]

            def collect(k):
                t = k % NT
                dve.wait_ge(tr, k + 1)
                if k < NT:
                    dve.tensor_copy(m.qT[:, :, t * P:(t + 1) * P], ps[:, 4 + k % 2, :].rearrange("p (a b) -> p a b", b=P)).then_inc(tr_free, 1)
                else:
                    dve.tensor_copy(m.kT[:, :, t * P:(t + 1) * P], ps[:, 4 + k % 2, 0:2 * P].rearrange("p (a b) -> p a b", b=P)).then_inc(tr_free, 1)

            for k in range(2 * NT):
                if k < NT:
                    dve.wait_ge(mm_free, k + 1)
                else:
                    dve.wait_ge(rot_in, k - NT + 1)
                rotate(k, k % NT, q_heads if k < NT else k_heads)
                dve.memset(m.mark[:], 0.0).then_inc(rot, 1)
                if k:
                    collect(k - 1)
            collect(2 * NT - 1)
            dve.wait_ge(gate_exp, 1)
            g = m.gates[:].rearrange("p a b -> p (a b)")
            link(dve.tensor_scalar(g, g, 1.0, None, ALU.add))
            link(dve.reciprocal(g, g))


class Count:

    def __init__(self, sem, steps, credit=0):
        self.sem, self.credit = sem, credit
        self.upto = [0]
        for s in steps:
            self.upto.append(self.upto[-1] + s)
        self.total = self.upto[-1]

    def after(self, it, n):
        k = len(self.upto) - 1
        back = 0
        while n < 0:
            n, back = n + k, back + self.total
        c = self.upto[n + 1] - back + self.credit
        return it * self.total + c


def stick_breaking(nc, ctx, m, a):
    sem = lambda n: ctx.enter_context(nc.semaphore(n))
    units = []
    for j in range(2):
        for i in range(NT):
            top = 4 if i >= 4 else 0
            w = i + 1 - top
            if 2 * w <= 4:
                units.append((j, i, [(0, top, i + 1, 0), (1, top, i + 1, w)]))
            else:
                units += [(j, i, [(h, top, i + 1, 0)]) for h in range(2)]
            if top:
                units += [(j, i, [(h, 0, top, 0)]) for h in range(2)]
    N = len(units)
    width = [sum(b1 - b0 for _, b0, b1, _ in u[2]) * P for u in units]
    last = [n + 1 == N or units[n + 1][:2] != units[n][:2] for n in range(N)]
    tile_of = [sum(last[:n]) for n in range(N)]
    one = [1] * N
    loaded = [sem("sb_in0"), sem("sb_in1")]
    scores = Count(sem("sb_scores"), one)
    soft = Count(sem("sb_soft"), one)
    arg = Count(sem("sb_arg"), one, 4)
    prob = Count(sem("sb_prob"), one)
    trans = Count(sem("sb_trans"), one, 4)
    moved = Count(sem("sb_moved"), one, 2)
    summed = Count(sem("sb_summed"), [int(any(b0 == 0 for _, b0, _, _ in u[2])) for u in units], 4)
    out = Count(sem("sb_out"), [1] * sum(last), 2)
    alink, dlink = sem("sb_alink"), sem("sb_dlink")
    ps = m.ps
    q, v = view(m.S, 0, 2, T), view(m.S, 2 * T, 2, NT, P)
    k = m.keys
    zeroed = sem("sb_zeroed")
    E, C, AT = view(m.V, 0, 6, BANK), view(m.V, 6 * BANK, 4, BANK), view(m.S, 4 * T, 4, BANK)
    m.w1 = view(m.Y, 0, CMP_LEN, CMP_HID)
    LAG_P, LAG_T, LAG_W = 2, 3, 4

    def cols(span):
        h, b0, b1, at = span
        return slice(at * P, (at + b1 - b0) * P)

    def later(n, h):
        return next((b, span) for b in range(n) for span in units[b][2] if units[b][:2] == units[n][:2] and span[0] == h)

    with nc.Block() as block:
        @block.sync
        def _(sp):
            def load(j, hp):
                sp.dma_start(q[:, j], m.sbqk_rows[bass.ds(hp * P, P), :]).then_inc(loaded[j], 16)
                for h in range(2):
                    sp.dma_start(k[h * DH:(h + 1) * DH, j, h], m.sbqk_rows[bass.ds(hp * P + SB_H * DH + h * DH, DH), :]).then_inc(loaded[j], 16)
                sp.dma_start(v[:, j], m.sbv_d[:, :, bass.ds(hp * P, P)].rearrange("t p c -> p t c")).then_inc(loaded[j], 16)

            for n in range(4):
                sp.wait_ge(m.proj_stored[n], 96)
            sp.wait_ge(zeroed, 2)
            load(0, 0)
            load(1, 1)
            for kv, (w1, w2, pe_) in enumerate(((a.cmp_k_w1, a.cmp_k_w2, a.cmp_pe_k), (a.cmp_v_w1, a.cmp_v_w2, a.cmp_pe_v))):
                sp.dma_start(m.w1[kv * DH:(kv + 1) * DH], w1.rearrange("(l d) h -> d l h", d=DH)).then_inc(m.cmp_w, 16)
                sp.dma_start(m.pe_rows[:, kv, :], pe_).then_inc(m.cmp_w, 16)
                for dup in range(2):
                    sp.dma_start(m.w2[:, kv, :, dup, :], w2.rearrange("(c p) n -> p c n", p=P)).then_inc(m.cmp_w, 16)
            for j in range(2):
                sp.wait_ge(summed.sem, summed.after(0, (j + 1) * N // 2 - 1))
                load(j, 2 + j)

        @block.tensor
        def _(pe):
            pe.sem_inc(trans.sem, trans.credit)
            pe.sem_inc(summed.sem, summed.credit)

            def score(it, n):
                j, i, spans = units[n]
                if n % (N // 2) == 0:
                    pe.wait_ge(loaded[j], it * 64 + 64)
                pe.wait_ge(arg.sem, arg.after(it, n - 4))
                for span in spans:
                    h, b0, b1, at = span
                    ins = pe.matmul(ps[:, n % 4, cols(span)], q[:, j, i * P:(i + 1) * P], k[:, j, h, b0 * P:b1 * P],
                                    start=True, stop=b1 <= i)
                    if b1 > i:
                        d = (at + i - b0) * P
                        ins = pe.matmul(ps[:, n % 4, d:d + P], m.ident_b[:], m.strict[:], start=False, stop=True)
                ins.then_inc(scores.sem, 1)

            def transpose(it, n):
                pe.wait_ge(prob.sem, prob.after(it, n))
                pe.wait_ge(moved.sem, moved.after(it, n - 2))
                for c in range(width[n] // P):
                    ins = pe.transpose(ps[:, 4 + n % 2, c * P:(c + 1) * P], C[:, n % 4, c * P:(c + 1) * P], m.ident[:])
                ins.then_inc(trans.sem, 1)

            def weigh(it, n):
                j, i, spans = units[n]
                t = tile_of[n]
                pe.wait_ge(moved.sem, moved.after(it, n))
                pe.wait_ge(out.sem, out.after(it, t - 2))
                ins = None
                for span in spans:
                    h, b0, b1, at = span
                    if b0 > 0:
                        continue
                    parts = ([] if b1 > i else [later(n, h)]) + [(n, span)]
                    for b, (_, c0, c1, to) in parts:
                        for c in range(c0, c1):
                            ins = pe.matmul(ps[:, 6 + t % 2, h * DH:(h + 1) * DH], AT[:, b % 4, (to + c - c0) * P:(to + c - c0 + 1) * P],
                                            v[:, j, c, h * DH:(h + 1) * DH], start=c == parts[0][1][1], stop=c == b1 - 1 and b == n)
                if ins:
                    ins.then_inc(summed.sem, 1)

            with pe.Fori(0, 2) as it:
                for s in range(N + LAG_W):
                    if s < N:
                        score(it, s)
                    if 0 <= s - LAG_T < N:
                        transpose(it, s - LAG_T)
                    if s >= LAG_W:
                        weigh(it, s - LAG_W)

        @block.scalar
        def _(act):
            act.sem_inc(out.sem, out.credit)
            link = Link(act, alink)
            with act.Fori(0, 2) as it:
                link.restart()
                for s in range(N + LAG_W + 1):
                    if s < N:
                        e = E[:, s % 6, 0:width[s]]
                        act.wait_ge(scores.sem, scores.after(it, s))
                        act.wait_ge(arg.sem, arg.after(it, s - 4))
                        link(act.activation(e, ps[:, s % 4, 0:width[s]], ACT.Relu, scale=-SCALE, bias=m.clip[:, 0:1]))
                        link(act.activation(e, e, ACT.Exp, scale=-1.0, bias=m.clip[:, 0:1]))
                        act.activation(e, e, ACT.Ln, bias=m.one[:, 0:1]).then_inc(soft.sem, 1)
                    if 0 <= s - LAG_P < N:
                        n = s - LAG_P
                        c = C[:, n % 4, 0:width[n]]
                        act.wait_ge(arg.sem, arg.after(it, n))
                        act.activation(c, c, ACT.Exp).then_inc(prob.sem, 1)
                    n = s - LAG_W - 1
                    if n >= 0 and last[n]:
                        j, i, _ = units[n]
                        act.wait_ge(summed.sem, summed.after(it, n))
                        act.activation(m.o[:, i, bass.ds(it * 2 * P + N_Q + j * P, P)], ps[:, 6 + tile_of[n] % 2, 0:P],
                                       ACT.Copy).then_inc(out.sem, 1)

        @block.vector
        def _(dve):
            for h in range(2):
                dve.memset(k[(1 - h) * DH:(2 - h) * DH, :, h, :], 0.0).then_inc(zeroed, 1)
            dve.sem_inc(arg.sem, arg.credit)
            dve.sem_inc(moved.sem, moved.credit)
            link = Link(dve, dlink)

            def exponent(it, n):
                j, i, spans = units[n]
                w = width[n]
                z, e, c = ps[:, n % 4, 0:w], E[:, n % 6, 0:w], C[:, n % 4, 0:w]
                dve.wait_ge(soft.sem, soft.after(it, n))
                link(dve.scalar_tensor_tensor(out=e, in0=z, scalar=SCALE, in1=e, op0=ALU.mult, op1=ALU.max))
                for x, span in enumerate(spans):
                    h, b0, b1, at = span
                    es = e[:, cols(span)][:, ::-1]
                    start = 0.0
                    if b1 <= i:
                        b, (_, _, _, to) = later(n, h)
                        start = E[:, b % 6, to * P:to * P + 1]
                    ins = dve.tensor_tensor_scan(es, m.one[:, 0:1].broadcast_to([P, (b1 - b0) * P]), es, start, ALU.mult, ALU.add)
                    link(ins)
                dve.wait_ge(trans.sem, trans.after(it, n - 4))
                dve.scalar_tensor_tensor(out=c, in0=z, scalar=SCALE, in1=e, op0=ALU.mult, op1=ALU.subtract).then_inc(arg.sem, 1)

            with dve.Fori(0, 2) as it:
                link.restart()
                for s in range(N + 2):
                    if s < N:
                        exponent(it, s)
                    if s >= 2:
                        n = s - 2
                        dve.wait_ge(trans.sem, trans.after(it, n))
                        dve.wait_ge(summed.sem, summed.after(it, n - 2))
                        dve.tensor_copy(AT[:, n % 4, 0:width[n]], ps[:, 4 + n % 2, 0:width[n]]).then_inc(moved.sem, 1)


def compression(nc, ctx, m, a):
    sem = lambda n: ctx.enter_context(nc.semaphore(n))
    pe_t, pe_c, blocks, hid, hexp, hsilu, fin, clink = map(
        sem, ("cmp_pe_t", "cmp_pe_c", "cmp_blocks", "cmp_hid", "cmp_exp", "cmp_silu", "cmp_fin", "cmp_link"))
    ps = m.ps
    kb = view(m.S, 0, KV_G, CMP_LEN, N_CMP)
    peT = m.S[:, 4096:4096 + CMP_LEN]
    ex = view(m.S, 4352, 2, 2, KV_G * N_CMP)
    hk = view(m.S, 4864, 2, KV_G * N_CMP)
    hv = view(m.S, 5120, 2, KV_G, 2, N_CMP)

    with nc.Block() as block:
        @block.tensor
        def _(pe):
            pe.wait_ge(m.cmp_w, 128)
            pe.transpose(ps[:, 7, 0:CMP_LEN], m.pe_rows[:].rearrange("p a b -> p (a b)"), m.ident[0:CMP_LEN, 0:CMP_LEN]).then_inc(pe_t, 1)
            pe.wait_ge(blocks, 5)
            for kv in range(2):
                lo = kv * DH
                for c in range(2):
                    for l in range(CMP_LEN):
                        ins = pe.matmul(ps[:, 2 * kv + c, 0:P], m.w1[lo:lo + DH, l, c * P:(c + 1) * P], kb[lo:lo + DH, :, l, :],
                                        start=l == 0, stop=l == CMP_LEN - 1)
                    ins.then_inc(hid, 1)
            pe.wait_ge(hsilu, 4)
            for c in range(2):
                pe.matmul(ps[:, 4, 0:P], m.w2[:, 0, c].rearrange("p a b -> p (a b)"), hk[:, c], start=c == 0, stop=c == 1)
            for g in range(KV_G):
                for c in range(2):
                    ins = pe.matmul(ps[:, 5, g * DH:(g + 1) * DH], hv[:, c, g].rearrange("p a b -> p (a b)"), m.w2[:, 1, c, 0],
                                    start=c == 0, stop=c == 1)
            ins.then_inc(fin, 1)

        @block.vector
        def _(dve):
            link = Link(dve, clink)
            dve.wait_ge(pe_t, 1)
            dve.tensor_copy(peT, ps[:, 7, 0:CMP_LEN]).then_inc(pe_c, 1)
            dve.wait_ge(pe_c, 1)
            dve.memset(kb[:, :, CMP_STRIDE:, N_CMP - 1:N_CMP], 0.0).then_inc(blocks, 1)
            for g in range(KV_G):
                src = m.ckv[:, g].rearrange("p (n l) -> p l n", l=CMP_STRIDE)
                for half, n1 in ((0, N_CMP), (1, N_CMP - 1)):
                    l0 = half * CMP_STRIDE
                    dve.tensor_tensor(kb[:, g, l0:l0 + CMP_STRIDE, 0:n1], src[:, :, half:half + n1],
                                      peT[:, l0:l0 + CMP_STRIDE].unsqueeze(2).broadcast_to([P, CMP_STRIDE, n1]), ALU.add).then_inc(blocks, 1)
            for kv in range(2):
                for c in range(2):
                    n = 2 * kv + c
                    e = ex[:, kv, c]
                    dve.wait_ge(hexp, n + 1)
                    link(dve.tensor_scalar(e, e, 1.0, None, ALU.add))
                    link(dve.reciprocal(e, e))
                    if kv == 0:
                        dve.tensor_tensor(hk[:, c], ps[:, n, 0:P], e, ALU.mult).then_inc(hsilu, 1)
                    else:
                        dst = hv[:, c]
                        for dup in range(2):
                            ins = dve.tensor_tensor(dst[:, :, dup, :], ps[:, n, 0:P].rearrange("p (g n) -> p g n", g=KV_G),
                                                    e.rearrange("p (g n) -> p g n", g=KV_G), ALU.mult)
                            if dup == 0:
                                link(ins)
                        ins.then_inc(hsilu, 1)
            dve.wait_ge(fin, 1)
            dve.tensor_copy(m.kc[:].rearrange("p a b -> p (a b)"), ps[:, 4, 0:P])
            dve.tensor_copy(m.vc[:].rearrange("p a b -> p (a b)"), ps[:, 5, 0:P])

        @block.scalar
        def _(act):
            for kv in range(2):
                for c in range(2):
                    act.wait_ge(hid, 2 * kv + c + 1)
                    act.activation(ex[:, kv, c], ps[:, 2 * kv + c, 0:P], ACT.Exp, scale=-1.0).then_inc(hexp, 1)


def native_sparse(nc, ctx, m, a):
    sem = lambda n: ctx.enter_context(nc.semaphore(n))
    items = []
    for i in range(NT):
        items.append(("cmp", i, None, 0, 2))
        for h in range(R_G):
            items.append(("sel", i, h, 0, i + 1))
            items.append(("win", i, h, max(0, i - WIN_TILES), i + 1))
    N = len(items)
    LAG_T, LAG_W, LAG_A = 2, 3, 4
    blocks = [b1 - b0 for _, _, _, b0, b1 in items]
    one = [1] * N
    two = [int(b > 4) for b in blocks]
    first, users, owner, at = [], [], [-1] * 4, 0
    for n in range(N):
        nb = 1 + two[n]
        if at + nb > 4:
            at = 0
        first.append(at)
        users.append(max(owner[at:at + nb]))
        owner[at:at + nb] = [n] * nb
        at = (at + nb) % 4
    turns = [(n, half) for n in range(N) for half in range(1 + two[n])]
    loaded = sem("nsa_in")
    scores = Count(sem("nsa_scores"), one)
    shift = Count(sem("nsa_shift"), one)
    prob = Count(sem("nsa_prob"), one, 4)
    transA = Count(sem("nsa_transA"), one, 4)
    transB = Count(sem("nsa_transB"), two, 4)
    movedA = Count(sem("nsa_movedA"), one, 2)
    movedB = Count(sem("nsa_movedB"), two, 2)
    summed = Count(sem("nsa_summed"), one, 3)
    added = Count(sem("nsa_added"), one, 8)
    dlink = sem("nsa_dlink")
    ps = m.ps
    q, v = view(m.S, 0, 2, T), view(m.S, 2 * T, 2, NT, DH)
    keys = m.keys
    kc, vc = view(m.S, 3 * T, 2, N_CMP), view(m.S, 3 * T + 2 * N_CMP, 2, DH)
    gate = view(m.S, 3 * T + 4 * N_CMP, NT, 3 * R_G)
    zeroed = sem("nsa_zeroed")
    Pr, PT = view(m.V, 0, 4, T), view(m.S, 4 * T, 2, T)
    L = view(m.V, 4 * T, 8, 8)
    mx = view(m.V, 4 * T + 64, 4, 8)
    valid = m.idx_c[:, C_VALID - C_KEY:C_VALID - C_KEY + NT]

    def s_of(n, w=None):
        return ps[:, first[n]:first[n] + 1 + two[n], :].rearrange("p a b -> p (a b)")[:, 0:w or blocks[n] * P]

    def bank_of(n, half):
        return 4 + turns.index((n, half)) % 2

    with nc.Block() as block:
        @block.sync
        def _(sp):
            sp.dma_start(m.w_out, a.w_out.rearrange("(c p) n -> p c n", p=P)).then_inc(m.w_out_in, 16)
            sp.wait_ge(zeroed, 2)
            with sp.Fori(0, KV_G) as g:
                sp.wait_ge(summed.sem, g * N + summed.credit)
                sp.dma_start(q, m.qT[:, bass.ds(g * 2, 2), :]).then_inc(loaded, 16)
                for group, mine in ((0, g < 1), (1, g > 0)):
                    with sp.If(mine):
                        for up in range(2):
                            for kind in range(2):
                                sp.dma_start(keys[up * DH:(up + 1) * DH, kind, up], m.kT[group * DH:(group + 1) * DH, kind, :]).then_inc(loaded, 16)
                for b in range(2):
                    sp.dma_start(v[:, b], m.vsw[:, :, b, bass.ds(g * DH, DH)]).then_inc(loaded, 16)
                for up in range(2):
                    half = slice(up * DH, (up + 1) * DH)
                    sp.dma_start(kc[half, up], m.kc[half, g, :]).then_inc(loaded, 16)
                    sp.dma_start(vc[half, up], m.vc[half, g, :]).then_inc(loaded, 16)
                sp.wait_ge(added.sem, g * N + added.credit)
                sp.dma_start(gate, m.gates[:, :, bass.ds(g * 3 * R_G, 3 * R_G)]).then_inc(loaded, 16)
        LOADS = 16 * 12

        @block.tensor
        def _(pe):
            for c in (transA, transB, summed):
                pe.sem_inc(c.sem, c.credit)

            def score(it, n):
                kind, i, h, b0, b1 = items[n]
                if n == 0:
                    pe.wait_ge(loaded, it * LOADS + LOADS)
                pe.wait_ge(prob.sem, prob.after(it, users[n]))
                s = s_of(n, (1 + two[n]) * BANK)
                if kind == "cmp":
                    pe.matmul(s[:, 0:R_G * N_CMP], m.ident_b[:], m.cmpmask[:, i, :].unsqueeze(1).broadcast_to([P, R_G, N_CMP]),
                              start=True, stop=False)
                    for pair in range(2):
                        ins = pe.matmul(s[:, pair * P:(pair + 1) * P], q[:, pair, i * P:(i + 1) * P],
                                        kc.rearrange("p a b -> p (a b)"), start=False, stop=pair == 1)
                    ins.then_inc(scores.sem, 1)
                    return
                w = (b1 - b0) * P
                masks = [(i - b0, m.causal)] + ([(0, m.winmask)] if kind == "win" and i >= WIN_TILES else [])
                for c in range(0, w, BANK):
                    e = min(w, c + BANK)
                    here = [(blk, t) for blk, t in masks if c <= blk * P < e]
                    pe.matmul(s[:, c:e], q[:, h // 2, i * P:(i + 1) * P], keys[:, int(kind == "win"), h % 2, b0 * P + c:b0 * P + e],
                              start=True, stop=not here)
                    for x, (blk, t) in enumerate(here):
                        ins = pe.matmul(s[:, blk * P:(blk + 1) * P], m.ident_b[:], t[:], start=False, stop=x == len(here) - 1)
                ins.then_inc(scores.sem, 1)

            def transpose(it, n):
                pe.wait_ge(prob.sem, prob.after(it, n))
                for half, t in ((0, transA), (1, transB))[0:1 + two[n]]:
                    g = turns.index((n, half))
                    for use, mv in ((0, movedA), (1, movedB)):
                        if g < 2:
                            pe.wait_ge(mv.sem, mv.after(it, -1))
                        elif turns[g - 2][1] == use:
                            pe.wait_ge(mv.sem, mv.after(it, turns[g - 2][0]))
                    for c in range(4 * half, min(4 * half + 4, blocks[n])):
                        ins = pe.transpose(ps[:, bank_of(n, half), (c - 4 * half) * P:(c - 4 * half + 1) * P],
                                           Pr[:, n % 4, c * P:(c + 1) * P], m.ident[:])
                    ins.then_inc(t.sem, 1)

            def weigh(it, n):
                kind, i, h, b0, b1 = items[n]
                pe.wait_ge(movedA.sem, movedA.after(it, n))
                pe.wait_ge(movedB.sem, movedB.after(it, n))
                pe.wait_ge(added.sem, added.after(it, n - 2))
                if kind == "cmp":
                    for pair in range(2):
                        ins = pe.matmul(ps[:, 6 + n % 2, pair * P:(pair + 1) * P], PT[:, n % 2, pair * P:(pair + 1) * P],
                                        vc.rearrange("p a b -> p (a b)"), start=True, stop=True)
                else:
                    for c in range(b0, b1):
                        ins = pe.matmul(ps[:, 6 + n % 2, 0:DH], PT[:, n % 2, (c - b0) * P:(c - b0 + 1) * P],
                                        v[:, int(kind == "win"), c, :], start=c == b0, stop=c == b1 - 1)
                ins.then_inc(summed.sem, 1)

            with pe.Fori(0, KV_G) as it:
                for s in range(N + LAG_W):
                    if s < N:
                        score(it, s)
                    if 0 <= s - LAG_T < N:
                        transpose(it, s - LAG_T)
                    if s >= LAG_W:
                        weigh(it, s - LAG_W)

        @block.scalar
        def _(act):
            act.sem_inc(prob.sem, prob.credit)
            act.sem_inc(movedA.sem, movedA.credit)
            with act.Fori(0, KV_G) as it:
                for s in range(N + LAG_T):
                    if s < N:
                        kind = items[s][0]
                        p = Pr[:, s % 4, 0:blocks[s] * P]
                        act.wait_ge(shift.sem, shift.after(it, s))
                        if kind == "cmp":
                            act.activation(p, p, ACT.Exp, scale=SCALE).then_inc(prob.sem, 1)
                        else:
                            act.wait_ge(transA.sem, transA.after(it, s - 4))
                            act.wait_ge(transB.sem, transB.after(it, s - 4))
                            act.wait_ge(added.sem, added.after(it, s - 8))
                            act.activation(p, s_of(s), ACT.Exp, scale=SCALE, bias=mx[:, s % 4, 4:5],
                                           accum_out=L[:, s % 8, 0:1]).then_inc(prob.sem, 1)
                    if s >= LAG_T:
                        n = s - LAG_T
                        w = min(4, blocks[n]) * P
                        act.wait_ge(transA.sem, transA.after(it, n))
                        act.wait_ge(summed.sem, summed.after(it, n - 2))
                        act.activation(PT[:, n % 2, 0:w], ps[:, bank_of(n, 0), 0:w], ACT.Copy).then_inc(movedA.sem, 1)

        @block.vector
        def _(dve):
            dve.memset(kc.rearrange("p a b -> p (a b)"), 0.0).then_inc(zeroed, 1)
            dve.memset(vc.rearrange("p a b -> p (a b)"), 0.0).then_inc(zeroed, 1)
            dve.sem_inc(added.sem, added.credit)
            dve.sem_inc(movedB.sem, movedB.credit)
            link = Link(dve, dlink)

            def shift_of(it, n):
                kind = items[n][0]
                dve.wait_ge(scores.sem, scores.after(it, n))
                dve.wait_ge(prob.sem, prob.after(it, n - 4))
                if kind == "cmp":
                    s = s_of(n, R_G * N_CMP).rearrange("p (h n) -> p h n", h=R_G)
                    p = Pr[:, n % 4, 0:R_G * N_CMP].rearrange("p (h n) -> p h n", h=R_G)
                    link(dve.reduce_max(mx[:, n % 4, 0:R_G], s, AX_X))
                    dve.wait_ge(transA.sem, transA.after(it, n - 4))
                    dve.wait_ge(transB.sem, transB.after(it, n - 4))
                    dve.tensor_tensor(p, s, mx[:, n % 4, 0:R_G].unsqueeze(2).broadcast_to([P, R_G, N_CMP]),
                                      ALU.subtract).then_inc(shift.sem, 1)
                else:
                    link(dve.reduce_max(mx[:, n % 4, 0:1], s_of(n), AX_X))
                    dve.tensor_scalar(mx[:, n % 4, 4:5], mx[:, n % 4, 0:1], -SCALE, None, ALU.mult).then_inc(shift.sem, 1)

            def weight_cmp(it, n):
                i = items[n][1]
                l = L[:, n % 8, 0:R_G]
                dve.wait_ge(prob.sem, prob.after(it, n))
                link(dve.reduce_sum(l, Pr[:, n % 4, 0:R_G * N_CMP].rearrange("p (h n) -> p h n", h=R_G), AX_X))
                link(dve.reciprocal(l, l))
                link(dve.scalar_tensor_tensor(out=l, in0=l, scalar=valid[:, i:i + 1], in1=gate[:, i, 0:3 * R_G:3], op0=ALU.mult, op1=ALU.mult))

            def add(it, n):
                kind, i, h, _, _ = items[n]
                l = L[:, n % 8, 0:R_G if kind == "cmp" else 1]
                if kind == "cmp":
                    dve.wait_ge(summed.sem, summed.after(it, n))
                    o = m.o[:, i, bass.ds(it * R_G * DH, R_G * DH)].rearrange("p (h c) -> p h c", c=DH)
                    link(dve.tensor_tensor(o, ps[:, 6 + n % 2, 0:R_G * DH].rearrange("p (h c) -> p h c", c=DH),
                                           l.unsqueeze(2).broadcast_to([P, R_G, DH]), ALU.mult))
                    dve.memset(m.mark[:], 0.0).then_inc(added.sem, 1)
                    return
                g = 3 * h + (1 if kind == "sel" else 2)
                link(dve.reciprocal(l, l))
                link(dve.tensor_tensor(l, l, gate[:, i, g:g + 1], ALU.mult))
                dve.wait_ge(summed.sem, summed.after(it, n))
                o = m.o[:, i, bass.ds(it * R_G * DH + h * DH, DH)]
                dve.scalar_tensor_tensor(out=o, in0=ps[:, 6 + n % 2, 0:DH], scalar=l, in1=o, op0=ALU.mult,
                                         op1=ALU.add).then_inc(added.sem, 1)

            with dve.Fori(0, KV_G) as it:
                link.restart()
                dve.wait_ge(loaded, it * LOADS + LOADS)
                for s in range(N + LAG_A):
                    if s < N:
                        shift_of(it, s)
                    n = s - LAG_T
                    if 0 <= n < N and two[n]:
                        w = (blocks[n] - 4) * P
                        dve.wait_ge(transB.sem, transB.after(it, n))
                        dve.wait_ge(summed.sem, summed.after(it, n - 2))
                        dve.tensor_copy(PT[:, n % 2, 4 * P:4 * P + w], ps[:, bank_of(n, 1), 0:w]).then_inc(movedB.sem, 1)
                    if 1 <= s <= N and items[s - 1][0] == "cmp":
                        weight_cmp(it, s - 1)
                    if s >= LAG_A:
                        add(it, s - LAG_A)


def mix_and_route(nc, ctx, m, a):
    sem = lambda n: ctx.enter_context(nc.semaphore(n))
    U = 4
    one = [1] * U
    x_in = [sem(f"res_in{j}") for j in range(2)]
    o_sq = Count(sem("mix_sq"), one)
    o_norm = Count(sem("mix_norm"), one, 3)
    o_tr = Count(sem("mix_tr"), [2] * U, 5)
    oT_in = Count(sem("mix_oT"), [2] * U, 2)
    proj = Count(sem("mix_proj"), one, 3)
    x1_done = Count(sem("mix_x1"), one, 3)
    h_sq = Count(sem("ffn_sq"), one)
    h_norm = Count(sem("ffn_norm"), one, 3)
    h_tr = Count(sem("ffn_tr"), [2] * U, 5)
    hT_in = Count(sem("ffn_hT"), [2] * U, 2)
    logit = Count(sem("logits_mm"), one, 3)
    logit_in = Count(sem("logits_in"), one, 2)
    stored = [sem(f"h_stored{j}") for j in range(2)]
    m.h_stored = stored
    aln, dlink = sem("mix_ln"), sem("mix_dlink")
    ps = m.ps
    xt, oT, hr = view(m.V, 0, 2, D), view(m.V, 2 * D, 2, ND, P), view(m.V, 4 * D, 2, D)
    hT, junk = view(m.S, 0, 2, ND, P), view(m.S, 2 * D, D)
    o_stage = view(m.S, 3 * D, 2, D)
    st = view(m.S, 5 * D, 2, 8)
    st2 = view(m.S, 5 * D + 16, 2, 8)

    with nc.Block() as block:
        @block.sync
        def _(sp):
            sp.sem_inc(stored[0], 16)
            sp.sem_inc(stored[1], 16)
            sp.dma_start(m.list_d.rearrange("(p n) o -> p (n o)", p=P), m.zero_i[:]).then_inc(m.list_zero, 16)
            with sp.Fori(0, NT // U) as it:
                for n in range(U + 2):
                    if n < U:
                        sp.wait_ge(x1_done.sem, x1_done.after(it, n - 2))
                        sp.dma_start(xt[:, n % 2], a.x[bass.ds((it * U + n) * P, P), :]).then_inc(x_in[n % 2], 16)
                    if n >= 2:
                        k = n - 2
                        sp.wait_ge(h_norm.sem, h_norm.after(it, k))
                        sp.dma_start(m.h_d[bass.ds((it * U + k) * P, P), :], hr[:, k % 2]).then_inc(stored[k % 2], 16)

        @block.scalar
        def _(act):
            link = Link(act, aln)
            with act.Fori(0, NT // U) as it:
                link.restart()
                for s in range(U + 1):
                    if s < U:
                        t = it * U + s
                        act.wait_ge(o_norm.sem, o_norm.after(it, s - 2))
                        for g in range(2):
                            link(act.activation(junk[:, 0:N_Q], m.o[:, bass.ds(t, 1), g * N_Q:(g + 1) * N_Q].rearrange("p a b -> p (a b)"),
                                                ACT.Square, accum_out=st[:, s % 2, g:g + 1]))
                        r = st[:, s % 2, 4:6]
                        link(act.activation(r, st[:, s % 2, 0:2], ACT.Ln, scale=1.0 / N_Q, bias=m.eps[:, 0:1]))
                        act.activation(r, r, ACT.Exp, scale=-0.5).then_inc(o_sq.sem, 1)
                    if s >= 1:
                        n = s - 1
                        t = it * U + n
                        act.wait_ge(x1_done.sem, x1_done.after(it, n))
                        act.wait_ge(h_norm.sem, h_norm.after(it, n - 2))
                        link(act.activation(junk, m.x1[:, bass.ds(t, 1), :].rearrange("p a b -> p (a b)"), ACT.Square,
                                            accum_out=st2[:, n % 2, 0:1]))
                        r = st2[:, n % 2, 4:5]
                        link(act.activation(r, st2[:, n % 2, 0:1], ACT.Ln, scale=1.0 / D, bias=m.eps[:, 0:1]))
                        act.activation(r, r, ACT.Exp, scale=-0.5).then_inc(h_sq.sem, 1)

        @block.vector
        def _(dve):
            for c in (o_norm, oT_in, x1_done, h_norm, hT_in, logit_in):
                dve.sem_inc(c.sem, c.credit)
            link = Link(dve, dlink)

            def gain(it, n, tr, done, w, dst, bank, used):
                dve.wait_ge(used.sem, used.after(it, n - 2))
                for half in range(2):
                    dve.wait_ge(tr.sem, tr.after(it, n) - 1 + half)
                    dve.tensor_tensor(dst[:, n % 2, 4 * half:4 * half + 4, :], ps[:, bank + half, :].rearrange("p (c n) -> p c n", n=P),
                                      w[:, 4 * half:4 * half + 4].unsqueeze(2).broadcast_to([P, 4, P]), ALU.mult).then_inc(done.sem, 1)

            with dve.Fori(0, NT // U) as it:
                link.restart()
                for s in range(U + 2):
                    if s < U:
                        t = it * U + s
                        dve.wait_ge(o_sq.sem, o_sq.after(it, s))
                        newton_rsqrt(dve, link, st[:, s % 2, 4:6], st[:, s % 2, 0:2], N_Q)
                        dve.wait_ge(o_tr.sem, o_tr.after(it, s - 2))
                        for g in range(2):
                            o = m.o[:, bass.ds(t, 1), g * N_Q:(g + 1) * N_Q].rearrange("p a b -> p (a b)")
                            ins = dve.tensor_scalar(o_stage[:, s % 2, g * N_Q:(g + 1) * N_Q], o, st[:, s % 2, 4 + g:5 + g], None, ALU.mult)
                        ins.then_inc(o_norm.sem, 1)
                        gain(it, s, o_tr, oT_in, m.w_mix, oT, 0, proj)
                    if 1 <= s <= U:
                        n = s - 1
                        t = it * U + n
                        dve.wait_ge(proj.sem, proj.after(it, n))
                        dve.wait_ge(x_in[n % 2], it * 16 * (U // 2) + 16 * (n // 2) + 16)
                        dve.tensor_tensor(m.x1[:, bass.ds(t, 1), :].rearrange("p a b -> p (a b)"),
                                          ps[:, 2:4, :].rearrange("p a b -> p (a b)"), xt[:, n % 2], ALU.add).then_inc(x1_done.sem, 1)
                        dve.wait_ge(h_sq.sem, h_sq.after(it, n))
                        newton_rsqrt(dve, link, st2[:, n % 2, 4:5], st2[:, n % 2, 0:1], D)
                        dve.wait_ge(stored[n % 2], it * 16 * (U // 2) + 16 * (n // 2) + 16)
                        dve.wait_ge(h_tr.sem, h_tr.after(it, n - 2))
                        dve.tensor_scalar(hr[:, n % 2], m.x1[:, bass.ds(t, 1), :].rearrange("p a b -> p (a b)"), st2[:, n % 2, 4:5], None,
                                          ALU.mult).then_inc(h_norm.sem, 1)
                    if s >= 2:
                        n = s - 2
                        t = it * U + n
                        gain(it, n, h_tr, hT_in, m.w_ffn, hT, 4, logit)
                        dve.wait_ge(logit.sem, logit.after(it, n))
                        dve.tensor_tensor(m.logits[:, bass.ds(t, 1), :].rearrange("p a b -> p (a b)"), ps[:, 6, 0:N_GRP + N_EXP],
                                          m.b_router[:], ALU.add).then_inc(logit_in.sem, 1)

        @block.tensor
        def _(pe):
            for c in (o_tr, proj, h_tr, logit):
                pe.sem_inc(c.sem, c.credit)
            pe.wait_ge(m.w_out_in, 16)
            pe.wait_ge(m.router_in, 64)
            with pe.Fori(0, NT // U) as it:
                for s in range(U + 2):
                    if s < U:
                        pe.wait_ge(o_norm.sem, o_norm.after(it, s))
                        for half in range(2):
                            pe.wait_ge(oT_in.sem, oT_in.after(it, s - 1) - 1 + half)
                            for c in range(4):
                                k = 4 * half + c
                                ins = pe.transpose(ps[:, half, c * P:(c + 1) * P], o_stage[:, s % 2, k * P:(k + 1) * P], m.ident[:])
                            ins.then_inc(o_tr.sem, 1)
                    if 1 <= s <= U:
                        n = s - 1
                        pe.wait_ge(oT_in.sem, oT_in.after(it, n))
                        pe.wait_ge(x1_done.sem, x1_done.after(it, n - 1))
                        for half in range(2):
                            for c in range(ND):
                                ins = pe.matmul(ps[:, 2 + half, :], oT[:, n % 2, c, :], m.w_out[:, c, half * BANK:(half + 1) * BANK],
                                                start=c == 0, stop=c == ND - 1)
                        ins.then_inc(proj.sem, 1)
                    if s >= 2:
                        n = s - 2
                        pe.wait_ge(h_norm.sem, h_norm.after(it, n))
                        for half in range(2):
                            pe.wait_ge(hT_in.sem, hT_in.after(it, n - 1) - 1 + half)
                            for c in range(4):
                                k = 4 * half + c
                                ins = pe.transpose(ps[:, 4 + half, c * P:(c + 1) * P], hr[:, n % 2, k * P:(k + 1) * P], m.ident[:])
                            ins.then_inc(h_tr.sem, 1)
                        pe.wait_ge(hT_in.sem, hT_in.after(it, n))
                        pe.wait_ge(logit_in.sem, logit_in.after(it, n - 1))
                        for c in range(ND):
                            ins = pe.matmul(ps[:, 6, 0:N_GRP + N_EXP], hT[:, n % 2, c, :], m.w_router[:, c, :], start=c == 0, stop=c == ND - 1)
                        ins.then_inc(logit.sem, 1)


def route(nc, ctx, m, a):
    sem = lambda n: ctx.enter_context(nc.semaphore(n))
    link_s, dif, ex_s, hot, rank, table, listed = map(
        sem, ("route_link", "route_dif", "route_exp", "route_hot", "route_rank", "route_table", "route_listed"))
    ps = m.ps
    r4 = lambda k: view(m.S, k * 32, NT, 4)
    eq, key, og, df, es, o1, o2, e2 = (r4(k) for k in range(8))
    r1 = lambda k: m.S[:, 256 + 8 * k:264 + 8 * k]
    gmax, kmax, gg, m1, m2, ex, den = (r1(k) for k in range(7))
    r16 = lambda k: view(m.S, 512 + k * 128, NT, N_GRP, E_PG)
    sel, H1, H2, dst, pick = (r16(k) for k in range(5))
    cnt, nb, end, start = (m.S[:, 1280 + 16 * k:1296 + 16 * k] for k in range(4))
    over = view(m.S, 1408, N_EXP, N_THR)
    d_f = view(m.S, 1600, 2, NT)
    gl = m.logits[:, :, 0:N_GRP]
    el = m.logits[:, :, N_GRP:].rearrange("p t (g e) -> p t g e", g=N_GRP)
    keys = m.idx_c[:, 0:4].unsqueeze(1).broadcast_to([P, NT, 4])
    thr = m.idx_c[:, C_THR - C_KEY:C_THR - C_KEY + N_THR].unsqueeze(1).broadcast_to([P, N_EXP, N_THR])
    over4 = lambda v: v.unsqueeze(2).broadcast_to([P, NT, 4])

    with nc.Block() as block:
        @block.vector
        def _(dve):
            link = Link(dve, link_s)

            def first_max(v, top, hot_):
                link(dve.reduce_max(top, v, AX_X))
                link(dve.tensor_tensor(eq, v, over4(top), ALU.is_equal))
                link(dve.tensor_tensor(key, eq, keys, ALU.mult))
                link(dve.reduce_max(kmax, key, AX_X))
                link(dve.tensor_tensor(hot_, key, over4(kmax), ALU.is_equal))

            first_max(gl, gmax, og)
            dve.tensor_tensor(df, gl, over4(gmax), ALU.subtract).then_inc(dif, 1)
            link(dve.tensor_tensor(sel, el, og.unsqueeze(3).broadcast_to([P, NT, N_GRP, E_PG]), ALU.mult))
            link(dve.reduce_sum(es, sel.rearrange("p t g e -> p t e g"), AX_X))
            first_max(es, m1, o1)
            link(dve.scalar_tensor_tensor(out=e2.rearrange("p a b -> p (a b)"), in0=o1.rearrange("p a b -> p (a b)"), scalar=NEG,
                                          in1=es.rearrange("p a b -> p (a b)"), op0=ALU.mult, op1=ALU.add))
            first_max(e2, m2, o2)
            dve.tensor_tensor(ex, m2, m1, ALU.subtract).then_inc(dif, 1)
            for hot_, o in ((H1, o1), (H2, o2)):
                link(dve.tensor_tensor(hot_, og.unsqueeze(3).broadcast_to([P, NT, N_GRP, E_PG]),
                                       o.unsqueeze(2).broadcast_to([P, NT, N_GRP, E_PG]), ALU.mult))
            dve.tensor_tensor(m.hot[:].rearrange("p t (g e) -> p t g e", g=N_GRP), H1, H2, ALU.add).then_inc(hot, 1)
            dve.wait_ge(ex_s, 2)
            link(dve.reduce_sum(gg, df, AX_X))
            link(dve.tensor_scalar(den, ex, 1.0, None, ALU.add))
            link(dve.tensor_tensor(den, den, gg, ALU.mult))
            link(dve.reciprocal(m.weight[:, 0, :], den))
            link(dve.tensor_tensor(m.weight[:, 1, :], m.weight[:, 0, :], ex, ALU.mult))
            dve.wait_ge(rank, 1)
            link(dve.tensor_copy(cnt, ps[:, 1, 0:N_EXP]))
            link(dve.tensor_tensor(over, cnt.unsqueeze(2).broadcast_to([P, N_EXP, N_THR]), thr, ALU.is_gt))
            link(dve.reduce_sum(nb, over, AX_X))
            link(dve.tensor_scalar(nb, nb, 1.0, None, ALU.add))
            link(dve.tensor_tensor_scan(end, m.one[:, 0:1].broadcast_to([P, N_EXP]), nb, 0.0, ALU.mult, ALU.add))
            link(dve.tensor_tensor(start, end, nb, ALU.subtract))
            link(dve.tensor_copy(m.blocks[:, 2 * N_EXP:3 * N_EXP], start))
            link(dve.tensor_scalar(m.blocks[:, 3 * N_EXP:], end[:, N_EXP - 1:N_EXP], -1.0, MAX_BLK + 1.0, ALU.mult, ALU.add))
            link(dve.tensor_scalar(start, start, float(BLK), None, ALU.mult))
            d16 = dst.rearrange("p t g e -> p t (g e)")
            link(dve.tensor_tensor(d16, ps[:, 0, 0:NT * N_EXP].rearrange("p (t e) -> p t e", e=N_EXP),
                                   start.unsqueeze(1).broadcast_to([P, NT, N_EXP]), ALU.add))
            for k, hot_ in enumerate((H1, H2)):
                link(dve.tensor_tensor(pick, hot_, dst, ALU.mult))
                link(dve.reduce_sum(d_f[:, k, :], pick.rearrange("p t g e -> p t (g e)"), AX_X))
            dve.tensor_copy(m.dest[:].rearrange("p a b -> p (a b)"), d_f.rearrange("p a b -> p (a b)"))
            dve.tensor_copy(m.tokens[:], m.idx_c[:, C_TOK - C_KEY:C_TOK - C_KEY + NT])
            dve.tensor_copy(m.blocks[:, 0:N_EXP], nb)
            dve.tensor_copy(m.blocks[:, N_EXP:2 * N_EXP], end).then_inc(table, 1)

        @block.scalar
        def _(act):
            act.wait_ge(dif, 1)
            act.activation(df, df, ACT.Exp).then_inc(ex_s, 1)
            act.wait_ge(dif, 2)
            act.activation(ex, ex, ACT.Exp).then_inc(ex_s, 1)

        @block.tensor
        def _(pe):
            pe.wait_ge(hot, 1)
            for t in range(NT):
                for u in range(t + 1):
                    pe.matmul(ps[:, 0, t * N_EXP:(t + 1) * N_EXP], m.tri[:] if u == t else m.ones_b[:], m.hot[:, u, :],
                              start=u == 0, stop=u == t)
            for t in range(NT):
                ins = pe.matmul(ps[:, 1, 0:N_EXP], m.ones_b[:], m.hot[:, t, :], start=t == 0, stop=t == NT - 1)
            ins.then_inc(rank, 1)

        @block.gpsimd
        def _(pool):
            pool.wait_ge(m.list_zero, 16)
            pool.wait_ge(table, 1)
            for k in range(2):
                for t in range(NT):
                    pool.indirect_dma_start(m.list_d, bass.IndirectOffsetOnAxis(ap=m.dest[:, k, t:t + 1], axis=0),
                                            m.tokens[:, t:t + 1], None).then_inc(listed, 16)

        @block.sync
        def _(sp):
            for i in range(4):
                load_matrix(sp, m, a, i, i % 3, i // 3)
            sp.wait_ge(listed, 16 * 2 * NT)
            with nc.allow_non_contiguous_dma("17 KiB of row numbers, to one block a column"):
                sp.dma_start(m.row_tok[:], m.list_d.rearrange("(b p) o -> p (b o)", p=P)).then_inc(m.rows_in, 16)


class Weights:

    def __init__(self, m):
        self.raw = [view(region, 0, 8, BANK) for region in (m.X, m.Y, m.M, m.V)]
        X, Y, M, V, Z = (m.as_r32[name] for name in "XYMVZ")
        self.low = [view(region, 0, 8, BANK) for region in (X, Y, M, V)]
        high = [view(region, 8 * BANK, 8, BANK) for region in (X, Y, M)]
        self.high = [(h[:, 0:4], h[:, 4:8]) for h in high] + [(view(V, 8 * BANK, 4, BANK), view(Z, NT * D, 4, BANK))]

    def hi(self, slot, u, n=1):
        return self.high[slot][u // 4][:, u % 4:u % 4 + n]

    def lo(self, slot, u, n=1):
        return self.low[slot][:, u:u + n]


def load_matrix(eng, m, a, i, kind, e):
    rows, src = (FF, a.w_down_rows) if kind == 2 else (D, (a.w_gate_rows, a.w_up_rows)[kind])
    dst = m.weights.raw[i % 4].rearrange("p a b -> p (a b)").rearrange("p (c f) -> p c f", c=rows // P)
    eng.dma_start(dst, src[bass.ds(e * rows, rows), :].rearrange("(c p) f -> p c f", p=P)).then_inc(m.w_raw[i % 4], 16)


def experts(nc, ctx, m, a):
    sem = lambda n: ctx.enter_context(nc.semaphore(n))
    w_hi, w_lo = sem("moe_w_hi"), sem("moe_w_lo")
    idx_s, x_tr, x_full, x_hi, x_in = map(sem, ("moe_idx", "moe_x_tr", "moe_x_full", "moe_x_hi", "moe_x_in"))
    g_mm, u_mm, silu, hidden = map(sem, ("moe_gate", "moe_up", "moe_silu", "moe_hidden"))
    h_tr, h_hi, h_in, y_mm, y_out = map(sem, ("moe_h_tr", "moe_h_hi", "moe_h_in", "moe_down", "moe_y_out"))
    gathered, m.y_stored, m.y_zeroed, zeroed = sem("moe_gathered"), sem("moe_y_stored"), sem("moe_y_zeroed"), sem("moe_zeros")
    ps, w = m.ps, m.weights
    R = 4
    PASSES = N_EXP // R
    SLOTS = 4
    S = m.as_r32["S"]
    xg, xf, hm = view(m.S, 0, D), view(m.S, 2 * D, ND, P), view(m.S, 3 * D, FF)
    xh, xl = view(S, D, ND, P), view(S, 2 * D, ND, P)
    hh, hl = view(S, 3 * D + FF, NF, P), view(S, 4 * D, NF, P)
    y, zeros = view(m.S, 4 * D + FF, D), view(m.S, 5 * D + FF, D // 2)
    H = FF // 2
    U, HT = (1, 7), (4, 1)

    def blocks_in_all(eng):
        return eng.value_load(m.blocks[0:1, 2 * N_EXP - 1:2 * N_EXP], min_val=N_EXP, max_val=MAX_BLK)

    def blocks_of(eng, it, r):
        return [eng.value_load(m.blocks[0:1, bass.ds(c * N_EXP + it * R + r, 1)], min_val=2 - c, max_val=MAX_BLK - 2 + c) for c in (2, 1)]

    def arrived(it, i):
        return it * (16 * 3 * R // SLOTS) + 16 * (i // SLOTS + 1)

    def split(it, i, q):
        return it * (4 * 3 * R) + 4 * i + q + 1

    with nc.Block() as block:
        @block.sync
        def _(sp):
            sp.wait_ge(zeroed, 1)
            with sp.Fori(blocks_in_all(sp), MAX_BLK + 1) as b:
                for half in range(2):
                    sp.dma_start(m.y_d[bass.ds(b * P, P), half * BANK:(half + 1) * BANK], zeros).then_inc(m.y_zeroed, 16)

            def loads(it, r, gate):
                end = sp.value_load(m.blocks[0:1, bass.ds(N_EXP + it * R + r, 1)], min_val=1, max_val=MAX_BLK)
                e = it * R + r + 1
                sp.wait_ge(g_mm, end)
                load_matrix(sp, m, a, 3 * (r + 1) + 1, 1, e)
                sp.wait_ge(u_mm, end * 2 + 2)
                load_matrix(sp, m, a, 3 * (r + 1) + 2, 2, e)
                if gate:
                    sp.wait_ge(y_mm, end + 1)
                    load_matrix(sp, m, a, 3 * (r + 1) + 3, 0, e + 1)

            with sp.Fori(0, PASSES - 1) as it:
                for r in range(R):
                    loads(it, r, True)
            for r in range(R - 1):
                loads(PASSES - 1, r, r < R - 2)

        @block.gpsimd
        def _(pool):
            pool.wait_ge(m.rows_in, 16)
            for j in range(2):
                pool.wait_ge(m.h_stored[j], 80)
            n = blocks_in_all(pool)
            with pool.Fori(0, n + 1) as b:
                pool.sem_clear(idx_s)
                pool.wait_ge(x_tr, b + 1)
                pool.tensor_copy(m.row_now[:], m.row_tok[:, bass.ds(b, 1)]).then_inc(idx_s, 1)
                pool.wait_ge(idx_s, 1)
                pool.indirect_dma_start(xg, None, m.h_d, bass.IndirectOffsetOnAxis(ap=m.row_now[:], axis=0)).then_inc(gathered, 16)
                pool.wait_ge(gathered, b * 16 + 16)

        @block.tensor
        def _(pe):
            pe.sem_inc(x_tr, 1)
            pe.sem_inc(y_mm, 1)
            pe.sem_inc(u_mm, 2)
            pe.sem_inc(h_tr, 2)

            def transpose_x(b):
                pe.wait_ge(gathered, b * 16 + 16)
                for c in range(ND):
                    ins = pe.transpose(ps[:, 2 + c // 4, c % 4 * P:(c % 4 + 1) * P], xg[:, c * P:(c + 1) * P], m.ident[:])
                ins.then_inc(x_tr, 1)

            def transpose_h(b, half):
                pe.wait_ge(hidden, b * 2 + half + 1)
                for f in range(2):
                    ins = pe.transpose(ps[:, HT[half], f * P:(f + 1) * P], hm[:, (2 * half + f) * P:(2 * half + f + 1) * P], m.ident[:])
                ins.then_inc(h_tr, 1)

            def product(out, left, slot, u, cols, start, stop):
                high, low = left
                hi, lo = (f(slot, u).rearrange("p a b -> p (a b)")[:, cols] for f in (w.hi, w.lo))
                pe.matmul(out, high, hi, start=start, stop=False)
                pe.matmul(out, high, lo, start=False, stop=False)
                return pe.matmul(out, low, hi, start=False, stop=stop)

            transpose_x(0)
            with pe.Fori(0, PASSES) as it:
                for r in range(R):
                    g, u, d = 3 * r, 3 * r + 1, 3 * r + 2
                    first, end = blocks_of(pe, it, r)
                    with pe.Fori(first, end) as b:
                        pe.wait_ge(x_in, b + 1)
                        pe.wait_ge(silu, b + 1)
                        for c in range(ND):
                            if c % 2 == 0:
                                pe.wait_ge(w_lo, split(it, g, c // 2))
                            ins = product(ps[:, 0, :], (xh[:, c], xl[:, c]), g % SLOTS, c, slice(0, FF), c == 0, c == ND - 1)
                        ins.then_inc(g_mm, 1)
                        for half in range(2):
                            cols = slice(half * H, (half + 1) * H)
                            for c in range(ND):
                                if half == 0 and c % 2 == 0:
                                    pe.wait_ge(w_lo, split(it, u, c // 2))
                                ins = product(ps[:, U[half], 0:H], (xh[:, c], xl[:, c]), u % SLOTS, c, cols, c == 0, c == ND - 1)
                            ins.then_inc(u_mm, 1)
                        transpose_h(b, 0)
                        transpose_x(b + 1)
                        transpose_h(b, 1)
                        pe.wait_ge(y_out, b + 1)
                        for f in range(NF):
                            if f % 2 == 0:
                                pe.wait_ge(h_in, b * 2 + f // 2 + 1)
                            pe.wait_ge(w_lo, split(it, d, f))
                            for half in range(2):
                                ins = product(ps[:, 5 + half, :], (hh[:, f], hl[:, f]), d % SLOTS, 2 * f + half, slice(0, BANK),
                                              f == 0, f == NF - 1)
                        ins.then_inc(y_mm, 1)

        @block.scalar
        def _(act):
            act.preload_act_table_set("silu_and_others")
            act.sem_inc(silu, 1)
            act.sem_inc(y_out, 1)
            act.sem_inc(m.y_stored, 16)

            def high_halves(it, i):
                act.wait_ge(m.w_raw[i % SLOTS], arrived(it, i))
                for q in range(4):
                    act.activation(w.hi(i % SLOTS, 2 * q, 2), w.raw[i % SLOTS][:, 2 * q:2 * q + 2], ACT.Copy).then_inc(w_hi, 1)

            def rows_high(b):
                act.wait_ge(x_full, b + 1)
                act.activation(xh, xf, ACT.Copy).then_inc(x_hi, 1)

            def hidden_of(b):
                act.wait_ge(g_mm, b + 1)
                act.wait_ge(h_tr, b * 2 + 2)
                act.activation(hm, ps[:, 0, :], ACT.Silu).then_inc(silu, 1)
                act.wait_ge(y_mm, b + 1)
                for half in range(2):
                    act.wait_ge(h_tr, b * 2 + half + 3)
                    act.activation(hh[:, 2 * half:2 * half + 2],
                                   ps[:, HT[half], 0:2 * P].rearrange("p (a b) -> p a b", b=P), ACT.Copy).then_inc(h_hi, 1)
                rows_high(b + 1)

            def rows_out(b):
                act.wait_ge(y_mm, b + 2)
                act.wait_ge(m.y_stored, b * 16 + 16)
                act.activation(y, ps[:, 5:7, :].rearrange("p a b -> p (a b)"), ACT.Copy).then_inc(y_out, 1)
                act.wait_ge(y_out, b + 2)
                act.dma_start(m.y_d[bass.ds(b * P, P), :], y).then_inc(m.y_stored, 16)

            def last_before(it, r):
                return act.value_load(m.blocks[0:1, bass.ds(N_EXP - 1 + it * R + r, 1)], min_val=1, max_val=MAX_BLK) - 1

            rows_high(0)
            high_halves(0, 0)
            with act.Fori(0, PASSES) as it:
                for r in range(R):
                    high_halves(it, 3 * r + 1)
                    high_halves(it, 3 * r + 2)
                    first, end = blocks_of(act, it, r)
                    if r:
                        rows_out(last_before(it, r))
                    else:
                        with act.If(it > 0):
                            rows_out(last_before(it, r))
                    hidden_of(first)
                    if r < R - 1:
                        high_halves(it, 3 * r + 3)
                    else:
                        with act.If(it < PASSES - 1):
                            high_halves(it, 3 * r + 3)
                    with act.If(first + 1 < end):
                        with act.Fori(first + 1, end) as b:
                            rows_out(b - 1)
                            hidden_of(b)
            rows_out(blocks_in_all(act) - 1)

        @block.vector
        def _(dve):
            dve.memset(zeros, 0.0).then_inc(zeroed, 1)

            def low_halves(it, i):
                raw = w.raw[i % SLOTS]
                for q in range(4):
                    dve.wait_ge(w_hi, split(it, i, q))
                    dve.tensor_tensor(w.lo(i % SLOTS, 2 * q, 2), raw[:, 2 * q:2 * q + 2], w.hi(i % SLOTS, 2 * q, 2), ALU.subtract).then_inc(w_lo, 1)

            def rows_in(b):
                dve.wait_ge(x_tr, b + 2)
                dve.wait_ge(u_mm, b * 2 + 2)
                dve.tensor_tensor(xf, ps[:, 2:4, :].rearrange("p a (c n) -> p (a c) n", n=P),
                                  m.w_ffn[:].unsqueeze(2).broadcast_to([P, ND, P]), ALU.mult).then_inc(x_full, 1)
                dve.wait_ge(x_hi, b + 1)
                dve.tensor_tensor(xl, xf, xh, ALU.subtract).then_inc(x_in, 1)

            def hidden_of(b):
                dve.wait_ge(silu, b + 2)
                for half in range(2):
                    c = slice(half * H, (half + 1) * H)
                    dve.wait_ge(u_mm, b * 2 + half + 3)
                    dve.tensor_tensor(hm[:, c], hm[:, c], ps[:, U[half], 0:H], ALU.mult).then_inc(hidden, 1)
                for half in range(2):
                    fs = slice(2 * half, 2 * half + 2)
                    dve.wait_ge(h_hi, b * 2 + half + 1)
                    dve.tensor_tensor(hl[:, fs], ps[:, HT[half], 0:2 * P].rearrange("p (a b) -> p a b", b=P),
                                      hh[:, fs], ALU.subtract).then_inc(h_in, 1)
                rows_in(b + 1)

            rows_in(0)
            low_halves(0, 0)
            with dve.Fori(0, PASSES) as it:
                for r in range(R):
                    low_halves(it, 3 * r + 1)
                    low_halves(it, 3 * r + 2)
                    first, end = blocks_of(dve, it, r)
                    hidden_of(first)
                    if r < R - 1:
                        low_halves(it, 3 * r + 3)
                    else:
                        with dve.If(it < PASSES - 1):
                            low_halves(it, 3 * r + 3)
                    with dve.If(first + 1 < end):
                        with dve.Fori(first + 1, end) as b:
                            hidden_of(b)


def combine(nc, ctx, m, a, out):
    sem = lambda n: ctx.enter_context(nc.semaphore(n))
    one = [1, 1]
    gathered = [sem("end_g0"), sem("end_g1")]
    idx_s = sem("end_idx")
    added = Count(sem("end_added"), one, 3)
    sq = Count(sem("end_sq"), one)
    done = Count(sem("end_done"), one, 3)
    stored = [sem("out_stored0"), sem("out_stored1")]
    aln, dlink, wf = sem("end_ln"), sem("end_dlink"), sem("end_wf")
    y = view(m.X, 0, 2, 2, D)
    acc, junk, w = view(m.X, 4 * D, 2, D), view(m.X, 6 * D, D), view(m.X, 7 * D, D)
    o = view(m.Y, 0, 2, D)
    st = view(m.S, 0, 2, 8)

    with nc.Block() as block:
        @block.gpsimd
        def _(pool):
            n = pool.value_load(m.blocks[0:1, 2 * N_EXP - 1:2 * N_EXP], min_val=N_EXP, max_val=MAX_BLK)
            unused = pool.value_load(m.blocks[0:1, 3 * N_EXP:3 * N_EXP + 1], min_val=1, max_val=MAX_BLK + 1 - N_EXP)
            with pool.Fori(0, NT // 2) as it:
                pool.sem_clear(idx_s)
                pool.wait_ge(m.y_stored, n * 16 + 16)
                pool.wait_ge(m.y_zeroed, unused * 32)
                for s in range(2):
                    pool.wait_ge(added.sem, added.after(it, s - 2))
                    for k in range(2):
                        pool.tensor_copy(m.dest_now[:, s, k:k + 1], m.dest[:, k, bass.ds(it * 2 + s, 1)]).then_inc(idx_s, 1)
                        pool.wait_ge(idx_s, 2 * s + k + 1)
                        pool.indirect_dma_start(y[:, s, k], None, m.y_d, bass.IndirectOffsetOnAxis(ap=m.dest_now[:, s, k:k + 1], axis=0)).then_inc(gathered[s], 16)

        @block.vector
        def _(dve):
            dve.sem_inc(added.sem, added.credit)
            dve.sem_inc(done.sem, done.credit)
            link = Link(dve, dlink)
            dve.wait_ge(wf, 16)
            with dve.Fori(0, NT // 2) as it:
                link.restart()
                for s in range(2):
                    t = it * 2 + s
                    dve.wait_ge(gathered[s], it * 32 + 32)
                    x1 = m.x1[:, bass.ds(t, 1), :].rearrange("p a b -> p (a b)")
                    wt = [m.weight[:, k, bass.ds(t, 1)] for k in range(2)]
                    link(dve.scalar_tensor_tensor(out=acc[:, s], in0=y[:, s, 0], scalar=wt[0], in1=x1, op0=ALU.mult, op1=ALU.add))
                    dve.scalar_tensor_tensor(out=acc[:, s], in0=y[:, s, 1], scalar=wt[1], in1=acc[:, s], op0=ALU.mult,
                                             op1=ALU.add).then_inc(added.sem, 1)
                    dve.wait_ge(sq.sem, sq.after(it, s))
                    newton_rsqrt(dve, link, st[:, s, 4:5], st[:, s, 0:1], D)
                    dve.wait_ge(stored[s], it * 16 + 16)
                    dve.scalar_tensor_tensor(out=o[:, s], in0=acc[:, s], scalar=st[:, s, 4:5], in1=w, op0=ALU.mult,
                                             op1=ALU.mult).then_inc(done.sem, 1)

        @block.scalar
        def _(act):
            act.preload_act_table_set("natural_log_exp_and_others")
            link = Link(act, aln)
            with act.Fori(0, NT // 2) as it:
                link.restart()
                for s in range(2):
                    act.wait_ge(added.sem, added.after(it, s))
                    act.wait_ge(done.sem, done.after(it, s - 2))
                    link(act.activation(junk, acc[:, s], ACT.Square, accum_out=st[:, s, 0:1]))
                    r = st[:, s, 4:5]
                    link(act.activation(r, st[:, s, 0:1], ACT.Ln, scale=1.0 / D, bias=m.eps[:, 0:1]))
                    act.activation(r, r, ACT.Exp, scale=-0.5).then_inc(sq.sem, 1)

        @block.sync
        def _(sp):
            for s in range(2):
                sp.sem_inc(stored[s], 16)
            sp.dma_start(w, a.final_norm_w.partition_broadcast(P)).then_inc(wf, 16)
            with sp.Fori(0, NT // 2) as it:
                for s in range(2):
                    sp.wait_ge(done.sem, done.after(it, s))
                    sp.dma_start(out[bass.ds((it * 2 + s) * P, P), :], o[:, s]).then_inc(stored[s], 16)
            for s in range(2):
                sp.wait_ge(stored[s], 16 + 16 * (NT // 2))


INPUTS = ["x", "positions", "attn_norm_w", "w_in", "cmp_pe_k", "cmp_pe_v", "cmp_k_w1", "cmp_k_w2", "cmp_v_w1",
          "cmp_v_w2", "nsa_out_norm_w", "sb_out_norm_w", "w_out", "ffn_norm_w", "router_group_w",
          "router_group_b", "router_expert_w", "router_expert_b", "w_gate", "w_up", "w_down", "final_norm_w"]


def build(nc, a, out):
    m = Mem()
    with ExitStack() as ctx:
        sb = lambda n, s, d=F32: ctx.enter_context(nc.sbuf_tensor(n, s, d))
        sem = lambda n: ctx.enter_context(nc.semaphore(n))
        m.ident = sb("ident", [P, P])
        m.ident_b = sb("ident_b", [P, P], BF16)
        m.causal = sb("causal", [P, P], BF16)
        m.strict = sb("strict", [P, P], BF16)
        m.winmask = sb("winmask", [P, P], BF16)
        m.tri = sb("tri", [P, P], BF16)
        m.ones_b = sb("ones_b", [P, P], BF16)
        m.ones = sb("ones", [P, 2])
        m.cmpmask = sb("cmpmask", [P, NT, N_CMP], BF16)
        m.idx_c = sb("idx_c", [P, C_ALL - C_KEY])
        m.w_attn = sb("w_attn", [P, ND])
        m.w_mix = sb("w_mix", [P, ND])
        m.w_ffn = sb("w_ffn", [P, ND])
        m.pos = sb("pos", [P, NT], I32)
        m.trig = sb("trig", [P, 2, NT, 8])
        m.eps, m.clip, m.one = sb("eps", [P, 1]), sb("clip", [P, 1]), sb("one", [P, 1])
        m.stat = sb("stat", [P, 8])
        m.rstd = sb("rstd", [P, 8])
        m.w_gates = sb("w_gates", [P, ND, N_GATE])
        m.gates = sb("gates", [P, NT, N_GATE])
        m.w_router = sb("w_router", [P, ND, N_GRP + N_EXP])
        m.b_router = sb("b_router", [P, N_GRP + N_EXP])
        def region(name, kib):
            at = -(-nc.sbuf_base // 32) * 32
            return sb(name, [P, kib * KB]), nc.alloc_sbuf_tensor_at(name + "_r32", [P, kib * KB], F32R, offset=at)

        m.as_r32 = {}
        m.X, m.as_r32["X"] = region("X", 32)
        m.Y, m.as_r32["Y"] = region("Y", 32)
        m.Z, m.as_r32["Z"] = region("Z", 40)
        m.V, m.as_r32["V"] = region("V", 24)
        m.S, m.as_r32["S"] = region("S", 24)
        m.M, m.as_r32["M"] = region("M", 32)
        m.ps = ctx.enter_context(nc.psum_tensor("ps", [P, 8, BANK], F32))
        m.hT = view(m.X, 0, ND, T)
        m.keys = view(m.M, 0, 2, 2, T)
        m.w_ring = view(m.Y, 0, 2, ND, BANK)
        m.groups = [0, COL_SEL, COL_SBV]
        m.w_loaded = [sem("w_loaded0"), sem("w_loaded1")]
        m.w_gates_loaded = sem("w_gates_loaded")
        m.router_in = sem("router_in")
        m.qT = view(m.Z, 0, 4, T)
        m.kT = view(m.Z, 16 * KB, 2, T)
        m.vsw = view(m.Z, 24 * KB, NT, 2, P)
        m.ckv = view(m.Z, 32 * KB, KV_G, T)
        m.mark = sb("mark", [P, 1])
        m.sbqk_rows = nc.dram_tensor("sb_qk_scratch", (2 * SB_H * DH, T), F32, kind="Internal").ap()
        m.sbv_d = nc.dram_tensor("sb_v_scratch", (NT, P, BANK), F32, kind="Internal").ap()
        m.w_out = view(m.Y, 0, ND, D)
        m.w_out_in = sem("w_out_in")
        m.x1 = view(m.Z, 0, NT, D)
        m.logits = sb("logits", [P, NT, N_GRP + N_EXP])
        m.hot = sb("hot", [P, NT, N_EXP], BF16)
        m.weight = sb("weight", [P, 2, NT])
        m.dest = sb("dest", [P, 2, NT], I32)
        m.dest_now = sb("dest_now", [P, 2, 2], I32)
        m.tokens = sb("tokens", [P, NT], I32)
        m.blocks = sb("blocks", [P, 3 * N_EXP + 1], I32)
        m.row_tok = sb("row_tok", [P, MAX_BLK + 1], I32)
        m.row_now = sb("row_now", [P, 1], I32)
        m.zero_i = sb("zero_i", [P, MAX_BLK + 1], I32)
        m.list_zero, m.rows_in = sem("list_zero"), sem("rows_in")
        m.weights = Weights(m)
        m.w_raw = [sem(f"w_raw{j}") for j in range(4)]
        m.list_d = nc.dram_tensor("row_list_scratch", (ROWS, 1), I32, kind="Internal").ap()
        m.h_d = nc.dram_tensor("h_scratch", (T, D), F32, kind="Internal").ap()
        m.y_d = nc.dram_tensor("y_scratch", (ROWS, D), F32, kind="Internal").ap()
        m.o = view(m.X, 0, NT, D)
        m.w2 = sb("cmp_w2", [P, 2, 2, 2, DH])
        m.pe_rows = sb("cmp_pe", [CMP_LEN, 2, DH])
        m.kc = sb("kc", [P, KV_G, N_CMP])
        m.vc = sb("vc", [P, KV_G, DH])
        m.cmp_w = sem("cmp_w_loaded")
        hidden_states(nc, ctx, m, a)
        projections(nc, ctx, m, a)
        stick_breaking(nc, ctx, m, a)
        compression(nc, ctx, m, a)
        native_sparse(nc, ctx, m, a)
        mix_and_route(nc, ctx, m, a)
        route(nc, ctx, m, a)
        experts(nc, ctx, m, a)
        combine(nc, ctx, m, a, out)


class Args:
    pass


def kernel(**inputs):
    import concourse.bacc as _bacc
    from concourse.bass_utils import run_bass_kernel_spmd as _run

    nc = _bacc.Bacc("TRN2", target_bir_lowering=False, num_devices=1)
    arrays, a = {}, Args()
    for name in INPUTS:
        arr = np.ascontiguousarray(inputs[name])
        if arr.ndim > 1:
            arr = arr[0]
        arrays[name] = arr
        a.__dict__[name] = nc.dram_tensor(name, arr.shape, mybir.dt.from_np(arr.dtype), kind="ExternalInput").ap()
    arrays["shape_constants"] = constants()
    a.cst = nc.dram_tensor("shape_constants", (P, C_ALL), F32, kind="ExternalInput").ap()
    a.w_gate_rows = a.w_gate.rearrange("e d f -> (e d) f")
    a.w_up_rows = a.w_up.rearrange("e d f -> (e d) f")
    a.w_down_rows = a.w_down.rearrange("e f d -> (e f) d")
    a.w_in_rows = a.w_in.rearrange("(c p) n -> p c n", p=P)
    out = nc.dram_tensor("out", (T, D), F32, kind="ExternalOutput").ap()
    build(nc, a, out)
    r = _run(nc, [arrays], core_ids=[0])
    return r.results[0]["out"].reshape(1, T, D)
```

```python
from contextlib import ExitStack

import numpy as np

import concourse.bass as bass
from concourse import mybir
from concourse.alu_op_type import AluOpType as ALU

F32 = mybir.dt.float32
F32R = mybir.dt.float32r
BF16 = mybir.dt.bfloat16
I32 = mybir.dt.int32
U32 = mybir.dt.uint32
ACT = mybir.ActivationFunctionType
AX_X = mybir.AxisListType.X

P = 128
T = 1024
D = 1024
NT = T // P
ND = D // P
BANK = 512
DH = 64
HALF = DH // 8
NSA_H, KV_G, SB_H = 8, 2, 8
R_G = NSA_H // KV_G
N_Q = NSA_H * DH
COL_CMP = N_Q
COL_SEL = COL_CMP + 2 * KV_G * DH
COL_GATE = N_Q + 6 * KV_G * DH
N_GATE = 3 * NSA_H
COL_SBQ = COL_GATE + N_GATE
COL_SBK = COL_SBQ + SB_H * DH
COL_SBV = COL_SBK + SB_H * DH
CMP_LEN, CMP_STRIDE, CMP_HID = 32, 16, 256
N_CMP = 64
WIN_TILES = 512 // P
N_EXP, N_GRP, E_PG, FF = 16, 4, 4, 512
NF = FF // P
BLK = 128
MAX_BLK = 2 * T // BLK + N_EXP
ROWS = (MAX_BLK + 1) * BLK
EPS = 1e-6
NEG = -1e30
SCALE = DH ** -0.5
THETA = 500000.0
CLIP = 40.0

C_ID, C_CAUSAL, C_STRICT, C_WIN, C_TRI, C_CMP = 0, 128, 256, 384, 512, 640
C_FREQ = C_CMP + NT * N_CMP
C_KEY = C_FREQ + 8
C_THR = C_KEY + 4
N_THR = T // BLK - 1
C_VALID = C_THR + N_THR
C_TOK = C_VALID + NT
C_ALL = C_TOK + NT


def constants():
    c = np.zeros((P, C_ALL), np.float32)
    r, k = np.arange(P)[:, None], np.arange(P)[None, :]
    c[:, C_ID:C_ID + P] = r == k
    c[:, C_CAUSAL:C_CAUSAL + P] = np.where(k > r, NEG, 0.0)
    c[:, C_STRICT:C_STRICT + P] = np.where(k >= r, NEG, 0.0)
    c[:, C_WIN:C_WIN + P] = np.where(k <= r, NEG, 0.0)
    c[:, C_TRI:C_TRI + P] = r < k
    n = np.arange(N_CMP)[None, :]
    for i in range(NT):
        seen = (n * CMP_STRIDE + CMP_LEN - 1 <= i * P + r) & (n < N_CMP - 1)
        c[:, C_CMP + i * N_CMP:C_CMP + (i + 1) * N_CMP] = np.where(seen, 0.0, NEG)
        c[:, C_VALID + i] = (i * P + r[:, 0]) >= CMP_LEN - 1
        c[:, C_TOK + i] = i * P + r[:, 0]
    c[:, C_FREQ:C_FREQ + 8] = np.float32(THETA) ** (-np.arange(0, 16, 2, dtype=np.float32) / np.float32(16))
    c[:, C_KEY:C_KEY + 4] = [4, 3, 2, 1]
    c[:, C_THR:C_THR + N_THR] = BLK * np.arange(1, N_THR + 1)
    return c


class Link:

    def __init__(self, eng, sem):
        self.eng, self.sem, self.n = eng, sem, 0

    def later(self, ins):
        self.n += 1
        ins.then_inc(self.sem, 1)
        return self.n

    def wait(self, n):
        self.eng.wait_ge(self.sem, n)

    def __call__(self, ins):
        self.wait(self.later(ins))

    def restart(self):
        self.eng.sem_clear(self.sem)
        self.n = 0


def table_rsqrt(act, m, ln_done, n, out, total, width):
    act.activation(out, total, ACT.Ln, scale=1.0 / width, bias=m.eps[:, 0:1]).then_inc(ln_done, 1)
    act.wait_ge(ln_done, n)
    return act.activation(out, out, ACT.Exp, scale=-0.5)


def newton_rsqrt(dve, link, r, total, width):
    t = total
    link(dve.tensor_scalar(t, total, -0.5 / width, -0.5 * EPS, ALU.mult, ALU.add))
    link(dve.tensor_tensor(t, t, r, ALU.mult))
    link(dve.tensor_tensor(t, t, r, ALU.mult))
    link(dve.scalar_tensor_tensor(out=r, in0=t, scalar=1.5, in1=r, op0=ALU.add, op1=ALU.mult))


def product(pe, out, left, right, start, stop):
    pe.matmul(out, left[0], right[0], start=start, stop=False)
    pe.matmul(out, left[0], right[1], start=False, stop=False)
    return pe.matmul(out, left[1], right[0], start=False, stop=stop)


class Mem:
    pass


def view(region, off, *shape):
    n = int(np.prod(shape))
    ap = region[:, off:off + n]
    if len(shape) == 2:
        ap = ap.rearrange("p (a b) -> p a b", b=shape[1])
    if len(shape) == 3:
        ap = ap.rearrange("p (a b c) -> p a b c", b=shape[1], c=shape[2])
    if len(shape) == 4:
        ap = ap.rearrange("p (a b c d) -> p a b c d", b=shape[1], c=shape[2], d=shape[3])
    return ap


KB = 256


def hidden_states(nc, ctx, m, a):
    sem = lambda n: ctx.enter_context(nc.semaphore(n))
    x_in = [sem(f"x_in{j}") for j in range(4)]
    const_in, small_in, x_sq, x_norm, h_tr, h_free, x_rstd, x_ln = map(
        sem, ("const_in", "small_in", "x_sq", "x_norm", "h_tr", "h_free", "x_rstd", "x_ln"))
    ang_r, trig, dlink, plink, ident_in, gain_in = sem("ang_r"), sem("trig"), sem("dlink_h"), sem("plink_h"), sem("ident_in"), sem("gain_in")
    x = view(m.V, 0, 4, D)
    junk = view(m.V, 4 * D, D)
    cst = m.S[:, 0:C_ALL]
    tmp = view(m.S, C_ALL, 8, NT, 8)
    ps = m.ps
    freq = cst[:, C_FREQ:C_FREQ + 8]
    h_hi = sem("h_hi")
    hT = view(m.M, 0, ND, T)

    def part(t, it, j, half):
        return t[:, 4 * half:4 * half + 4, bass.ds(it * 512 + j * P, P)]

    with nc.Block() as block:
        @block.sync
        def _(sp):
            sp.dma_start(x[:, 0, :], a.x[0:P, :]).then_inc(x_in[0], 16)
            sp.dma_start(m.ident[:], a.cst[:, C_ID:C_ID + P]).then_inc(ident_in, 16)
            with nc.allow_non_contiguous_dma("gain columns, 12 KiB in all"):
                sp.dma_start(m.w_attn[:], a.attn_norm_w.rearrange("(c p) -> p c", p=P)).then_inc(gain_in, 16)
            for j in range(1, 4):
                sp.dma_start(x[:, j, :], a.x[j * P:(j + 1) * P, :]).then_inc(x_in[j], 16)
            sp.dma_start(cst, a.cst).then_inc(const_in, 16)
            with nc.allow_non_contiguous_dma("gain columns, 12 KiB in all"):
                sp.dma_start(m.w_ffn[:], a.ffn_norm_w.rearrange("(c p) -> p c", p=P)).then_inc(small_in, 16)
                sp.dma_start(m.w_mix[:, 0:4], a.nsa_out_norm_w.rearrange("(c p) -> p c", p=P)).then_inc(small_in, 16)
                sp.dma_start(m.w_mix[:, 4:8], a.sb_out_norm_w.rearrange("(c p) -> p c", p=P)).then_inc(small_in, 16)
                sp.dma_start(m.pos[:], a.positions.rearrange("(c p) -> p c", p=P)).then_inc(small_in, 16)
            for j in range(4):
                sp.wait_ge(h_tr, 2 * j + 2)
                sp.dma_start(x[:, j, :], a.x[(4 + j) * P:(5 + j) * P, :]).then_inc(x_in[j], 16)
            for g in range(2):
                sp.dma_start(m.w_raw_in[g], a.w_in_rows[:, :, m.groups[g]:m.groups[g] + BANK]).then_inc(m.w_loaded[g], 16)
            with nc.allow_non_contiguous_dma("the gate columns, 96 bytes a row"):
                sp.dma_start(m.w_gates[:], a.w_in_rows[:, :, COL_GATE:COL_GATE + N_GATE]).then_inc(m.w_gates_loaded, 16)
                sp.dma_start(m.w_router[:, :, 0:N_GRP], a.router_group_w.rearrange("(c p) n -> p c n", p=P)).then_inc(m.router_in, 16)
                sp.dma_start(m.w_router[:, :, N_GRP:N_GRP + N_EXP], a.router_expert_w.rearrange("(c p) n -> p c n", p=P)).then_inc(m.router_in, 16)
                sp.dma_start(m.b_router[:, 0:N_GRP], a.router_group_b.partition_broadcast(P)).then_inc(m.router_in, 16)
                sp.dma_start(m.b_router[:, N_GRP:N_GRP + N_EXP], a.router_expert_b.partition_broadcast(P)).then_inc(m.router_in, 16)

        @block.scalar
        def _(act):
            act.preload_act_table_set("natural_log_exp_and_others")
            with act.Fori(0, 2) as it:
                for j in range(5):
                    if j < 4:
                        act.wait_ge(x_in[j], it * 16 + 16)
                        if j == 0:
                            act.wait_ge(x_norm, it * 4 + 1)
                        act.activation(junk, x[:, j, :], ACT.Square, accum_out=m.stat[:, j:j + 1]).then_inc(x_sq, 1)
                        act.wait_ge(x_sq, it * 4 + j + 1)
                        table_rsqrt(act, m, x_ln, it * 4 + j + 1, m.rstd[:, j:j + 1], m.stat[:, j:j + 1], D).then_inc(x_rstd, 1)
                    if j:
                        for half in range(2):
                            act.wait_ge(h_free, it * 8 + 2 * (j - 1) + half + 3)
                            act.activation(part(m.hT_hi, it, j - 1, half), part(hT, it, j - 1, half), ACT.Copy).then_inc(h_hi, 1)
            act.wait_ge(ang_r, 1)
            act.activation(m.trig[:].rearrange("p a b c -> p (a b c)"), tmp[:, 4:6].rearrange("p a b c -> p (a b c)"), ACT.Sin).then_inc(trig, 1)
            act.preload_act_table_set("natural_log_exp_and_others")

        @block.vector
        def _(dve):
            link = Link(dve, dlink)
            dve.memset(m.clip[:], CLIP)
            dve.memset(m.zero_i[:], 0)
            dve.memset(m.one[:], 1.0)
            dve.memset(m.eps[:], EPS).then_inc(x_norm, 1)
            dve.wait_ge(gain_in, 16)
            with dve.Fori(0, 2) as it:
                link.restart()
                def low_halves(j):
                    for half in range(2):
                        dve.wait_ge(h_hi, it * 8 + 2 * j + half + 1)
                        dve.tensor_tensor(part(m.hT_lo, it, j, half), part(hT, it, j, half), part(m.hT_hi, it, j, half), ALU.subtract)

                for j in range(4):
                    dve.wait_ge(x_rstd, it * 4 + j + 1)
                    newton_rsqrt(dve, link, m.rstd[:, j:j + 1], m.stat[:, j:j + 1], D)
                    dve.tensor_scalar(x[:, j, :], x[:, j, :], m.rstd[:, j:j + 1], None, ALU.mult).then_inc(x_norm, 1)
                    for half in range(2):
                        dve.wait_ge(h_tr, it * 8 + 2 * j + half + 1)
                        dve.tensor_tensor(part(hT, it, j, half),
                                          ps[:, 4 + half, :].rearrange("p (c n) -> p c n", n=P),
                                          m.w_attn[:, 4 * half:4 * half + 4].unsqueeze(2).broadcast_to([P, 4, P]),
                                          ALU.mult).then_inc(h_free, 1)
                    if j:
                        low_halves(j - 1)
                low_halves(3)

        @block.gpsimd
        def _(pool):
            pool.wait_ge(const_in, 16)
            pool.wait_ge(small_in, 64)
            link = Link(pool, plink)
            for dst, c0 in ((m.ident_b, C_ID), (m.causal, C_CAUSAL), (m.strict, C_STRICT), (m.winmask, C_WIN), (m.tri, C_TRI)):
                pool.tensor_copy(dst[:], cst[:, c0:c0 + P])
            pool.tensor_copy(m.cmpmask[:].rearrange("p a b -> p (a b)"), cst[:, C_CMP:C_CMP + NT * N_CMP])
            pool.tensor_copy(m.idx_c[:], cst[:, C_KEY:C_ALL])
            pool.memset(m.ones_b[:], 1.0)
            pool.memset(m.ones[:], 1.0)
            pos, turns = tmp[:, 7, :, 0], tmp[:, 6]
            link(pool.tensor_copy(pos, m.pos[:]))
            ang = tmp[:, 0]
            link(pool.tensor_tensor(ang, pos.unsqueeze(2).broadcast_to([P, NT, 8]), freq.unsqueeze(1).broadcast_to([P, NT, 8]), ALU.mult))
            magic = 1.5 * 2 ** 23
            two_pi = 2 * np.pi
            c1 = 6.28125
            c2 = float(np.float32(int((two_pi - c1) * 2 ** 20) / 2 ** 20))
            c3 = two_pi - c1 - c2
            for which, turn, shift in ((0, 0.0, 0.0), (1, 0.25, np.pi / 2)):
                k, r = tmp[:, 2 + which], tmp[:, 4 + which]
                link(pool.tensor_scalar(k, ang, 1.0 / two_pi, turn, ALU.mult, ALU.add))
                link(pool.tensor_scalar(k, k, magic, None, ALU.add))
                link(pool.tensor_scalar(k, k, magic, None, ALU.subtract))
                for n, part_of_2pi in enumerate((c1, c2, c3)):
                    link(pool.tensor_scalar(turns, k, -part_of_2pi, None, ALU.mult))
                    link(pool.tensor_tensor(r, turns, r if n else ang, ALU.add))
                if which:
                    link(pool.tensor_scalar(r, r, shift, None, ALU.add))
                ins = pool.tensor_scalar(r, r, 3.1415925, -3.1415925, ALU.min, ALU.max)
                if which:
                    ins.then_inc(ang_r, 1)
                else:
                    link(ins)

        @block.tensor
        def _(pe):
            pe.sem_inc(h_free, 2)
            pe.wait_ge(ident_in, 16)
            with pe.Fori(0, 2) as it:
                for j in range(4):
                    pe.wait_ge(x_norm, it * 4 + j + 2)
                    for half in range(2):
                        pe.wait_ge(h_free, it * 8 + 2 * j + half + 1)
                        for c in range(4):
                            ins = pe.transpose(ps[:, 4 + half, c * P:(c + 1) * P], x[:, j, (4 * half + c) * P:(4 * half + c + 1) * P], m.ident[:])
                        ins.then_inc(h_tr, 1)


def projections(nc, ctx, m, a):
    sem = lambda n: ctx.enter_context(nc.semaphore(n))
    mm, mm_free, rot_in, rot, rtmp, tr, tr_free = map(
        sem, ("proj_mm", "proj_free", "rot_in", "rot_done", "rot_link", "rot_tr", "rot_free"))
    gate_mm, gate_in, gate_tr, gate_exp = sem("gate_mm"), sem("gate_in"), sem("gate_tr"), sem("gate_exp")
    stored = [sem(f"stage_stored{j}") for j in range(4)]
    m.proj_stored = stored
    ps = m.ps
    NB = 4
    stage = view(m.S, 0, 4, BANK)
    rows = view(m.S, 4 * BANK, 2, BANK)
    tmp = view(m.S, 6 * BANK, 4, 64)
    w_hi, w_lo, wg_hi, wg_lo = sem("win_hi"), sem("win_lo"), sem("gates_hi"), sem("gates_lo")
    Yr, Vr, Zr, Sr = (m.as_r32[name] for name in "YVZS")
    low = [view(Yr, g * ND * BANK, ND, BANK) for g in range(2)]
    high = [(view(Vr, 0, 4, BANK), view(Vr, 4 * BANK, 4, BANK)), (view(Vr, 8 * BANK, 4, BANK), view(Zr, 8 * T, 4, BANK))]
    CMP = 5
    cmp_raw = view(m.Y, ND * BANK, KV_G, ND, 2, DH)
    cmp_lo, cmp_hi = view(Yr, ND * BANK, KV_G, ND, P), view(Vr, 8 * BANK, KV_G, ND, P)
    gates_hi, gates_lo = (view(Sr, 6 * BANK + 256 + x * ND * N_GATE, ND, N_GATE) for x in range(2))
    gates_T = m.S[0:N_GATE, 4096:4096 + T]
    quarters = lambda g: 2 if g == CMP else 4
    first_item = [0, NT, 2 * NT, 3 * NT, 4 * NT, 5 * NT]
    N_ALL = 5 * NT + 2 * KV_G
    staged = [2 * NT, 5 * NT]

    with nc.Block() as block:
        @block.sync
        def _(sp):
            def load(g):
                sp.wait_ge(mm, first_item[g - 1])
                if g < CMP:
                    sp.dma_start(m.w_raw_in[g % 2], a.w_in_rows[:, :, m.groups[g]:m.groups[g] + BANK]).then_inc(m.w_loaded[g % 2], 16)
                else:
                    for kvg in range(KV_G):
                        for kv in range(2):
                            c0 = COL_CMP + kv * KV_G * DH + kvg * DH
                            sp.dma_start(cmp_raw[:, kvg, :, kv, :], a.w_in_rows[:, :, c0:c0 + DH]).then_inc(m.w_loaded[g % 2], 16)

            load(2)
            load(3)
            for n in range(*staged):
                if n % NT == 0 and n > staged[0]:
                    load(n // NT + 1)
                sp.wait_ge(mm_free, n + 1)
                k = n - 3 * NT
                dst = m.sbv_d[n % NT] if k < 0 else m.sbqk_rows[k // 2 * P:(k // 2 + 1) * P, k % 2 * BANK:(k % 2 + 1) * BANK]
                sp.dma_start(dst, stage[:, n % 4]).then_inc(stored[n % 4], 16)

        @block.tensor
        def _(pe):
            def item(n, g, operands):
                if n >= NB:
                    pe.wait_ge(mm_free, n - NB + 1)
                for c in range(ND):
                    if n == first_item[g] and c % 2 == 0:
                        pe.wait_ge(w_lo, 4 * g + (c // 2 + 1 if g < CMP else 2))
                    left, right = operands(c)
                    ins = product(pe, ps[:, n % NB, :], left, right, c == 0, c == ND - 1)
                ins.then_inc(mm, 1)

            def h(c, cols):
                return m.hT_hi[:, c, cols], m.hT_lo[:, c, cols]

            def w(g, c, cols):
                return high[g % 2][c // 4][:, c % 4, cols], low[g % 2][:, c, cols]

            def rows_of(g, t):
                item(NT * g + t, g, lambda c: (h(c, slice(t * P, (t + 1) * P)), w(g, c, slice(0, BANK))))

            def back(k, heads):
                pe.wait_ge(rot, k + 1)
                if k >= 2:
                    pe.wait_ge(tr_free, k - 1)
                for q, c0 in enumerate(heads):
                    ins = pe.transpose(ps[:, 4 + k % 2, q * P:(q + 1) * P], rows[:, k % 2, c0:c0 + P], m.ident[:])
                ins.then_inc(tr, 1)

            q_cols, k_cols = [0, P, 2 * P, 3 * P], [0, 2 * P]
            for t in range(NT):
                rows_of(0, t)
                if t:
                    back(t - 1, q_cols)
            for t in range(NT):
                rows_of(1, t)
                back(NT + t - 1, q_cols if t == 0 else k_cols)
            pe.wait_ge(wg_lo, 1)
            for half in range(2):
                for c in range(ND):
                    ins = product(pe, ps[0:N_GATE, 6 + half, :], (gates_hi[:, c], gates_lo[:, c]), h(c, slice(half * BANK, (half + 1) * BANK)),
                                  c == 0, c == ND - 1)
            ins.then_inc(gate_mm, 1)
            back(2 * NT - 1, k_cols)
            rows_of(2, 0)
            pe.wait_ge(gate_in, 1)
            for t in range(NT):
                ins = pe.transpose(ps[:, 6, t * N_GATE:(t + 1) * N_GATE], gates_T[:, t * P:(t + 1) * P], m.ident[0:N_GATE, 0:N_GATE])
            ins.then_inc(gate_tr, 1)
            for t in range(1, NT):
                rows_of(2, t)
            for g in (3, 4):
                for k in range(NT):
                    cols, tokens = slice(k // 2 * P, (k // 2 + 1) * P), slice(k % 2 * BANK, (k % 2 + 1) * BANK)
                    item(g * NT + k, g, lambda c: (w(g, c, cols), h(c, tokens)))
            for k in range(2 * KV_G):
                tokens = slice(k % 2 * BANK, (k % 2 + 1) * BANK)
                item(CMP * NT + k, CMP, lambda c: ((cmp_hi[:, k // 2, c], cmp_lo[:, k // 2, c]), h(c, tokens)))

        @block.scalar
        def _(act):
            def high_halves(g):
                act.wait_ge(m.w_loaded[g % 2], 16 * (g // 2 + 1) if g < CMP else 16 * (g // 2) + 64)
                for q in range(quarters(g)):
                    act.activation(high[g % 2][q // 2][:, 2 * (q % 2):2 * (q % 2) + 2], m.w_raw_in[g % 2][:, 2 * q:2 * q + 2], ACT.Copy).then_inc(w_hi, 1)

            high_halves(0)
            for n in range(N_ALL):
                g, t = n // NT, n % NT
                if g == 2 and t == 0:
                    act.wait_ge(gate_mm, 1)
                    act.activation(gates_T, ps[0:N_GATE, 6:8, :].rearrange("p a b -> p (a b)"), ACT.Copy).then_inc(gate_in, 1)
                if g == 2 and t == 1:
                    act.wait_ge(gate_tr, 1)
                    act.activation(m.gates[:].rearrange("p a b -> p (a b)"), ps[:, 6, 0:NT * N_GATE], ACT.Exp, scale=-1.0).then_inc(gate_exp, 1)
                act.wait_ge(mm, n + 1)
                out = ps[:, n % NB, :]
                if g < 2:
                    if n >= 2:
                        act.wait_ge(tr, n - 1)
                    act.activation(rows[:, n % 2], out, ACT.Copy).then_inc(mm_free if g == 0 else rot_in, 1)
                    if g == 1:
                        act.activation(m.vsw[:, t, :, :], out.rearrange("p (w v c) -> p w v c", w=2, v=2)[:, :, 1, :],
                                       ACT.Copy).then_inc(mm_free, 1)
                elif g < CMP:
                    if n >= staged[0] + 4:
                        act.wait_ge(stored[n % 4], 16 * ((n - staged[0]) // 4))
                    act.activation(stage[:, n % 4], out, ACT.Copy).then_inc(mm_free, 1)
                else:
                    act.activation(m.ckv[:, t // 2, t % 2 * BANK:(t % 2 + 1) * BANK], out, ACT.Copy).then_inc(mm_free, 1)
                if t == 3 and g < CMP:
                    high_halves(g + 1)
                    if g == 0:
                        act.wait_ge(m.w_gates_loaded, 16)
                        act.activation(gates_hi, m.w_gates[:], ACT.Copy).then_inc(wg_hi, 1)

        @block.vector
        def _(dve):
            link = Link(dve, rtmp)

            def rotate(k, t, heads):
                v = heads(rows[:, k % 2])
                nh = NSA_H if len(v.shape) == 3 else 4
                x1, x2 = v[..., 0:8], v[..., 8:16]
                shape = [P] + list(v.shape[1:-1]) + [8]
                sin, cos = m.trig[:, 0, t, :], m.trig[:, 1, t, :]
                for _ in shape[1:-1]:
                    sin, cos = sin.unsqueeze(1), cos.unsqueeze(1)
                sin, cos = sin.broadcast_to(shape), cos.broadcast_to(shape)
                pr = [tmp[:, q, 0:nh * 8].rearrange("p (h c) -> p h c", c=8) if len(shape) == 3 else
                      tmp[:, q, 0:nh * 8].rearrange("p (w h c) -> p w h c", w=2, c=8) for q in range(4)]
                dve.tensor_tensor(pr[0], x1, cos, ALU.mult)
                dve.tensor_tensor(pr[1], x2, sin, ALU.mult)
                dve.tensor_tensor(pr[2], x2, cos, ALU.mult)
                link(dve.tensor_tensor(pr[3], x1, sin, ALU.mult))
                dve.tensor_tensor(x1, pr[0], pr[1], ALU.subtract)
                link(dve.tensor_tensor(x2, pr[2], pr[3], ALU.add))

            q_heads = lambda r: r.rearrange("p (h c) -> p h c", c=DH)[:, :, 0:16]
            k_heads = lambda r: r.rearrange("p (w v h c) -> p w v h c", w=2, v=2, c=DH)[:, :, 0, :, 0:16]

            def collect(k):
                t = k % NT
                dve.wait_ge(tr, k + 1)
                if k < NT:
                    dve.tensor_copy(m.qT[:, :, t * P:(t + 1) * P], ps[:, 4 + k % 2, :].rearrange("p (a b) -> p a b", b=P)).then_inc(tr_free, 1)
                else:
                    dve.tensor_copy(m.kT[:, :, t * P:(t + 1) * P], ps[:, 4 + k % 2, 0:2 * P].rearrange("p (a b) -> p a b", b=P)).then_inc(tr_free, 1)

            def low_halves(g):
                for q in range(quarters(g)):
                    u = slice(2 * q, 2 * q + 2)
                    dve.wait_ge(w_hi, 4 * g + q + 1)
                    dve.tensor_tensor(low[g % 2][:, u], m.w_raw_in[g % 2][:, u], high[g % 2][q // 2][:, 2 * (q % 2):2 * (q % 2) + 2],
                                      ALU.subtract).then_inc(w_lo, 1)

            low_halves(0)
            for k in range(2 * NT):
                if k < NT:
                    dve.wait_ge(mm_free, k + 1)
                else:
                    dve.wait_ge(rot_in, k - NT + 1)
                rotate(k, k % NT, q_heads if k < NT else k_heads)
                dve.memset(m.mark[:], 0.0).then_inc(rot, 1)
                if k:
                    collect(k - 1)
                if k % NT == 3:
                    low_halves(k // NT + 1)
                    if k < NT:
                        dve.wait_ge(wg_hi, 1)
                        dve.tensor_tensor(gates_lo, m.w_gates[:], gates_hi, ALU.subtract).then_inc(wg_lo, 1)
            collect(2 * NT - 1)
            dve.wait_ge(gate_exp, 1)
            g = m.gates[:].rearrange("p a b -> p (a b)")
            link(dve.tensor_scalar(g, g, 1.0, None, ALU.add))
            link(dve.reciprocal(g, g))
            for g in range(3, CMP + 1):
                low_halves(g)


class Count:

    def __init__(self, sem, steps, credit=0):
        self.sem, self.credit = sem, credit
        self.upto = [0]
        for s in steps:
            self.upto.append(self.upto[-1] + s)
        self.total = self.upto[-1]

    def after(self, it, n):
        k = len(self.upto) - 1
        back = 0
        while n < 0:
            n, back = n + k, back + self.total
        c = self.upto[n + 1] - back + self.credit
        return it * self.total + c


def stick_breaking(nc, ctx, m, a):
    sem = lambda n: ctx.enter_context(nc.semaphore(n))
    units = []
    for j in range(2):
        for i in range(NT):
            top = 4 if i >= 4 else 0
            w = i + 1 - top
            if 2 * w <= 4:
                units.append((j, i, [(0, top, i + 1, 0), (1, top, i + 1, w)]))
            else:
                units += [(j, i, [(h, top, i + 1, 0)]) for h in range(2)]
            if top:
                units += [(j, i, [(h, 0, top, 0)]) for h in range(2)]
    N = len(units)
    width = [sum(b1 - b0 for _, b0, b1, _ in u[2]) * P for u in units]
    last = [n + 1 == N or units[n + 1][:2] != units[n][:2] for n in range(N)]
    tile_of = [sum(last[:n]) for n in range(N)]
    one = [1] * N
    loaded = [sem("sb_in0"), sem("sb_in1")]
    scores = Count(sem("sb_scores"), one)
    soft = Count(sem("sb_soft"), one)
    arg = Count(sem("sb_arg"), one, 4)
    prob = Count(sem("sb_prob"), one)
    trans = Count(sem("sb_trans"), one, 6)
    moved = Count(sem("sb_moved"), one, 2)
    summed = Count(sem("sb_summed"), [int(any(b0 == 0 for _, b0, _, _ in u[2])) for u in units], 4)
    out = Count(sem("sb_out"), [1] * sum(last), 2)
    alink, dlink = sem("sb_alink"), sem("sb_dlink")
    ps = m.ps
    q, v = view(m.S, 0, 2, T), view(m.S, 2 * T, 2, NT, P)
    k = m.keys
    zeroed = sem("sb_zeroed")
    E, C, AT = view(m.V, 0, 6, BANK), view(m.V, 6 * BANK, 6, BANK), view(m.S, 4 * T, 4, BANK)
    m.w1 = view(m.Y, 0, 2, CMP_STRIDE, CMP_HID)
    m.kv2 = view(m.M, 4 * T, 2, KV_G, T)
    LAG_P, LAG_C, LAG_T, LAG_W = 2, 3, 4, 5

    def cols(span):
        h, b0, b1, at = span
        return slice(at * P, (at + b1 - b0) * P)

    def later(n, h):
        return next((b, span) for b in range(n) for span in units[b][2] if units[b][:2] == units[n][:2] and span[0] == h)

    with nc.Block() as block:
        @block.sync
        def _(sp):
            def load(j, hp):
                sp.dma_start(q[:, j], m.sbqk_rows[bass.ds(hp * P, P), :]).then_inc(loaded[j], 16)
                for h in range(2):
                    sp.dma_start(k[h * DH:(h + 1) * DH, j, h], m.sbqk_rows[bass.ds(hp * P + SB_H * DH + h * DH, DH), :]).then_inc(loaded[j], 16)
                sp.dma_start(v[:, j], m.sbv_d[:, :, bass.ds(hp * P, P)].rearrange("t p c -> p t c")).then_inc(loaded[j], 16)

            for n in range(4):
                sp.wait_ge(m.proj_stored[n], 96)
            sp.wait_ge(zeroed, 2)
            load(0, 0)
            load(1, 1)
            for kv, (w1, w2, pe_) in enumerate(((a.cmp_k_w1, a.cmp_k_w2, a.cmp_pe_k), (a.cmp_v_w1, a.cmp_v_w2, a.cmp_pe_v))):
                for up in range(2):
                    half, rows = slice(up * DH, (up + 1) * DH), CMP_STRIDE * DH
                    sp.dma_start(m.w1[half, kv], w1[up * rows:(up + 1) * rows, :].rearrange("(l d) h -> d l h", d=DH)).then_inc(m.cmp_w, 16)
                    sp.dma_start(m.pe_rows[:, kv, up, :], pe_[up * CMP_STRIDE:(up + 1) * CMP_STRIDE, :]).then_inc(m.cmp_w, 16)
                    sp.dma_start(m.kv2[half, kv, :, 0:T - up * CMP_STRIDE], m.ckv[kv * DH:(kv + 1) * DH, :, up * CMP_STRIDE:T]).then_inc(m.cmp_w, 16)
                for dup in range(2):
                    sp.dma_start(m.w2[:, kv, :, dup, :], w2.rearrange("(c p) n -> p c n", p=P)).then_inc(m.cmp_w, 16)
            for j in range(2):
                sp.wait_ge(summed.sem, summed.after(0, (j + 1) * N // 2 - 1))
                load(j, 2 + j)

        @block.tensor
        def _(pe):
            pe.sem_inc(trans.sem, trans.credit)
            pe.sem_inc(summed.sem, summed.credit)

            def score(it, n):
                j, i, spans = units[n]
                if n % (N // 2) == 0:
                    pe.wait_ge(loaded[j], it * 64 + 64)
                pe.wait_ge(arg.sem, arg.after(it, n - 4))
                for span in spans:
                    h, b0, b1, at = span
                    ins = pe.matmul(ps[:, n % 4, cols(span)], q[:, j, i * P:(i + 1) * P], k[:, j, h, b0 * P:b1 * P],
                                    start=True, stop=b1 <= i)
                    if b1 > i:
                        d = (at + i - b0) * P
                        ins = pe.matmul(ps[:, n % 4, d:d + P], m.ident_b[:], m.strict[:], start=False, stop=True)
                ins.then_inc(scores.sem, 1)

            def transpose(it, n):
                pe.wait_ge(prob.sem, prob.after(it, n))
                pe.wait_ge(moved.sem, moved.after(it, n - 2))
                for c in range(width[n] // P):
                    ins = pe.transpose(ps[:, 4 + n % 2, c * P:(c + 1) * P], C[:, n % 6, c * P:(c + 1) * P], m.ident[:])
                ins.then_inc(trans.sem, 1)

            def weigh(it, n):
                j, i, spans = units[n]
                t = tile_of[n]
                pe.wait_ge(moved.sem, moved.after(it, n))
                pe.wait_ge(out.sem, out.after(it, t - 2))
                ins = None
                for span in spans:
                    h, b0, b1, at = span
                    if b0 > 0:
                        continue
                    parts = ([] if b1 > i else [later(n, h)]) + [(n, span)]
                    for b, (_, c0, c1, to) in parts:
                        for c in range(c0, c1):
                            ins = pe.matmul(ps[:, 6 + t % 2, h * DH:(h + 1) * DH], AT[:, b % 4, (to + c - c0) * P:(to + c - c0 + 1) * P],
                                            v[:, j, c, h * DH:(h + 1) * DH], start=c == parts[0][1][1], stop=c == b1 - 1 and b == n)
                if ins:
                    ins.then_inc(summed.sem, 1)

            with pe.Fori(0, 2) as it:
                for s in range(N + LAG_W):
                    if s < N:
                        score(it, s)
                    if 0 <= s - LAG_T < N:
                        transpose(it, s - LAG_T)
                    if s >= LAG_W:
                        weigh(it, s - LAG_W)

        @block.scalar
        def _(act):
            act.sem_inc(out.sem, out.credit)

            link = Link(act, alink)
            with act.Fori(0, 2) as it:
                link.restart()
                for s in range(N + LAG_W + 1):
                    if s < N:
                        e = E[:, s % 6, 0:width[s]]
                        act.wait_ge(scores.sem, scores.after(it, s))
                        act.wait_ge(arg.sem, arg.after(it, s - 4))
                        link(act.activation(e, ps[:, s % 4, 0:width[s]], ACT.Relu, scale=-SCALE, bias=m.clip[:, 0:1]))
                        link(act.activation(e, e, ACT.Exp, scale=-1.0, bias=m.clip[:, 0:1]))
                        act.activation(e, e, ACT.Ln, bias=m.one[:, 0:1]).then_inc(soft.sem, 1)
                    if 0 <= s - LAG_P < N:
                        n = s - LAG_P
                        c = C[:, n % 6, 0:width[n]]
                        act.wait_ge(arg.sem, arg.after(it, n))
                        act.activation(c, c, ACT.Exp).then_inc(prob.sem, 1)
                    n = s - LAG_W - 1
                    if n >= 0 and last[n]:
                        j, i, _ = units[n]
                        act.wait_ge(summed.sem, summed.after(it, n))
                        act.activation(m.o[:, i, bass.ds(it * 2 * P + N_Q + j * P, P)], ps[:, 6 + tile_of[n] % 2, 0:P],
                                       ACT.Copy).then_inc(out.sem, 1)

        @block.vector
        def _(dve):
            for h in range(2):
                dve.memset(k[(1 - h) * DH:(2 - h) * DH, :, h, :], 0.0).then_inc(zeroed, 1)
            dve.memset(m.kv2[DH:P, :, :, T - CMP_STRIDE:T].rearrange("p a b n -> p (a b) n"), 0.0)
            dve.sem_inc(arg.sem, arg.credit)
            dve.sem_inc(moved.sem, moved.credit)
            link = Link(dve, dlink)

            def copy_out(it, n):
                dve.wait_ge(trans.sem, trans.after(it, n))
                dve.wait_ge(summed.sem, summed.after(it, n - 2))
                dve.tensor_copy(AT[:, n % 4, 0:width[n]], ps[:, 4 + n % 2, 0:width[n]]).then_inc(moved.sem, 1)

            def exponent(it, n):
                j, i, spans = units[n]
                w = width[n]
                z, e, c = ps[:, n % 4, 0:w], E[:, n % 6, 0:w], C[:, n % 6, 0:w]
                dve.wait_ge(soft.sem, soft.after(it, n))
                softplus = link.later(dve.scalar_tensor_tensor(out=e, in0=z, scalar=SCALE, in1=e, op0=ALU.mult, op1=ALU.max))
                if n >= LAG_C:
                    copy_out(it, n - LAG_C)
                link.wait(softplus)
                for span in spans:
                    h, b0, b1, at = span
                    es = e[:, cols(span)][:, ::-1]
                    start = 0.0
                    if b1 <= i:
                        b, (_, _, _, to) = later(n, h)
                        start = E[:, b % 6, to * P:to * P + 1]
                    ins = dve.tensor_tensor_scan(es, m.one[:, 0:1].broadcast_to([P, (b1 - b0) * P]), es, start, ALU.mult, ALU.add)
                    link(ins)
                dve.wait_ge(trans.sem, trans.after(it, n - 6))
                dve.scalar_tensor_tensor(out=c, in0=z, scalar=SCALE, in1=e, op0=ALU.mult, op1=ALU.subtract).then_inc(arg.sem, 1)

            with dve.Fori(0, 2) as it:
                link.restart()
                for s in range(N + LAG_C):
                    if s < N:
                        exponent(it, s)
                    else:
                        copy_out(it, s - LAG_C)


def compression(nc, ctx, m, a):
    sem = lambda n: ctx.enter_context(nc.semaphore(n))
    pe_t, pe_c, blocks, hid, hexp, hsilu, fin, clink = map(
        sem, ("cmp_pe_t", "cmp_pe_c", "cmp_blocks", "cmp_hid", "cmp_exp", "cmp_silu", "cmp_fin", "cmp_link"))
    ps = m.ps
    kb = view(m.S, 0, 2 * KV_G, CMP_STRIDE, N_CMP)
    peT = view(m.S, 4096, 2, CMP_STRIDE)
    ex = view(m.S, 4352, 2, 2, KV_G * N_CMP)
    hk = view(m.S, 4864, 2, KV_G * N_CMP)
    hv = view(m.S, 5120, 2, KV_G, 2, N_CMP)

    with nc.Block() as block:
        @block.tensor
        def _(pe):
            pe.wait_ge(m.cmp_w, 256)
            for kv in range(2):
                ins = pe.transpose(ps[:, 7, kv * CMP_STRIDE:(kv + 1) * CMP_STRIDE], m.pe_rows[:, kv].rearrange("p a b -> p (a b)"),
                                   m.ident[0:CMP_STRIDE, 0:CMP_STRIDE])
            ins.then_inc(pe_t, 1)
            for kv in range(2):
                pe.wait_ge(blocks, KV_G * (kv + 1))
                for c in range(2):
                    for l in range(CMP_STRIDE):
                        ins = pe.matmul(ps[:, 2 * kv + c, 0:P], m.w1[:, kv, l, c * P:(c + 1) * P], kb[:, KV_G * kv:KV_G * (kv + 1), l, :],
                                        start=l == 0, stop=l == CMP_STRIDE - 1)
                    ins.then_inc(hid, 1)
            pe.wait_ge(hsilu, 4)
            for c in range(2):
                pe.matmul(ps[:, 4, 0:P], m.w2[:, 0, c].rearrange("p a b -> p (a b)"), hk[:, c], start=c == 0, stop=c == 1)
            for g in range(KV_G):
                for c in range(2):
                    ins = pe.matmul(ps[:, 5, g * DH:(g + 1) * DH], hv[:, c, g].rearrange("p a b -> p (a b)"), m.w2[:, 1, c, 0],
                                    start=c == 0, stop=c == 1)
            ins.then_inc(fin, 1)

        @block.vector
        def _(dve):
            link = Link(dve, clink)
            dve.wait_ge(pe_t, 1)
            dve.tensor_copy(peT, ps[:, 7, 0:2 * CMP_STRIDE].rearrange("p (a b) -> p a b", b=CMP_STRIDE)).then_inc(pe_c, 1)
            dve.wait_ge(pe_c, 1)
            for kv in range(2):
                for g in range(KV_G):
                    dve.tensor_tensor(kb[:, KV_G * kv + g], m.kv2[:, kv, g].rearrange("p (n l) -> p l n", l=CMP_STRIDE),
                                      peT[:, kv].unsqueeze(2).broadcast_to([P, CMP_STRIDE, N_CMP]), ALU.add).then_inc(blocks, 1)
            for kv in range(2):
                for c in range(2):
                    n = 2 * kv + c
                    e = ex[:, kv, c]
                    dve.wait_ge(hexp, n + 1)
                    link(dve.tensor_scalar(e, e, 1.0, None, ALU.add))
                    link(dve.reciprocal(e, e))
                    if kv == 0:
                        dve.tensor_tensor(hk[:, c], ps[:, n, 0:P], e, ALU.mult).then_inc(hsilu, 1)
                    else:
                        dst = hv[:, c]
                        for dup in range(2):
                            ins = dve.tensor_tensor(dst[:, :, dup, :], ps[:, n, 0:P].rearrange("p (g n) -> p g n", g=KV_G),
                                                    e.rearrange("p (g n) -> p g n", g=KV_G), ALU.mult)
                            if dup == 0:
                                link(ins)
                        ins.then_inc(hsilu, 1)
            dve.wait_ge(fin, 1)
            dve.tensor_copy(m.kc[:].rearrange("p a b -> p (a b)"), ps[:, 4, 0:P])
            dve.tensor_copy(m.vc[:].rearrange("p a b -> p (a b)"), ps[:, 5, 0:P])

        @block.scalar
        def _(act):
            for kv in range(2):
                for c in range(2):
                    act.wait_ge(hid, 2 * kv + c + 1)
                    act.activation(ex[:, kv, c], ps[:, 2 * kv + c, 0:P], ACT.Exp, scale=-1.0).then_inc(hexp, 1)


def native_sparse(nc, ctx, m, a):
    sem = lambda n: ctx.enter_context(nc.semaphore(n))
    items = []
    for i in range(NT):
        items.append(("cmp", i, None, 0, 2))
        for h in range(R_G):
            items.append(("sel", i, h, 0, i + 1))
            items.append(("win", i, h, max(0, i - WIN_TILES), i + 1))
    N = len(items)
    LAG_T, LAG_W, LAG_A = 2, 3, 4
    blocks = [b1 - b0 for _, _, _, b0, b1 in items]
    one = [1] * N
    two = [int(b > 4) for b in blocks]
    first, users, owner, at = [], [], [-1] * 4, 0
    for n in range(N):
        nb = 1 + two[n]
        if at + nb > 4:
            at = 0
        first.append(at)
        users.append(max(owner[at:at + nb]))
        owner[at:at + nb] = [n] * nb
        at = (at + nb) % 4
    turns = [(n, half) for n in range(N) for half in range(1 + two[n])]
    loaded = sem("nsa_in")
    scores = Count(sem("nsa_scores"), one)
    shift = Count(sem("nsa_shift"), one)
    prob = Count(sem("nsa_prob"), one, 4)
    transA = Count(sem("nsa_transA"), one, 4)
    transB = Count(sem("nsa_transB"), two, 4)
    movedA = Count(sem("nsa_movedA"), one, 2)
    movedB = Count(sem("nsa_movedB"), two, 2)
    summed = Count(sem("nsa_summed"), one, 3)
    added = Count(sem("nsa_added"), one, 8)
    dlink = sem("nsa_dlink")
    w_out_hi = sem("w_out_hi")
    ps = m.ps
    q, v = view(m.S, 0, 2, T), view(m.S, 2 * T, 2, NT, DH)
    keys = m.keys
    kc, vc = view(m.S, 3 * T, 2, N_CMP), view(m.S, 3 * T + 2 * N_CMP, 2, DH)
    gate = view(m.S, 3 * T + 4 * N_CMP, NT, 3 * R_G)
    zeroed = sem("nsa_zeroed")
    Pr, PT = view(m.V, 0, 4, T), view(m.S, 4 * T, 2, T)
    L = view(m.S, 3 * T + 384, 8, 8)
    mx = view(m.S, 3 * T + 448, 4, 8)
    valid = m.idx_c[:, C_VALID - C_KEY:C_VALID - C_KEY + NT]

    def s_of(n, w=None):
        return ps[:, first[n]:first[n] + 1 + two[n], :].rearrange("p a b -> p (a b)")[:, 0:w or blocks[n] * P]

    def bank_of(n, half):
        return 4 + turns.index((n, half)) % 2

    with nc.Block() as block:
        @block.sync
        def _(sp):
            sp.wait_ge(zeroed, 2)
            with sp.Fori(0, KV_G) as g:
                sp.wait_ge(summed.sem, g * N + summed.credit)
                sp.dma_start(q, m.qT[:, bass.ds(g * 2, 2), :]).then_inc(loaded, 16)
                for group, mine in ((0, g < 1), (1, g > 0)):
                    with sp.If(mine):
                        for up in range(2):
                            for kind in range(2):
                                sp.dma_start(keys[up * DH:(up + 1) * DH, kind, up], m.kT[group * DH:(group + 1) * DH, kind, :]).then_inc(loaded, 16)
                for b in range(2):
                    sp.dma_start(v[:, b], m.vsw[:, :, b, bass.ds(g * DH, DH)]).then_inc(loaded, 16)
                for up in range(2):
                    half = slice(up * DH, (up + 1) * DH)
                    sp.dma_start(kc[half, up], m.kc[half, g, :]).then_inc(loaded, 16)
                    sp.dma_start(vc[half, up], m.vc[half, g, :]).then_inc(loaded, 16)
                sp.wait_ge(added.sem, g * N + added.credit)
                sp.dma_start(gate, m.gates[:, :, bass.ds(g * 3 * R_G, 3 * R_G)]).then_inc(loaded, 16)
            sp.dma_start(m.w_out, a.w_out.rearrange("(c p) n -> p c n", p=P)).then_inc(m.w_out_in, 16)
        LOADS = 16 * 12

        @block.gpsimd
        def _(pool):
            pool.wait_ge(m.w_out_in, 16)
            for half in range(2):
                cols = slice(half * BANK, (half + 1) * BANK)
                for quad in range(2):
                    cs = slice(4 * quad, 4 * quad + 4)
                    pool.tensor_copy(m.w_out_hi[half][quad], m.w_out[:, cs, cols]).then_inc(w_out_hi, 1)
                    pool.wait_ge(w_out_hi, 2 * half + quad + 1)
                    pool.tensor_tensor(m.w_out_lo[:, cs, cols], m.w_out[:, cs, cols], m.w_out_hi[half][quad], ALU.subtract).then_inc(m.w_out_split, 1)

        @block.tensor
        def _(pe):
            for c in (transA, transB, summed):
                pe.sem_inc(c.sem, c.credit)

            def score(it, n):
                kind, i, h, b0, b1 = items[n]
                if n == 0:
                    pe.wait_ge(loaded, it * LOADS + LOADS)
                pe.wait_ge(prob.sem, prob.after(it, users[n]))
                s = s_of(n, (1 + two[n]) * BANK)
                if kind == "cmp":
                    pe.matmul(s[:, 0:R_G * N_CMP], m.ident_b[:], m.cmpmask[:, i, :].unsqueeze(1).broadcast_to([P, R_G, N_CMP]),
                              start=True, stop=False)
                    for pair in range(2):
                        ins = pe.matmul(s[:, pair * P:(pair + 1) * P], q[:, pair, i * P:(i + 1) * P],
                                        kc.rearrange("p a b -> p (a b)"), start=False, stop=pair == 1)
                    ins.then_inc(scores.sem, 1)
                    return
                w = (b1 - b0) * P
                masks = [(i - b0, m.causal)] + ([(0, m.winmask)] if kind == "win" and i >= WIN_TILES else [])
                for c in range(0, w, BANK):
                    e = min(w, c + BANK)
                    here = [(blk, t) for blk, t in masks if c <= blk * P < e]
                    pe.matmul(s[:, c:e], q[:, h // 2, i * P:(i + 1) * P], keys[:, int(kind == "win"), h % 2, b0 * P + c:b0 * P + e],
                              start=True, stop=not here)
                    for x, (blk, t) in enumerate(here):
                        ins = pe.matmul(s[:, blk * P:(blk + 1) * P], m.ident_b[:], t[:], start=False, stop=x == len(here) - 1)
                ins.then_inc(scores.sem, 1)

            def transpose(it, n):
                pe.wait_ge(prob.sem, prob.after(it, n))
                for half, t in ((0, transA), (1, transB))[0:1 + two[n]]:
                    g = turns.index((n, half))
                    for use, mv in ((0, movedA), (1, movedB)):
                        if g < 2:
                            pe.wait_ge(mv.sem, mv.after(it, -1))
                        elif turns[g - 2][1] == use:
                            pe.wait_ge(mv.sem, mv.after(it, turns[g - 2][0]))
                    for c in range(4 * half, min(4 * half + 4, blocks[n])):
                        ins = pe.transpose(ps[:, bank_of(n, half), (c - 4 * half) * P:(c - 4 * half + 1) * P],
                                           Pr[:, n % 4, c * P:(c + 1) * P], m.ident[:])
                    ins.then_inc(t.sem, 1)

            def weigh(it, n):
                kind, i, h, b0, b1 = items[n]
                pe.wait_ge(movedA.sem, movedA.after(it, n))
                pe.wait_ge(movedB.sem, movedB.after(it, n))
                pe.wait_ge(added.sem, added.after(it, n - 2))
                if kind == "cmp":
                    for pair in range(2):
                        ins = pe.matmul(ps[:, 6 + n % 2, pair * P:(pair + 1) * P], PT[:, n % 2, pair * P:(pair + 1) * P],
                                        vc.rearrange("p a b -> p (a b)"), start=True, stop=True)
                else:
                    for c in range(b0, b1):
                        ins = pe.matmul(ps[:, 6 + n % 2, 0:DH], PT[:, n % 2, (c - b0) * P:(c - b0 + 1) * P],
                                        v[:, int(kind == "win"), c, :], start=c == b0, stop=c == b1 - 1)
                ins.then_inc(summed.sem, 1)

            with pe.Fori(0, KV_G) as it:
                for s in range(N + LAG_W):
                    if s < N:
                        score(it, s)
                    if 0 <= s - LAG_T < N:
                        transpose(it, s - LAG_T)
                    if s >= LAG_W:
                        weigh(it, s - LAG_W)

        @block.scalar
        def _(act):
            act.sem_inc(prob.sem, prob.credit)
            act.sem_inc(movedA.sem, movedA.credit)
            with act.Fori(0, KV_G) as it:
                for s in range(N + LAG_T):
                    if s < N:
                        kind = items[s][0]
                        p = Pr[:, s % 4, 0:blocks[s] * P]
                        act.wait_ge(shift.sem, shift.after(it, s))
                        if kind == "cmp":
                            act.activation(p, p, ACT.Exp, scale=SCALE).then_inc(prob.sem, 1)
                        else:
                            act.wait_ge(transA.sem, transA.after(it, s - 4))
                            act.wait_ge(transB.sem, transB.after(it, s - 4))
                            act.wait_ge(added.sem, added.after(it, s - 8))
                            act.activation(p, s_of(s), ACT.Exp, scale=SCALE, bias=mx[:, s % 4, 4:5],
                                           accum_out=L[:, s % 8, 0:1]).then_inc(prob.sem, 1)
                    if s >= LAG_T:
                        n = s - LAG_T
                        w = min(4, blocks[n]) * P
                        act.wait_ge(transA.sem, transA.after(it, n))
                        act.wait_ge(summed.sem, summed.after(it, n - 2))
                        act.activation(PT[:, n % 2, 0:w], ps[:, bank_of(n, 0), 0:w], ACT.Copy).then_inc(movedA.sem, 1)

        @block.vector
        def _(dve):
            dve.memset(kc.rearrange("p a b -> p (a b)"), 0.0).then_inc(zeroed, 1)
            dve.memset(vc.rearrange("p a b -> p (a b)"), 0.0).then_inc(zeroed, 1)
            dve.sem_inc(added.sem, added.credit)
            dve.sem_inc(movedB.sem, movedB.credit)
            link = Link(dve, dlink)

            def shift_of(it, n):
                kind = items[n][0]
                dve.wait_ge(scores.sem, scores.after(it, n))
                dve.wait_ge(prob.sem, prob.after(it, n - 4))
                if kind == "cmp":
                    s = s_of(n, R_G * N_CMP).rearrange("p (h n) -> p h n", h=R_G)
                    p = Pr[:, n % 4, 0:R_G * N_CMP].rearrange("p (h n) -> p h n", h=R_G)
                    link(dve.reduce_max(mx[:, n % 4, 0:R_G], s, AX_X))
                    dve.wait_ge(transA.sem, transA.after(it, n - 4))
                    dve.wait_ge(transB.sem, transB.after(it, n - 4))
                    dve.tensor_tensor(p, s, mx[:, n % 4, 0:R_G].unsqueeze(2).broadcast_to([P, R_G, N_CMP]),
                                      ALU.subtract).then_inc(shift.sem, 1)
                else:
                    link(dve.reduce_max(mx[:, n % 4, 0:1], s_of(n), AX_X))
                    dve.tensor_scalar(mx[:, n % 4, 4:5], mx[:, n % 4, 0:1], -SCALE, None, ALU.mult).then_inc(shift.sem, 1)

            def weight_cmp(it, n):
                i = items[n][1]
                l = L[:, n % 8, 0:R_G]
                dve.wait_ge(prob.sem, prob.after(it, n))
                link(dve.reduce_sum(l, Pr[:, n % 4, 0:R_G * N_CMP].rearrange("p (h n) -> p h n", h=R_G), AX_X))
                link(dve.reciprocal(l, l))
                link(dve.scalar_tensor_tensor(out=l, in0=l, scalar=valid[:, i:i + 1], in1=gate[:, i, 0:3 * R_G:3], op0=ALU.mult, op1=ALU.mult))

            def add(it, n):
                kind, i, h, _, _ = items[n]
                l = L[:, n % 8, 0:R_G if kind == "cmp" else 1]
                if kind == "cmp":
                    dve.wait_ge(summed.sem, summed.after(it, n))
                    o = m.o[:, i, bass.ds(it * R_G * DH, R_G * DH)].rearrange("p (h c) -> p h c", c=DH)
                    link(dve.tensor_tensor(o, ps[:, 6 + n % 2, 0:R_G * DH].rearrange("p (h c) -> p h c", c=DH),
                                           l.unsqueeze(2).broadcast_to([P, R_G, DH]), ALU.mult))
                    dve.memset(m.mark[:], 0.0).then_inc(added.sem, 1)
                    return
                g = 3 * h + (1 if kind == "sel" else 2)
                link(dve.reciprocal(l, l))
                link(dve.tensor_tensor(l, l, gate[:, i, g:g + 1], ALU.mult))
                dve.wait_ge(summed.sem, summed.after(it, n))
                o = m.o[:, i, bass.ds(it * R_G * DH + h * DH, DH)]
                dve.scalar_tensor_tensor(out=o, in0=ps[:, 6 + n % 2, 0:DH], scalar=l, in1=o, op0=ALU.mult,
                                         op1=ALU.add).then_inc(added.sem, 1)

            with dve.Fori(0, KV_G) as it:
                link.restart()
                dve.wait_ge(loaded, it * LOADS + LOADS)
                for s in range(N + LAG_A):
                    if s < N:
                        shift_of(it, s)
                    n = s - LAG_T
                    if 0 <= n < N and two[n]:
                        w = (blocks[n] - 4) * P
                        dve.wait_ge(transB.sem, transB.after(it, n))
                        dve.wait_ge(summed.sem, summed.after(it, n - 2))
                        dve.tensor_copy(PT[:, n % 2, 4 * P:4 * P + w], ps[:, bank_of(n, 1), 0:w]).then_inc(movedB.sem, 1)
                    if 1 <= s <= N and items[s - 1][0] == "cmp":
                        weight_cmp(it, s - 1)
                    if s >= LAG_A:
                        add(it, s - LAG_A)


def mix_and_route(nc, ctx, m, a):
    sem = lambda n: ctx.enter_context(nc.semaphore(n))
    U = 4
    one = [1] * U
    x_in = [sem(f"res_in{j}") for j in range(2)]
    o_sq = Count(sem("mix_sq"), one)
    o_norm = Count(sem("mix_norm"), one, 4)
    o_tr = Count(sem("mix_tr"), [2] * U, 5)
    oT_full = Count(sem("mix_oT"), [2] * U, 2)
    oT_hi = Count(sem("mix_oT_hi"), [2] * U)
    oT_in = Count(sem("mix_oT_lo"), [2] * U)
    proj = Count(sem("mix_proj"), one, 3)
    x1_done = Count(sem("mix_x1"), one, 3)
    h_sq = Count(sem("ffn_sq"), one)
    h_norm = Count(sem("ffn_norm"), one, 3)
    h_tr = Count(sem("ffn_tr"), [2] * U, 5)
    hT_in = Count(sem("ffn_hT"), [2] * U, 2)
    logit = Count(sem("logits_mm"), one, 3)
    logit_in = Count(sem("logits_in"), one, 2)
    stored = [sem(f"h_stored{j}") for j in range(2)]
    m.h_stored = stored
    aln, dlink = sem("mix_ln"), sem("mix_dlink")
    ps = m.ps
    xt, hr = view(m.V, 0, 2, D), view(m.M, 2 * D, 2, D)
    oT, oTl, oTh = view(m.M, 0, 2, ND, P), view(m.as_r32["M"], 0, 2, ND, P), view(m.as_r32["V"], 2 * D, 2, ND, P)
    hT, junk = view(m.S, 0, 2, ND, P), view(m.S, 2 * D, D)
    o_stage = view(m.S, 3 * D, 2, D)
    st = view(m.S, 5 * D, 4, 8)
    st2 = view(m.S, 5 * D + 32, 2, 8)

    with nc.Block() as block:
        @block.sync
        def _(sp):
            sp.sem_inc(stored[0], 16)
            sp.sem_inc(stored[1], 16)
            sp.dma_start(m.list_d.rearrange("(p n) o -> p (n o)", p=P), m.zero_i[:]).then_inc(m.list_zero, 16)
            with sp.Fori(0, NT // U) as it:
                for n in range(U + 2):
                    if n < U:
                        sp.wait_ge(x1_done.sem, x1_done.after(it, n - 2))
                        sp.dma_start(xt[:, n % 2], a.x[bass.ds((it * U + n) * P, P), :]).then_inc(x_in[n % 2], 16)
                    if n >= 2:
                        k = n - 2
                        sp.wait_ge(h_norm.sem, h_norm.after(it, k))
                        sp.dma_start(m.h_d[bass.ds((it * U + k) * P, P), :], hr[:, k % 2]).then_inc(stored[k % 2], 16)

        @block.scalar
        def _(act):
            link = Link(act, aln)

            def squares(it, n):
                t = it * U + n
                act.wait_ge(o_norm.sem, o_norm.after(it, n - 4))
                for g in range(2):
                    link(act.activation(junk[:, 0:N_Q], m.o[:, bass.ds(t, 1), g * N_Q:(g + 1) * N_Q].rearrange("p a b -> p (a b)"),
                                        ACT.Square, accum_out=st[:, n % 4, g:g + 1]))
                r = st[:, n % 4, 4:6]
                link(act.activation(r, st[:, n % 4, 0:2], ACT.Ln, scale=1.0 / N_Q, bias=m.eps[:, 0:1]))
                act.activation(r, r, ACT.Exp, scale=-0.5).then_inc(o_sq.sem, 1)

            with act.Fori(0, NT // U) as it:
                link.restart()
                squares(it, 0)
                squares(it, 1)
                for s in range(U + 1):
                    if s + 2 < U:
                        squares(it, s + 2)
                    if s < U:
                        for half in range(2):
                            quad = slice(4 * half, 4 * half + 4)
                            act.wait_ge(oT_full.sem, oT_full.after(it, s) - 1 + half)
                            act.activation(oTh[:, s % 2, quad, :], oT[:, s % 2, quad, :], ACT.Copy).then_inc(oT_hi.sem, 1)
                    if s >= 1:
                        n = s - 1
                        t = it * U + n
                        act.wait_ge(x1_done.sem, x1_done.after(it, n))
                        act.wait_ge(h_norm.sem, h_norm.after(it, n - 2))
                        link(act.activation(junk, m.x1[:, bass.ds(t, 1), :].rearrange("p a b -> p (a b)"), ACT.Square,
                                            accum_out=st2[:, n % 2, 0:1]))
                        r = st2[:, n % 2, 4:5]
                        link(act.activation(r, st2[:, n % 2, 0:1], ACT.Ln, scale=1.0 / D, bias=m.eps[:, 0:1]))
                        act.activation(r, r, ACT.Exp, scale=-0.5).then_inc(h_sq.sem, 1)

        @block.vector
        def _(dve):
            for c in (o_norm, oT_full, x1_done, h_norm, hT_in, logit_in):
                dve.sem_inc(c.sem, c.credit)
            link = Link(dve, dlink)

            def gain(it, n, tr, done, w, dst, bank, used):
                dve.wait_ge(used.sem, used.after(it, n - 2))
                for half in range(2):
                    dve.wait_ge(tr.sem, tr.after(it, n) - 1 + half)
                    dve.tensor_tensor(dst[:, n % 2, 4 * half:4 * half + 4, :], ps[:, bank + half, :].rearrange("p (c n) -> p c n", n=P),
                                      w[:, 4 * half:4 * half + 4].unsqueeze(2).broadcast_to([P, 4, P]), ALU.mult).then_inc(done.sem, 1)

            def norm(it, n):
                t = it * U + n
                dve.wait_ge(o_sq.sem, o_sq.after(it, n))
                newton_rsqrt(dve, link, st[:, n % 4, 4:6], st[:, n % 4, 0:2], N_Q)
                dve.wait_ge(o_tr.sem, o_tr.after(it, n - 2))
                for g in range(2):
                    o = m.o[:, bass.ds(t, 1), g * N_Q:(g + 1) * N_Q].rearrange("p a b -> p (a b)")
                    ins = dve.tensor_scalar(o_stage[:, n % 2, g * N_Q:(g + 1) * N_Q], o, st[:, n % 4, 4 + g:5 + g], None, ALU.mult)
                ins.then_inc(o_norm.sem, 1)

            with dve.Fori(0, NT // U) as it:
                link.restart()
                norm(it, 0)
                for s in range(U + 2):
                    if s + 1 < U:
                        norm(it, s + 1)
                    if s < U:
                        gain(it, s, o_tr, oT_full, m.w_mix, oT, 0, proj)
                    if s >= 2:
                        gain(it, s - 2, h_tr, hT_in, m.w_ffn, hT, 4, logit)
                    if s < U:
                        for half in range(2):
                            quad = slice(4 * half, 4 * half + 4)
                            dve.wait_ge(oT_hi.sem, oT_hi.after(it, s) - 1 + half)
                            dve.tensor_tensor(oTl[:, s % 2, quad, :], oT[:, s % 2, quad, :], oTh[:, s % 2, quad, :], ALU.subtract).then_inc(oT_in.sem, 1)
                    if 1 <= s <= U:
                        n = s - 1
                        t = it * U + n
                        dve.wait_ge(proj.sem, proj.after(it, n))
                        dve.wait_ge(x_in[n % 2], it * 16 * (U // 2) + 16 * (n // 2) + 16)
                        dve.tensor_tensor(m.x1[:, bass.ds(t, 1), :].rearrange("p a b -> p (a b)"),
                                          ps[:, 2:4, :].rearrange("p a b -> p (a b)"), xt[:, n % 2], ALU.add).then_inc(x1_done.sem, 1)
                        dve.wait_ge(h_sq.sem, h_sq.after(it, n))
                        newton_rsqrt(dve, link, st2[:, n % 2, 4:5], st2[:, n % 2, 0:1], D)
                        dve.wait_ge(stored[n % 2], it * 16 * (U // 2) + 16 * (n // 2) + 16)
                        dve.wait_ge(h_tr.sem, h_tr.after(it, n - 2))
                        dve.tensor_scalar(hr[:, n % 2], m.x1[:, bass.ds(t, 1), :].rearrange("p a b -> p (a b)"), st2[:, n % 2, 4:5], None,
                                          ALU.mult).then_inc(h_norm.sem, 1)
                    if s >= 2:
                        n = s - 2
                        t = it * U + n
                        dve.wait_ge(logit.sem, logit.after(it, n))
                        dve.tensor_tensor(m.logits[:, bass.ds(t, 1), :].rearrange("p a b -> p (a b)"), ps[:, 6, 0:N_GRP + N_EXP],
                                          m.b_router[:], ALU.add).then_inc(logit_in.sem, 1)

        @block.tensor
        def _(pe):
            for c in (o_tr, proj, h_tr, logit):
                pe.sem_inc(c.sem, c.credit)
            pe.wait_ge(m.w_out_split, 4)
            pe.wait_ge(m.router_in, 64)
            with pe.Fori(0, NT // U) as it:
                for s in range(U + 2):
                    if s < U:
                        pe.wait_ge(o_norm.sem, o_norm.after(it, s))
                        for half in range(2):
                            pe.wait_ge(oT_full.sem, oT_full.after(it, s - 1) - 1 + half)
                            for c in range(4):
                                k = 4 * half + c
                                ins = pe.transpose(ps[:, half, c * P:(c + 1) * P], o_stage[:, s % 2, k * P:(k + 1) * P], m.ident[:])
                            ins.then_inc(o_tr.sem, 1)
                    for half in range(2):
                        if 1 <= s <= U:
                            n = s - 1
                            if half == 0:
                                pe.wait_ge(oT_in.sem, oT_in.after(it, n))
                                pe.wait_ge(x1_done.sem, x1_done.after(it, n - 1))
                            for c in range(ND):
                                ins = product(pe, ps[:, 2 + half, :], (oTh[:, n % 2, c, :], oTl[:, n % 2, c, :]),
                                              (m.w_out_hi[half][c // 4][:, c % 4, :], m.w_out_lo[:, c, half * BANK:(half + 1) * BANK]),
                                              c == 0, c == ND - 1)
                            if half == 1:
                                ins.then_inc(proj.sem, 1)
                        if s >= 2 and half == 0:
                            n = s - 2
                            pe.wait_ge(h_norm.sem, h_norm.after(it, n))
                            for quad in range(2):
                                pe.wait_ge(hT_in.sem, hT_in.after(it, n - 1) - 1 + quad)
                                for c in range(4):
                                    k = 4 * quad + c
                                    ins = pe.transpose(ps[:, 4 + quad, c * P:(c + 1) * P], hr[:, n % 2, k * P:(k + 1) * P], m.ident[:])
                                ins.then_inc(h_tr.sem, 1)
                    if s >= 2:
                        n = s - 2
                        pe.wait_ge(hT_in.sem, hT_in.after(it, n))
                        pe.wait_ge(logit_in.sem, logit_in.after(it, n - 1))
                        for c in range(ND):
                            ins = pe.matmul(ps[:, 6, 0:N_GRP + N_EXP], hT[:, n % 2, c, :], m.w_router[:, c, :], start=c == 0, stop=c == ND - 1)
                        ins.then_inc(logit.sem, 1)


def route(nc, ctx, m, a):
    sem = lambda n: ctx.enter_context(nc.semaphore(n))
    link_s, dif, ex_s, hot, rank, table, listed = map(
        sem, ("route_link", "route_dif", "route_exp", "route_hot", "route_rank", "route_table", "route_listed"))
    ps = m.ps
    r4 = lambda k: view(m.S, k * 32, NT, 4)
    eq, key, og, df, es, o1, o2, e2 = (r4(k) for k in range(8))
    r1 = lambda k: m.S[:, 256 + 8 * k:264 + 8 * k]
    gmax, kmax, gg, m1, m2, ex, den = (r1(k) for k in range(7))
    r16 = lambda k: view(m.S, 512 + k * 128, NT, N_GRP, E_PG)
    sel, H1, H2, dst, pick = (r16(k) for k in range(5))
    cnt, nb, end, start = (m.S[:, 1280 + 16 * k:1296 + 16 * k] for k in range(4))
    over = view(m.S, 1408, N_EXP, N_THR)
    d_f = view(m.S, 1600, 2, NT)
    gl = m.logits[:, :, 0:N_GRP]
    el = m.logits[:, :, N_GRP:].rearrange("p t (g e) -> p t g e", g=N_GRP)
    keys = m.idx_c[:, 0:4].unsqueeze(1).broadcast_to([P, NT, 4])
    thr = m.idx_c[:, C_THR - C_KEY:C_THR - C_KEY + N_THR].unsqueeze(1).broadcast_to([P, N_EXP, N_THR])
    over4 = lambda v: v.unsqueeze(2).broadcast_to([P, NT, 4])

    with nc.Block() as block:
        @block.vector
        def _(dve):
            link = Link(dve, link_s)

            def first_max(v, top, hot_):
                link(dve.reduce_max(top, v, AX_X))
                link(dve.tensor_tensor(eq, v, over4(top), ALU.is_equal))
                link(dve.tensor_tensor(key, eq, keys, ALU.mult))
                link(dve.reduce_max(kmax, key, AX_X))
                link(dve.tensor_tensor(hot_, key, over4(kmax), ALU.is_equal))

            first_max(gl, gmax, og)
            dve.tensor_tensor(df, gl, over4(gmax), ALU.subtract).then_inc(dif, 1)
            link(dve.tensor_tensor(sel, el, og.unsqueeze(3).broadcast_to([P, NT, N_GRP, E_PG]), ALU.mult))
            link(dve.reduce_sum(es, sel.rearrange("p t g e -> p t e g"), AX_X))
            first_max(es, m1, o1)
            link(dve.scalar_tensor_tensor(out=e2.rearrange("p a b -> p (a b)"), in0=o1.rearrange("p a b -> p (a b)"), scalar=NEG,
                                          in1=es.rearrange("p a b -> p (a b)"), op0=ALU.mult, op1=ALU.add))
            first_max(e2, m2, o2)
            dve.tensor_tensor(ex, m2, m1, ALU.subtract).then_inc(dif, 1)
            for hot_, o in ((H1, o1), (H2, o2)):
                link(dve.tensor_tensor(hot_, og.unsqueeze(3).broadcast_to([P, NT, N_GRP, E_PG]),
                                       o.unsqueeze(2).broadcast_to([P, NT, N_GRP, E_PG]), ALU.mult))
            dve.tensor_tensor(m.hot[:].rearrange("p t (g e) -> p t g e", g=N_GRP), H1, H2, ALU.add).then_inc(hot, 1)
            dve.wait_ge(ex_s, 2)
            link(dve.reduce_sum(gg, df, AX_X))
            link(dve.tensor_scalar(den, ex, 1.0, None, ALU.add))
            link(dve.tensor_tensor(den, den, gg, ALU.mult))
            link(dve.reciprocal(m.weight[:, 0, :], den))
            link(dve.tensor_tensor(m.weight[:, 1, :], m.weight[:, 0, :], ex, ALU.mult))
            dve.wait_ge(rank, 1)
            link(dve.tensor_copy(cnt, ps[:, 1, 0:N_EXP]))
            link(dve.tensor_tensor(over, cnt.unsqueeze(2).broadcast_to([P, N_EXP, N_THR]), thr, ALU.is_gt))
            link(dve.reduce_sum(nb, over, AX_X))
            link(dve.tensor_scalar(nb, nb, 1.0, None, ALU.add))
            link(dve.tensor_tensor_scan(end, m.one[:, 0:1].broadcast_to([P, N_EXP]), nb, 0.0, ALU.mult, ALU.add))
            link(dve.tensor_tensor(start, end, nb, ALU.subtract))
            link(dve.tensor_copy(m.blocks[:, 2 * N_EXP:3 * N_EXP], start))
            link(dve.tensor_scalar(m.blocks[:, 3 * N_EXP:], end[:, N_EXP - 1:N_EXP], -1.0, MAX_BLK + 1.0, ALU.mult, ALU.add))
            link(dve.tensor_scalar(start, start, float(BLK), None, ALU.mult))
            d16 = dst.rearrange("p t g e -> p t (g e)")
            link(dve.tensor_tensor(d16, ps[:, 0, 0:NT * N_EXP].rearrange("p (t e) -> p t e", e=N_EXP),
                                   start.unsqueeze(1).broadcast_to([P, NT, N_EXP]), ALU.add))
            for k, hot_ in enumerate((H1, H2)):
                link(dve.tensor_tensor(pick, hot_, dst, ALU.mult))
                link(dve.reduce_sum(d_f[:, k, :], pick.rearrange("p t g e -> p t (g e)"), AX_X))
            dve.tensor_copy(m.dest[:].rearrange("p a b -> p (a b)"), d_f.rearrange("p a b -> p (a b)"))
            dve.tensor_copy(m.tokens[:], m.idx_c[:, C_TOK - C_KEY:C_TOK - C_KEY + NT])
            dve.tensor_copy(m.blocks[:, 0:N_EXP], nb)
            dve.tensor_copy(m.blocks[:, N_EXP:2 * N_EXP], end).then_inc(table, 1)

        @block.scalar
        def _(act):
            act.wait_ge(dif, 1)
            act.activation(df, df, ACT.Exp).then_inc(ex_s, 1)
            act.wait_ge(dif, 2)
            act.activation(ex, ex, ACT.Exp).then_inc(ex_s, 1)

        @block.tensor
        def _(pe):
            pe.wait_ge(hot, 1)
            for t in range(NT):
                for u in range(t + 1):
                    pe.matmul(ps[:, 0, t * N_EXP:(t + 1) * N_EXP], m.tri[:] if u == t else m.ones_b[:], m.hot[:, u, :],
                              start=u == 0, stop=u == t)
            for t in range(NT):
                ins = pe.matmul(ps[:, 1, 0:N_EXP], m.ones_b[:], m.hot[:, t, :], start=t == 0, stop=t == NT - 1)
            ins.then_inc(rank, 1)

        @block.gpsimd
        def _(pool):
            pool.wait_ge(m.list_zero, 16)
            pool.wait_ge(table, 1)
            for k in range(2):
                for t in range(NT):
                    pool.indirect_dma_start(m.list_d, bass.IndirectOffsetOnAxis(ap=m.dest[:, k, t:t + 1], axis=0),
                                            m.tokens[:, t:t + 1], None).then_inc(listed, 16)

        @block.sync
        def _(sp):
            for i in range(4):
                load_matrix(sp, m, a, i, i % 3, i // 3)
            sp.wait_ge(listed, 16 * 2 * NT)
            with nc.allow_non_contiguous_dma("17 KiB of row numbers, to one block a column"):
                sp.dma_start(m.row_tok[:], m.list_d.rearrange("(b p) o -> p (b o)", p=P)).then_inc(m.rows_in, 16)


class Weights:

    def __init__(self, m):
        self.raw = [view(region, 0, 8, BANK) for region in (m.X, m.Y, m.M, m.V)]
        X, Y, M, V, Z = (m.as_r32[name] for name in "XYMVZ")
        self.low = [view(region, 0, 8, BANK) for region in (X, Y, M, V)]
        high = [view(region, 8 * BANK, 8, BANK) for region in (X, Y, M)]
        self.high = [(h[:, 0:4], h[:, 4:8]) for h in high] + [(view(V, 8 * BANK, 4, BANK), view(Z, NT * D, 4, BANK))]

    def hi(self, slot, u, n=1):
        return self.high[slot][u // 4][:, u % 4:u % 4 + n]

    def lo(self, slot, u, n=1):
        return self.low[slot][:, u:u + n]


def load_matrix(eng, m, a, i, kind, e):
    rows, src = (FF, a.w_down_rows) if kind == 2 else (D, (a.w_gate_rows, a.w_up_rows)[kind])
    dst = m.weights.raw[i % 4].rearrange("p a b -> p (a b)").rearrange("p (c f) -> p c f", c=rows // P)
    eng.dma_start(dst, src[bass.ds(e * rows, rows), :].rearrange("(c p) f -> p c f", p=P)).then_inc(m.w_raw[i % 4], 16)


def experts(nc, ctx, m, a):
    sem = lambda n: ctx.enter_context(nc.semaphore(n))
    w_hi, w_lo = sem("moe_w_hi"), sem("moe_w_lo")
    idx_s, x_tr, x_full, x_hi, x_in = map(sem, ("moe_idx", "moe_x_tr", "moe_x_full", "moe_x_hi", "moe_x_in"))
    g_mm, u_mm, silu, hidden = map(sem, ("moe_gate", "moe_up", "moe_silu", "moe_hidden"))
    h_tr, h_hi, h_in, y_mm, y_out = map(sem, ("moe_h_tr", "moe_h_hi", "moe_h_in", "moe_down", "moe_y_out"))
    gathered, m.y_stored, m.y_zeroed, zeroed = sem("moe_gathered"), sem("moe_y_stored"), sem("moe_y_zeroed"), sem("moe_zeros")
    ps, w = m.ps, m.weights
    R = 4
    PASSES = N_EXP // R
    SLOTS = 4
    S = m.as_r32["S"]
    xg, xf, hm = view(m.S, 0, D), view(m.S, 2 * D, ND, P), view(m.S, 3 * D, FF)
    xh, xl = view(S, D, ND, P), view(S, 2 * D, ND, P)
    hh, hl = view(S, 3 * D + FF, NF, P), view(S, 4 * D, NF, P)
    y, zeros = view(m.S, 4 * D + FF, D), view(m.S, 5 * D + FF, D // 2)
    H = FF // 2
    U, HT = (1, 7), (4, 1)

    def blocks_in_all(eng):
        return eng.value_load(m.blocks[0:1, 2 * N_EXP - 1:2 * N_EXP], min_val=N_EXP, max_val=MAX_BLK)

    def blocks_of(eng, it, r):
        first = eng.value_load(m.blocks[0:1, bass.ds(2 * N_EXP + it * R + r, 1)], min_val=0, max_val=MAX_BLK - 1)
        end = eng.value_load(m.blocks[0:1, bass.ds(N_EXP + it * R + r, 1)], min_val=1, max_val=MAX_BLK)
        return first, end

    def arrived(it, i):
        return it * (16 * 3 * R // SLOTS) + 16 * (i // SLOTS + 1)

    def split(it, i, q):
        return it * (4 * 3 * R) + 4 * i + q + 1

    with nc.Block() as block:
        @block.sync
        def _(sp):
            sp.wait_ge(zeroed, 1)
            with sp.Fori(blocks_in_all(sp), MAX_BLK + 1) as b:
                for half in range(2):
                    sp.dma_start(m.y_d[bass.ds(b * P, P), half * BANK:(half + 1) * BANK], zeros).then_inc(m.y_zeroed, 16)

            def loads(it, r, gate):
                end = sp.value_load(m.blocks[0:1, bass.ds(N_EXP + it * R + r, 1)], min_val=1, max_val=MAX_BLK)
                e = it * R + r + 1
                sp.wait_ge(g_mm, end)
                load_matrix(sp, m, a, 3 * (r + 1) + 1, 1, e)
                sp.wait_ge(u_mm, end * 2 + 2)
                load_matrix(sp, m, a, 3 * (r + 1) + 2, 2, e)
                if gate:
                    sp.wait_ge(y_mm, end + 1)
                    load_matrix(sp, m, a, 3 * (r + 1) + 3, 0, e + 1)

            with sp.Fori(0, PASSES - 1) as it:
                for r in range(R):
                    loads(it, r, True)
            for r in range(R - 1):
                loads(PASSES - 1, r, r < R - 2)

        @block.gpsimd
        def _(pool):
            pool.wait_ge(m.rows_in, 16)
            for j in range(2):
                pool.wait_ge(m.h_stored[j], 80)
            n = blocks_in_all(pool)
            with pool.Fori(0, n + 1) as b:
                pool.sem_clear(idx_s)
                pool.wait_ge(x_tr, b + 1)
                pool.tensor_copy(m.row_now[:], m.row_tok[:, bass.ds(b, 1)]).then_inc(idx_s, 1)
                pool.wait_ge(idx_s, 1)
                pool.indirect_dma_start(xg, None, m.h_d, bass.IndirectOffsetOnAxis(ap=m.row_now[:], axis=0)).then_inc(gathered, 16)
                pool.wait_ge(gathered, b * 16 + 16)

        @block.tensor
        def _(pe):
            pe.sem_inc(x_tr, 1)
            pe.sem_inc(y_mm, 1)
            pe.sem_inc(u_mm, 2)
            pe.sem_inc(h_tr, 2)

            def transpose_x(b):
                pe.wait_ge(gathered, b * 16 + 16)
                for c in range(ND):
                    ins = pe.transpose(ps[:, 2 + c // 4, c % 4 * P:(c % 4 + 1) * P], xg[:, c * P:(c + 1) * P], m.ident[:])
                ins.then_inc(x_tr, 1)

            def transpose_h(b, half):
                pe.wait_ge(hidden, b * 2 + half + 1)
                for f in range(2):
                    ins = pe.transpose(ps[:, HT[half], f * P:(f + 1) * P], hm[:, (2 * half + f) * P:(2 * half + f + 1) * P], m.ident[:])
                ins.then_inc(h_tr, 1)

            def unit(slot, u, cols=slice(0, BANK)):
                return w.hi(slot, u)[:, 0, cols], w.lo(slot, u)[:, 0, cols]

            transpose_x(0)
            with pe.Fori(0, PASSES) as it:
                for r in range(R):
                    g, u, d = 3 * r, 3 * r + 1, 3 * r + 2
                    first, end = blocks_of(pe, it, r)
                    with pe.Fori(first, end) as b:
                        pe.wait_ge(x_in, b + 1)
                        pe.wait_ge(silu, b + 1)
                        for c in range(ND):
                            if c % 2 == 0:
                                pe.wait_ge(w_lo, split(it, g, c // 2))
                            ins = product(pe, ps[:, 0, :], (xh[:, c], xl[:, c]), unit(g % SLOTS, c), c == 0, c == ND - 1)
                        ins.then_inc(g_mm, 1)
                        for half in range(2):
                            cols = slice(half * H, (half + 1) * H)
                            for c in range(ND):
                                if half == 0 and c % 2 == 0:
                                    pe.wait_ge(w_lo, split(it, u, c // 2))
                                ins = product(pe, ps[:, U[half], 0:H], (xh[:, c], xl[:, c]), unit(u % SLOTS, c, cols), c == 0, c == ND - 1)
                            ins.then_inc(u_mm, 1)
                        transpose_h(b, 0)
                        transpose_x(b + 1)
                        transpose_h(b, 1)
                        pe.wait_ge(y_out, b + 1)
                        for f in range(NF):
                            if f % 2 == 0:
                                pe.wait_ge(h_in, b * 2 + f // 2 + 1)
                            pe.wait_ge(w_lo, split(it, d, f))
                            for half in range(2):
                                ins = product(pe, ps[:, 5 + half, :], (hh[:, f], hl[:, f]), unit(d % SLOTS, 2 * f + half), f == 0, f == NF - 1)
                        ins.then_inc(y_mm, 1)

        @block.scalar
        def _(act):
            act.preload_act_table_set("silu_and_others")
            act.sem_inc(silu, 1)
            act.sem_inc(y_out, 1)
            act.sem_inc(m.y_stored, 16)

            def high_halves(it, i):
                act.wait_ge(m.w_raw[i % SLOTS], arrived(it, i))
                for q in range(4):
                    act.activation(w.hi(i % SLOTS, 2 * q, 2), w.raw[i % SLOTS][:, 2 * q:2 * q + 2], ACT.Copy).then_inc(w_hi, 1)

            def rows_high(b):
                act.wait_ge(x_full, b + 1)
                act.activation(xh, xf, ACT.Copy).then_inc(x_hi, 1)

            def hidden_of(b):
                act.wait_ge(g_mm, b + 1)
                act.wait_ge(h_tr, b * 2 + 2)
                act.activation(hm, ps[:, 0, :], ACT.Silu).then_inc(silu, 1)
                act.wait_ge(y_mm, b + 1)
                for half in range(2):
                    act.wait_ge(h_tr, b * 2 + half + 3)
                    act.activation(hh[:, 2 * half:2 * half + 2],
                                   ps[:, HT[half], 0:2 * P].rearrange("p (a b) -> p a b", b=P), ACT.Copy).then_inc(h_hi, 1)
                rows_high(b + 1)

            def rows_out(b):
                act.wait_ge(y_mm, b + 2)
                act.wait_ge(m.y_stored, b * 16 + 16)
                act.activation(y, ps[:, 5:7, :].rearrange("p a b -> p (a b)"), ACT.Copy).then_inc(y_out, 1)
                act.wait_ge(y_out, b + 2)
                act.dma_start(m.y_d[bass.ds(b * P, P), :], y).then_inc(m.y_stored, 16)

            def last_before(it, r):
                return act.value_load(m.blocks[0:1, bass.ds(N_EXP - 1 + it * R + r, 1)], min_val=1, max_val=MAX_BLK) - 1

            high_halves(0, 0)
            rows_high(0)
            with act.Fori(0, PASSES) as it:
                for r in range(R):
                    high_halves(it, 3 * r + 1)
                    high_halves(it, 3 * r + 2)
                    first, end = blocks_of(act, it, r)
                    if r:
                        rows_out(last_before(it, r))
                    else:
                        with act.If(it > 0):
                            rows_out(last_before(it, r))
                    hidden_of(first)
                    if r < R - 1:
                        high_halves(it, 3 * r + 3)
                    else:
                        with act.If(it < PASSES - 1):
                            high_halves(it, 3 * r + 3)
                    with act.If(first + 1 < end):
                        with act.Fori(first + 1, end) as b:
                            rows_out(b - 1)
                            hidden_of(b)
            rows_out(blocks_in_all(act) - 1)

        @block.vector
        def _(dve):
            dve.memset(zeros, 0.0).then_inc(zeroed, 1)

            def low_halves(it, i):
                raw = w.raw[i % SLOTS]
                for q in range(4):
                    dve.wait_ge(w_hi, split(it, i, q))
                    dve.tensor_tensor(w.lo(i % SLOTS, 2 * q, 2), raw[:, 2 * q:2 * q + 2], w.hi(i % SLOTS, 2 * q, 2), ALU.subtract).then_inc(w_lo, 1)

            def rows_in(b):
                dve.wait_ge(x_tr, b + 2)
                dve.wait_ge(u_mm, b * 2 + 2)
                dve.tensor_tensor(xf, ps[:, 2:4, :].rearrange("p a (c n) -> p (a c) n", n=P),
                                  m.w_ffn[:].unsqueeze(2).broadcast_to([P, ND, P]), ALU.mult).then_inc(x_full, 1)
                dve.wait_ge(x_hi, b + 1)
                dve.tensor_tensor(xl, xf, xh, ALU.subtract).then_inc(x_in, 1)

            def hidden_of(b):
                dve.wait_ge(silu, b + 2)
                for half in range(2):
                    c = slice(half * H, (half + 1) * H)
                    dve.wait_ge(u_mm, b * 2 + half + 3)
                    dve.tensor_tensor(hm[:, c], hm[:, c], ps[:, U[half], 0:H], ALU.mult).then_inc(hidden, 1)
                for half in range(2):
                    fs = slice(2 * half, 2 * half + 2)
                    dve.wait_ge(h_hi, b * 2 + half + 1)
                    dve.tensor_tensor(hl[:, fs], ps[:, HT[half], 0:2 * P].rearrange("p (a b) -> p a b", b=P),
                                      hh[:, fs], ALU.subtract).then_inc(h_in, 1)
                rows_in(b + 1)

            low_halves(0, 0)
            rows_in(0)
            with dve.Fori(0, PASSES) as it:
                for r in range(R):
                    low_halves(it, 3 * r + 1)
                    low_halves(it, 3 * r + 2)
                    first, end = blocks_of(dve, it, r)
                    hidden_of(first)
                    if r < R - 1:
                        low_halves(it, 3 * r + 3)
                    else:
                        with dve.If(it < PASSES - 1):
                            low_halves(it, 3 * r + 3)
                    with dve.If(first + 1 < end):
                        with dve.Fori(first + 1, end) as b:
                            hidden_of(b)


def combine(nc, ctx, m, a, out):
    sem = lambda n: ctx.enter_context(nc.semaphore(n))
    U = 4
    one = [1] * U
    gathered = [sem(f"end_g{s}") for s in range(U)]
    idx_s = sem("end_idx")
    added = Count(sem("end_added"), one, U)
    sq = Count(sem("end_sq"), one)
    done = Count(sem("end_done"), one, 3)
    stored = [sem("out_stored0"), sem("out_stored1")]
    aln, dlink, wf = sem("end_ln"), sem("end_dlink"), sem("end_wf")
    y = view(m.X, 0, U, 2, D)
    acc, junk, w = view(m.Y, 0, 2, D), view(m.Y, 2 * D, D), view(m.Y, 3 * D, D)
    o = view(m.Y, 4 * D, 2, D)
    st = view(m.S, 0, 2, 8)

    with nc.Block() as block:
        @block.gpsimd
        def _(pool):
            n = pool.value_load(m.blocks[0:1, 2 * N_EXP - 1:2 * N_EXP], min_val=N_EXP, max_val=MAX_BLK)
            unused = pool.value_load(m.blocks[0:1, 3 * N_EXP:3 * N_EXP + 1], min_val=1, max_val=MAX_BLK + 1 - N_EXP)
            with pool.Fori(0, NT // U) as it:
                pool.sem_clear(idx_s)
                pool.wait_ge(m.y_stored, n * 16 + 16)
                pool.wait_ge(m.y_zeroed, unused * 32)
                for s in range(U):
                    pool.wait_ge(added.sem, added.after(it, s - U))
                    for k in range(2):
                        pool.tensor_copy(m.dest_now[:, s, k:k + 1], m.dest[:, k, bass.ds(it * U + s, 1)]).then_inc(idx_s, 1)
                        pool.wait_ge(idx_s, 2 * s + k + 1)
                        pool.indirect_dma_start(y[:, s, k], None, m.y_d, bass.IndirectOffsetOnAxis(ap=m.dest_now[:, s, k:k + 1], axis=0)).then_inc(gathered[s], 16)

        @block.vector
        def _(dve):
            dve.sem_inc(added.sem, added.credit)
            dve.sem_inc(done.sem, done.credit)
            link = Link(dve, dlink)
            dve.wait_ge(wf, 16)
            with dve.Fori(0, NT // U) as it:
                link.restart()
                for step in range(U + 1):
                    if step < U:
                        s, t = step, it * U + step
                        dve.wait_ge(gathered[s], it * 32 + 32)
                        dve.wait_ge(done.sem, done.after(it, s - 2))
                        x1 = m.x1[:, bass.ds(t, 1), :].rearrange("p a b -> p (a b)")
                        wt = [m.weight[:, k, bass.ds(t, 1)] for k in range(2)]
                        link(dve.scalar_tensor_tensor(out=acc[:, s % 2], in0=y[:, s, 0], scalar=wt[0], in1=x1, op0=ALU.mult, op1=ALU.add))
                        dve.scalar_tensor_tensor(out=acc[:, s % 2], in0=y[:, s, 1], scalar=wt[1], in1=acc[:, s % 2], op0=ALU.mult,
                                                 op1=ALU.add).then_inc(added.sem, 1)
                    if step:
                        s = step - 1
                        dve.wait_ge(sq.sem, sq.after(it, s))
                        newton_rsqrt(dve, link, st[:, s % 2, 4:5], st[:, s % 2, 0:1], D)
                        dve.wait_ge(stored[s % 2], it * 16 * (U // 2) + 16 * (s // 2) + 16)
                        dve.scalar_tensor_tensor(out=o[:, s % 2], in0=acc[:, s % 2], scalar=st[:, s % 2, 4:5], in1=w, op0=ALU.mult,
                                                 op1=ALU.mult).then_inc(done.sem, 1)

        @block.scalar
        def _(act):
            act.preload_act_table_set("natural_log_exp_and_others")
            link = Link(act, aln)
            with act.Fori(0, NT // U) as it:
                link.restart()
                for s in range(U):
                    act.wait_ge(added.sem, added.after(it, s))
                    act.wait_ge(done.sem, done.after(it, s - 2))
                    link(act.activation(junk, acc[:, s % 2], ACT.Square, accum_out=st[:, s % 2, 0:1]))
                    r = st[:, s % 2, 4:5]
                    link(act.activation(r, st[:, s % 2, 0:1], ACT.Ln, scale=1.0 / D, bias=m.eps[:, 0:1]))
                    act.activation(r, r, ACT.Exp, scale=-0.5).then_inc(sq.sem, 1)

        @block.sync
        def _(sp):
            for s in range(2):
                sp.sem_inc(stored[s], 16)
            sp.dma_start(w, a.final_norm_w.partition_broadcast(P)).then_inc(wf, 16)
            with sp.Fori(0, NT // U) as it:
                for s in range(U):
                    sp.wait_ge(done.sem, done.after(it, s))
                    sp.dma_start(out[bass.ds((it * U + s) * P, P), :], o[:, s % 2]).then_inc(stored[s % 2], 16)
            for s in range(2):
                sp.wait_ge(stored[s], 16 + 16 * (NT // 2))


INPUTS = ["x", "positions", "attn_norm_w", "w_in", "cmp_pe_k", "cmp_pe_v", "cmp_k_w1", "cmp_k_w2", "cmp_v_w1",
          "cmp_v_w2", "nsa_out_norm_w", "sb_out_norm_w", "w_out", "ffn_norm_w", "router_group_w",
          "router_group_b", "router_expert_w", "router_expert_b", "w_gate", "w_up", "w_down", "final_norm_w"]


def build(nc, a, out):
    m = Mem()
    with ExitStack() as ctx:
        sb = lambda n, s, d=F32: ctx.enter_context(nc.sbuf_tensor(n, s, d))
        sem = lambda n: ctx.enter_context(nc.semaphore(n))
        m.ident = sb("ident", [P, P])
        m.ident_b = sb("ident_b", [P, P], BF16)
        m.causal = sb("causal", [P, P], BF16)
        m.strict = sb("strict", [P, P], BF16)
        m.winmask = sb("winmask", [P, P], BF16)
        m.tri = sb("tri", [P, P], BF16)
        m.ones_b = sb("ones_b", [P, P], BF16)
        m.ones = sb("ones", [P, 2])
        m.cmpmask = sb("cmpmask", [P, NT, N_CMP], BF16)
        m.idx_c = sb("idx_c", [P, C_ALL - C_KEY])
        m.w_attn = sb("w_attn", [P, ND])
        m.w_mix = sb("w_mix", [P, ND])
        m.w_ffn = sb("w_ffn", [P, ND])
        m.pos = sb("pos", [P, NT], I32)
        m.trig = sb("trig", [P, 2, NT, 8])
        m.eps, m.clip, m.one = sb("eps", [P, 1]), sb("clip", [P, 1]), sb("one", [P, 1])
        m.stat = sb("stat", [P, 8])
        m.rstd = sb("rstd", [P, 8])
        m.w_gates = sb("w_gates", [P, ND, N_GATE])
        m.gates = sb("gates", [P, NT, N_GATE])
        m.w_router = sb("w_router", [P, ND, N_GRP + N_EXP])
        m.b_router = sb("b_router", [P, N_GRP + N_EXP])
        def region(name, kib):
            at = -(-nc.sbuf_base // 32) * 32
            return sb(name, [P, kib * KB]), nc.alloc_sbuf_tensor_at(name + "_r32", [P, kib * KB], F32R, offset=at)

        m.as_r32 = {}
        m.X, m.as_r32["X"] = region("X", 32)
        m.Y, m.as_r32["Y"] = region("Y", 32)
        m.Z, m.as_r32["Z"] = region("Z", 40)
        m.V, m.as_r32["V"] = region("V", 24)
        m.S, m.as_r32["S"] = region("S", 24)
        m.M, m.as_r32["M"] = region("M", 32)
        m.ps = ctx.enter_context(nc.psum_tensor("ps", [P, 8, BANK], F32))
        m.hT_hi, m.hT_lo = view(m.as_r32["X"], 0, ND, T), view(m.as_r32["M"], 0, ND, T)
        m.keys = view(m.M, 0, 2, 2, T)
        m.w_raw_in = [view(m.Y, g * ND * BANK, ND, BANK) for g in range(2)]
        m.groups = [0, COL_SEL, COL_SBV, COL_SBQ, COL_SBK]
        m.w_loaded = [sem("w_loaded0"), sem("w_loaded1")]
        m.w_gates_loaded = sem("w_gates_loaded")
        m.router_in = sem("router_in")
        m.qT = view(m.Z, 0, 4, T)
        m.kT = view(m.Z, 16 * KB, 2, T)
        m.vsw = view(m.Z, 24 * KB, NT, 2, P)
        m.ckv = view(m.Z, 32 * KB, KV_G, T)
        m.mark = sb("mark", [P, 1])
        m.sbqk_rows = nc.dram_tensor("sb_qk_scratch", (2 * SB_H * DH, T), F32, kind="Internal").ap()
        m.sbv_d = nc.dram_tensor("sb_v_scratch", (NT, P, BANK), F32, kind="Internal").ap()
        m.w_out = view(m.Y, 0, ND, D)
        m.w_out_in, m.w_out_split = sem("w_out_in"), sem("w_out_split")
        m.w_out_lo = view(m.as_r32["Y"], 0, ND, D)
        m.w_out_hi = [[view(m.as_r32["M"], 4 * T, 4, BANK), view(m.as_r32["M"], 6 * T, 4, BANK)],
                      [view(m.as_r32["Z"], 8 * T, 4, BANK), view(m.as_r32["V"], 4 * T, 4, BANK)]]
        m.x1 = view(m.Z, 0, NT, D)
        m.logits = sb("logits", [P, NT, N_GRP + N_EXP])
        m.hot = sb("hot", [P, NT, N_EXP], BF16)
        m.weight = sb("weight", [P, 2, NT])
        m.dest = sb("dest", [P, 2, NT], I32)
        m.dest_now = sb("dest_now", [P, 4, 2], I32)
        m.tokens = sb("tokens", [P, NT], I32)
        m.blocks = sb("blocks", [P, 3 * N_EXP + 1], I32)
        m.row_tok = sb("row_tok", [P, MAX_BLK + 1], I32)
        m.row_now = sb("row_now", [P, 1], I32)
        m.zero_i = sb("zero_i", [P, MAX_BLK + 1], I32)
        m.list_zero, m.rows_in = sem("list_zero"), sem("rows_in")
        m.weights = Weights(m)
        m.w_raw = [sem(f"w_raw{j}") for j in range(4)]
        m.list_d = nc.dram_tensor("row_list_scratch", (ROWS, 1), I32, kind="Internal").ap()
        m.h_d = nc.dram_tensor("h_scratch", (T, D), F32, kind="Internal").ap()
        m.y_d = nc.dram_tensor("y_scratch", (ROWS, D), F32, kind="Internal").ap()
        m.o = view(m.X, 0, NT, D)
        m.w2 = sb("cmp_w2", [P, 2, 2, 2, DH])
        m.pe_rows = sb("cmp_pe", [CMP_STRIDE, 2, 2, DH])
        m.kc = sb("kc", [P, KV_G, N_CMP])
        m.vc = sb("vc", [P, KV_G, DH])
        m.cmp_w = sem("cmp_w_loaded")
        hidden_states(nc, ctx, m, a)
        projections(nc, ctx, m, a)
        stick_breaking(nc, ctx, m, a)
        compression(nc, ctx, m, a)
        native_sparse(nc, ctx, m, a)
        mix_and_route(nc, ctx, m, a)
        route(nc, ctx, m, a)
        experts(nc, ctx, m, a)
        combine(nc, ctx, m, a, out)


class Args:
    pass


def kernel(**inputs):
    import concourse.bacc as _bacc
    from concourse.bass_utils import run_bass_kernel_spmd as _run

    nc = _bacc.Bacc("TRN2", target_bir_lowering=False, num_devices=1)
    arrays, a = {}, Args()
    for name in INPUTS:
        arr = np.ascontiguousarray(inputs[name])
        if arr.ndim > 1:
            arr = arr[0]
        arrays[name] = arr
        a.__dict__[name] = nc.dram_tensor(name, arr.shape, mybir.dt.from_np(arr.dtype), kind="ExternalInput").ap()
    arrays["shape_constants"] = constants()
    a.cst = nc.dram_tensor("shape_constants", (P, C_ALL), F32, kind="ExternalInput").ap()
    a.w_gate_rows = a.w_gate.rearrange("e d f -> (e d) f")
    a.w_up_rows = a.w_up.rearrange("e d f -> (e d) f")
    a.w_down_rows = a.w_down.rearrange("e f d -> (e f) d")
    a.w_in_rows = a.w_in.rearrange("(c p) n -> p c n", p=P)
    out = nc.dram_tensor("out", (T, D), F32, kind="ExternalOutput").ap()
    build(nc, a, out)
    r = _run(nc, [arrays], core_ids=[0])
    return r.results[0]["out"].reshape(1, T, D)
```
